# Optimizing a Trainium2 kernel written in Bass

```python
import math
import jax, jax.numpy as jnp
from jax import lax
import numpy as np

D_MODEL = 1024
BATCH = 1
SEQ = 256
DEPTH = 2

CHUNK = 64
N_MIXERS = 2
N_SSM_LAYERS = (DEPTH + N_MIXERS - 1) // N_MIXERS
N_ATTN_LAYERS = DEPTH // N_MIXERS

SSM_GROUP = 16
SSM_GROUPS = D_MODEL // SSM_GROUP
SSM_STATE = 64
DT_MIN = 1e-3
DT_MAX = 1e-1

DIFF_HEAD_DIM = 64
DIFF_HEADS = D_MODEL // (2 * DIFF_HEAD_DIM)
V_HEAD_DIM = 2 * DIFF_HEAD_DIM
ROPE_THETA = 10000.0
Q_BLOCK = 128

N_EXPERT_GROUPS = 4
EXPERTS_PER_GROUP = 8
TOP_K = 2
D_EXPERT = D_MODEL // 4

EPS = 1e-6

kernel_name = "hybrid_s5_diffattn_hiermoe_stream"

def rms_norm(x, g):
    xf = x.astype(jnp.float32)
    y = xf * lax.rsqrt(jnp.mean(xf * xf, axis=-1, keepdims=True) + EPS)
    return (y * g.astype(jnp.float32)).astype(x.dtype)

def rope_tables(seq):
    pos = jnp.arange(seq, dtype=jnp.float32)
    inv = ROPE_THETA ** (-jnp.arange(0, DIFF_HEAD_DIM, 2, dtype=jnp.float32) / DIFF_HEAD_DIM)
    ang = pos[:, None] * inv[None, :]
    return jnp.cos(ang), jnp.sin(ang)

def apply_rope(x, cos, sin):
    half = DIFF_HEAD_DIM // 2
    x1, x2 = x[..., :half], x[..., half:]
    c = cos[None, :, None, None, :].astype(x.dtype)
    s = sin[None, :, None, None, :].astype(x.dtype)
    return jnp.concatenate([x1 * c - x2 * s, x2 * c + x1 * s], axis=-1)

def _scan_op(left, right):
    a_l, b_l = left
    a_r, b_r = right
    return a_r * a_l, a_r * b_l + b_r

def s5_mixer(h, w_in, lam_re, lam_im, log_dt, b_re, b_im, c_re, c_im, d_skip, w_glu):
    bsz, seq, _ = h.shape
    u = (h @ w_in).astype(jnp.float32)
    lam = lax.complex(lam_re.astype(jnp.float32), lam_im.astype(jnp.float32))
    dt = jnp.exp(log_dt.astype(jnp.float32))[:, None]
    lam_bar = jnp.exp(lam * dt)
    b_c = lax.complex(b_re.astype(jnp.float32), b_im.astype(jnp.float32))
    b_bar = ((lam_bar - 1.0) / lam)[..., None] * b_c
    c_c = lax.complex(c_re.astype(jnp.float32), c_im.astype(jnp.float32))
    n_chunks = seq // CHUNK
    u_chunks = u.reshape(bsz, n_chunks, CHUNK, SSM_GROUPS, SSM_GROUP).transpose(1, 0, 2, 3, 4)
    a = jnp.broadcast_to(lam_bar, (bsz, CHUNK, SSM_GROUPS, SSM_STATE))

    def chunk_step(state, u_c):
        bu = jnp.einsum('bcgh,gph->bcgp', u_c.astype(jnp.complex64), b_bar)
        a_cum, x_loc = lax.associative_scan(_scan_op, (a, bu), axis=1)
        xs = x_loc + a_cum * state[:, None]
        y = jnp.real(jnp.einsum('bcgp,ghp->bcgh', xs, c_c))
        return xs[:, -1], y

    state0 = jnp.zeros((bsz, SSM_GROUPS, SSM_STATE), jnp.complex64)
    _, y = lax.scan(chunk_step, state0, u_chunks)
    y = y.transpose(1, 0, 2, 3, 4).reshape(bsz, seq, D_MODEL) + d_skip.astype(jnp.float32) * u
    g = jax.nn.gelu(y).astype(h.dtype)
    val, gate = jnp.split(g @ w_glu, 2, axis=-1)
    return val * jax.nn.sigmoid(gate)

def diff_attention(h, w_qkv, lq1, lk1, lq2, lk2, subln_g, w_o, cos, sin, lambda_init):
    bsz, seq, _ = h.shape
    q, k, v = jnp.split(h @ w_qkv, 3, axis=-1)
    q = q.reshape(bsz, seq, DIFF_HEADS, 2, DIFF_HEAD_DIM)
    k = k.reshape(bsz, seq, DIFF_HEADS, 2, DIFF_HEAD_DIM)
    v32 = v.reshape(bsz, seq, DIFF_HEADS, V_HEAD_DIM).astype(jnp.float32)
    q = apply_rope(q, cos, sin) * (DIFF_HEAD_DIM ** -0.5)
    k = apply_rope(k, cos, sin)
    lam = (jnp.exp(jnp.sum(lq1.astype(jnp.float32) * lk1.astype(jnp.float32)))
           - jnp.exp(jnp.sum(lq2.astype(jnp.float32) * lk2.astype(jnp.float32)))
           + lambda_init)
    key_chunk = jnp.arange(seq) // CHUNK
    n_blocks = seq // Q_BLOCK
    q_blocks = q.reshape(bsz, n_blocks, Q_BLOCK, DIFF_HEADS, 2, DIFF_HEAD_DIM).transpose(1, 0, 2, 3, 4, 5)

    def block(args):
        qb, bi = args
        s = jnp.einsum('bqhcd,bkhcd->bhcqk', qb, k, preferred_element_type=jnp.float32)
        q_chunk = (bi * Q_BLOCK + jnp.arange(Q_BLOCK)) // CHUNK
        mask = key_chunk[None, :] <= q_chunk[:, None]
        s = jnp.where(mask, s, -jnp.inf)
        p = jax.nn.softmax(s, axis=-1)
        attn = p[:, :, 0] - lam * p[:, :, 1]
        o = jnp.einsum('bhqk,bkhe->bqhe', attn, v32)
        o = o * lax.rsqrt(jnp.mean(o * o, axis=-1, keepdims=True) + EPS)
        o = o * subln_g.astype(jnp.float32) * (1.0 - lambda_init)
        return o.astype(h.dtype)

    o = lax.map(block, (q_blocks, jnp.arange(n_blocks)))
    o = o.transpose(1, 0, 2, 3, 4).reshape(bsz, seq, D_MODEL)
    return o @ w_o

def hier_moe(h, w_rg, b_rg, w_re, b_re, w_gate, w_up, w_down):
    bsz, seq, d = h.shape
    t = h.reshape(-1, d)
    gl = (t @ w_rg).astype(jnp.float32)
    gp = jax.nn.softmax(gl, axis=-1)
    g_sel = jnp.argmax(gl + b_rg.astype(jnp.float32), axis=-1)
    g_onehot = jax.nn.one_hot(g_sel, N_EXPERT_GROUPS, dtype=jnp.float32)
    g_w = jnp.sum(gp * g_onehot, axis=-1)
    el = jnp.einsum('td,dge->tge', t, w_re).astype(jnp.float32)
    el_sel = jnp.sum(el * g_onehot[:, :, None], axis=1)
    ep = jax.nn.softmax(el_sel, axis=-1)
    bias_sel = g_onehot @ b_re.astype(jnp.float32)
    _, e_idx = lax.top_k(ep + bias_sel, TOP_K)
    e_w = jnp.take_along_axis(ep, e_idx, axis=-1)
    e_w = e_w / jnp.sum(e_w, axis=-1, keepdims=True)
    within = jnp.sum(jax.nn.one_hot(e_idx, EXPERTS_PER_GROUP, dtype=jnp.float32) * e_w[..., None], axis=1)
    combine = (g_onehot[:, :, None] * within[:, None, :] * g_w[:, None, None]).astype(t.dtype)
    out = jnp.zeros_like(t)
    for g in range(N_EXPERT_GROUPS):
        gate = jnp.einsum('td,edf->tef', t, w_gate[g])
        up = jnp.einsum('td,edf->tef', t, w_up[g])
        hid = jax.nn.silu(gate) * up * combine[:, g, :, None]
        out = out + jnp.einsum('tef,efd->td', hid, w_down[g])
    return out.reshape(bsz, seq, d)

def setup_inputs(seed: int = 0) -> dict:
    key = jax.random.key(seed)
    ks = jax.random.split(key, 32)
    f32 = jnp.float32

    def nrm(k, shape, scale):
        return jax.random.normal(k, shape, f32) * scale

    NA, NB, L = N_SSM_LAYERS, N_ATTN_LAYERS, DEPTH
    G, P, HG = SSM_GROUPS, SSM_STATE, SSM_GROUP
    NG, NE, F = N_EXPERT_GROUPS, EXPERTS_PER_GROUP, D_EXPERT
    D = D_MODEL
    n_idx = jnp.arange(P, dtype=f32)
    return {
        'x': nrm(ks[0], (BATCH, SEQ, D), 1.0),
        'norm_mix_g': 1.0 + nrm(ks[1], (L, D), 0.02),
        'norm_ffn_g': 1.0 + nrm(ks[2], (L, D), 0.02),
        'final_norm_g': 1.0 + nrm(ks[3], (D,), 0.02),
        'ssm_w_in': nrm(ks[4], (NA, D, D), D ** -0.5),
        'ssm_lam_re': -0.5 + nrm(ks[5], (NA, G, P), 0.01),
        'ssm_lam_im': math.pi * n_idx + nrm(ks[6], (NA, G, P), 0.01),
        'ssm_log_dt': jax.random.uniform(ks[7], (NA, G), f32, math.log(DT_MIN), math.log(DT_MAX)),
        'ssm_b_re': nrm(ks[8], (NA, G, P, HG), (0.5 / HG) ** 0.5),
        'ssm_b_im': nrm(ks[9], (NA, G, P, HG), (0.5 / HG) ** 0.5),
        'ssm_c_re': nrm(ks[10], (NA, G, HG, P), (0.5 / P) ** 0.5),
        'ssm_c_im': nrm(ks[11], (NA, G, HG, P), (0.5 / P) ** 0.5),
        'ssm_d': nrm(ks[12], (NA, D), 1.0),
        'ssm_w_glu': nrm(ks[13], (NA, D, 2 * D), D ** -0.5),
        'attn_w_qkv': nrm(ks[14], (NB, D, 3 * D), D ** -0.5),
        'attn_lambda_q1': nrm(ks[15], (NB, DIFF_HEAD_DIM), 0.1),
        'attn_lambda_k1': nrm(ks[16], (NB, DIFF_HEAD_DIM), 0.1),
        'attn_lambda_q2': nrm(ks[17], (NB, DIFF_HEAD_DIM), 0.1),
        'attn_lambda_k2': nrm(ks[18], (NB, DIFF_HEAD_DIM), 0.1),
        'attn_subln_g': 1.0 + nrm(ks[19], (NB, V_HEAD_DIM), 0.02),
        'attn_w_o': nrm(ks[20], (NB, D, D), D ** -0.5),
        'moe_w_router_group': nrm(ks[21], (L, D, NG), D ** -0.5),
        'moe_b_router_group': nrm(ks[22], (L, NG), 0.01),
        'moe_w_router_expert': nrm(ks[23], (L, D, NG, NE), D ** -0.5),
        'moe_b_router_expert': nrm(ks[24], (L, NG, NE), 0.01),
        'moe_w_gate': nrm(ks[25], (L, NG, NE, D, F), D ** -0.5),
        'moe_w_up': nrm(ks[26], (L, NG, NE, D, F), D ** -0.5),
        'moe_w_down': nrm(ks[27], (L, NG, NE, F, D), F ** -0.5),
    }

def reference(x, norm_mix_g, norm_ffn_g, final_norm_g,
              ssm_w_in, ssm_lam_re, ssm_lam_im, ssm_log_dt, ssm_b_re, ssm_b_im,
              ssm_c_re, ssm_c_im, ssm_d, ssm_w_glu,
              attn_w_qkv, attn_lambda_q1, attn_lambda_k1, attn_lambda_q2, attn_lambda_k2,
              attn_subln_g, attn_w_o,
              moe_w_router_group, moe_b_router_group, moe_w_router_expert, moe_b_router_expert,
              moe_w_gate, moe_w_up, moe_w_down):
    cos, sin = rope_tables(x.shape[1])
    for i in range(DEPTH):
        h = rms_norm(x, norm_mix_g[i])
        j = i // N_MIXERS
        if i % N_MIXERS == 0:
            mix = s5_mixer(h, ssm_w_in[j], ssm_lam_re[j], ssm_lam_im[j], ssm_log_dt[j],
                           ssm_b_re[j], ssm_b_im[j], ssm_c_re[j], ssm_c_im[j], ssm_d[j], ssm_w_glu[j])
        else:
            lambda_init = 0.8 - 0.6 * math.exp(-0.3 * i)
            mix = diff_attention(h, attn_w_qkv[j], attn_lambda_q1[j], attn_lambda_k1[j],
                                 attn_lambda_q2[j], attn_lambda_k2[j], attn_subln_g[j], attn_w_o[j],
                                 cos, sin, lambda_init)
        x = x + mix
        h = rms_norm(x, norm_ffn_g[i])
        x = x + hier_moe(h, moe_w_router_group[i], moe_b_router_group[i], moe_w_router_expert[i],
                         moe_b_router_expert[i], moe_w_gate[i], moe_w_up[i], moe_w_down[i])
    return rms_norm(x, final_norm_g)


_drawn_inputs = setup_inputs


def setup_inputs(seed=0):
    import zlib

    import numpy as np

    out = dict(_drawn_inputs(seed))
    spreads = {}
    factors = {'final_norm_g': 3.013, 'ssm_lam_re': 8.0, 'attn_subln_g': 3.108}
    for name, (base, spread) in spreads.items():
        noise = np.random.default_rng([zlib.crc32(name.encode()), seed]).standard_normal(out[name].shape)
        drawn = base * np.exp(spread * noise) if base else spread * noise
        out[name] = __import__('jax').numpy.asarray(drawn.astype(out[name].dtype))
    for name, factor in factors.items():
        out[name] = (out[name] * factor).astype(out[name].dtype)
    return out
```

```python
import math
from contextlib import ExitStack

import numpy as np
import concourse.bass as bass
from concourse import mybir

F32 = mybir.dt.float32
I32 = mybir.dt.int32
ALU = mybir.AluOpType
ACT = mybir.ActivationFunctionType
AX = mybir.AxisListType

P = 128
D = 1024
T = 256
TT = T // P
KD = D // P
EPS = 1e-6
SB = 4
M = T // SB
PAIRS = 32
PC = 32
OCT = 8
H = 8
DH = 64
CHUNK = 64
NG, NE, FE = 4, 8, 256
E = NG * NE
QE = 4
NQ = E // QE
SLOTS = 32
MAXPASS = T // SLOTS
UNIT = 4096
UNITS = 6
NO = -1.0e30

C_ID = 0
C_BEFORE = C_ID + P
C_ONES = C_BEFORE + P
C_SLOT = C_ONES + P
C_SKIP = C_SLOT + T
C_ROPE = C_SKIP + P
C_ZERO = C_ROPE + TT * 4 * 32
C_STEP = C_ZERO + 96
C_UPTO = C_STEP + NQ * 7
C_TURN = C_UPTO + 9 * 8
C_N = C_TURN + 1


def constants():
    c = np.zeros((P, C_N), np.float32)
    i = np.arange(P)
    c[:, C_ID:C_ID + P] = np.eye(P)
    c[:, C_BEFORE:C_BEFORE + P] = i[:, None] < i[None, :]
    c[:, C_ONES:C_ONES + P] = 1.0
    c[:, C_SLOT:C_SLOT + T] = np.arange(1, T + 1)
    c[:, C_SKIP:C_SKIP + P] = (i[:, None] % 32 == i[None, :] % 32) & (i[None, :] // 32 == 3 - i[:, None] // 32)
    inv = np.float32(10000.0) ** (-np.arange(0, DH, 2, dtype=np.float32) / np.float32(DH))
    ang = np.arange(T, dtype=np.float32)[:, None] * inv[None, :]
    cos, sin = np.cos(ang).astype(np.float32), np.sin(ang).astype(np.float32)
    rope = np.concatenate([cos, cos, -sin, sin], axis=1).reshape(TT, P, 128)
    for tt in range(TT):
        c[:, C_ROPE + 128 * tt:C_ROPE + 128 * (tt + 1)] = rope[tt]
    c[:, C_STEP:C_STEP + NQ * 7] = np.tile(SLOTS * np.arange(1, 8), NQ)
    c[:, C_UPTO:C_UPTO + 72] = (np.arange(8)[None, :] < np.arange(9)[:, None]).reshape(-1)
    c[:, C_TURN] = math.pi / 2
    return c


def spread(ap, axis, n):
    a = ap.unsqueeze(axis)
    shape = list(a.shape)
    shape[axis] = n
    return a.to_broadcast(shape)


def build(nc, a, out):
    with ExitStack() as ctx:
        ctx.enter_context(nc.allow_non_contiguous_dma(reason="short runs of the small parameters"))

        def sb(name, shape, dt=F32):
            return ctx.enter_context(nc.sbuf_tensor(name, shape, dt))

        def sem(name):
            return ctx.enter_context(nc.semaphore(name))

        ring = sb("ring", [P, UNITS, UNIT])
        x = sb("x", [P, TT, D])
        xr = sb("xr", [P, TT, KD, P])
        hT = sb("hT", [P, KD, T])
        gains = sb("gains", [P, 2, D])
        con = sb("con", [P, C_N])
        wr = sb("wr", [P, 2, KD, NG + E])
        rb = sb("rb", [P, 2, NG + E])
        small = sb("small", [P, 64])
        cum = [sb(f"cum{l}", [P, 17], I32) for l in range(2)]
        work = sb("work", [P, 18400])
        ps = ctx.enter_context(nc.psum_tensor("ps", [P, 8, 512], F32))

        ident = con[:, C_ID:C_ID + P]
        before = con[:, C_BEFORE:C_BEFORE + P]
        ones = con[:, C_ONES:C_ONES + P]

        def part(off, n):
            return work[:, off:off + n]

        Fw = part(0, 4096).rearrange("p (r c) -> p r c", r=PAIRS)
        W2 = part(4096, 8192).rearrange("p (i r c) -> p i r c", i=2, r=PAIRS)
        X = part(12288, (M + 1) * 64).rearrange("p (m i r) -> p m i r", i=2, r=PAIRS)
        o = 12288 + (M + 1) * 64
        Pw = part(o, 3 * 5 * PAIRS).rearrange("p (i j r) -> p i j r", i=3, j=5)
        o += 480
        LB = part(o, 64).rearrange("p (i r) -> p i r", i=2)
        o += 64
        LA = part(o, 64).rearrange("p (i r) -> p i r", i=2)
        o += 64
        sc2 = part(o, 64).rearrange("p (i r) -> p i r", i=2)
        o += 64
        dcol = part(o, 32)
        o += 32
        step = part(o, 192).rearrange("p (n i r) -> p n i r", n=3, i=2)
        o += 192
        drep = part(o, 128)
        o += 128
        assert o <= 18400
        U4 = hT[:].rearrange("p k t -> p (k t)").rearrange("p (r m) -> p r m", r=PAIRS)
        gT = xr[:].rearrange("p a k q -> p (a k q)").rearrange("p (c t) -> p c t", c=KD)
        pre = ring[:, 3:6, :].rearrange("p u n -> p (u n)")
        W1 = pre[:, 0:2048].rearrange("p (i r j c) -> p i r j c", i=2, r=OCT, j=SB)
        W1T = pre[:, 2048:4096].rearrange("p (i r c) -> p i r c", i=2, r=OCT)
        Bn = pre[:, 4096:5120].rearrange("p (i r c) -> p i r c", i=2, r=PAIRS)
        Bb = pre[:, 5120:6144].rearrange("p (i r c) -> p i r c", i=2, r=PAIRS)
        Cn = pre[:, 6144:7168].rearrange("p (i c s) -> p i c s", i=2, c=KD)
        Cc = pre[:, 7168:8192].rearrange("p (i r c) -> p i r c", i=2, r=PAIRS)
        Cb = pre[:, 8192:10240].rearrange("p (i r c) -> p i r c", i=2, r=PAIRS)
        t1 = pre[:, 10240:10752]
        t2 = pre[:, 10752:11264]
        lam = pre[0:32, 11264:12288].rearrange("p (n c) -> p n c", c=P)
        lam2 = xr[0:32, 0, :, :]
        sig = part(12288, 1024).rearrange("p (n c) -> p n c", n=2)
        o = 0
        xg = part(o, 1024).rearrange("p (k s) -> p k s", k=KD)
        o += 1024
        sel = part(o, 256).rearrange("p (a s) -> p a s", a=TT)
        o += 256
        scw = part(o, 256).rearrange("p (a s) -> p a s", a=TT)
        o += 256
        sil = part(o, 256)
        o += 256
        hid = part(o, 256)
        o += 256
        hidT = part(o, 256)
        o += 256
        swT = part(o, 256)
        o += 256
        yy = part(o, 1024)
        o += 1024
        lg = part(o, 72).rearrange("p (a n) -> p a n", a=TT)
        o += 72
        slot1 = part(o, 64).rearrange("p (a e) -> p a e", a=TT)
        o += 64
        comb = part(o, 64).rearrange("p (a e) -> p a e", a=TT)
        o += 64
        msk = part(o, 64).rearrange("p (a e) -> p a e", a=TT)
        o += 64
        rt = part(o, 512)
        o += 512
        assert o <= 8192
        wo = part(10208, 8192).rearrange("p (k n) -> p k n", k=KD)
        qk = part(0, 4096).rearrange("p (h t) -> p h t", h=16)
        vv = part(4096, 2048).rearrange("p (a n) -> p a n", a=TT)
        nat = part(6144, 2048)
        osb = nat.rearrange("p (a n) -> p a n", a=TT)
        oT = part(0, 2048).rearrange("p (k t) -> p k t", k=KD)
        at = part(8192, 256)
        atT = part(8448, 256)
        rope1 = part(8704, 512)
        rope2 = part(9216, 512)
        pv_rest = part(9728, 480)
        Pb = part(8704, 1024).rearrange("p (b i n) -> p b i n", b=2, i=2)
        lam4 = pv_rest[:, 0:256].rearrange("p (n c) -> p n c", n=4)
        subg = pv_rest[:, 256:384]
        asm = pv_rest[:, 384:480]

        s_con, s_x, s_lam, s_bc, s_router, s_gain, s_att, s_wo = (
            sem(n) for n in ("con_in", "x_in", "lam_in", "bc_in", "router_in", "gain_in", "att_in", "wo_in"))
        landed = [sem(f"landed{u}") for u in range(UNITS)]
        used = [sem(f"used{u}") for u in range(UNITS)]
        out_done = sem("out_done")
        dstep, pstep = sem("dve_steps"), sem("pool_steps")
        squares, var_ready, root_ready, normed = (sem(n) for n in ("squares", "var_ready", "root_ready", "normed"))
        hT_psum, hT_ready = sem("hT_psum"), sem("hT_ready")
        mixed = sem("mixed")
        dt_ready, er_ready, arg_ready, sin_ready = (sem(n) for n in ("dt_ready", "er_ready", "arg_ready", "sin_ready"))
        lam_ready, lam_psum, c_psum, c_ready = (sem(n) for n in ("lam_ready", "lam_psum", "c_psum", "c_ready"))
        cleared = sem("cleared")
        u_done, u4_act, u4_dve = sem("u_done"), sem("u4_act"), sem("u4_dve")
        w1_ready, w2_ready, w1_turned, w1T_ready = (sem(n) for n in ("w1_ready", "w2_ready", "w1_turned", "w1T_ready"))
        f_done, f_ready, v_done, v_ready = (sem(n) for n in ("f_done", "f_ready", "v_done", "v_ready"))
        drep_ready, prod_a, prod_b, summed, state = (sem(n) for n in ("drep_ready", "prod_a", "prod_b", "summed", "state"))
        y_done, g_ready = sem("y_done"), sem("g_ready")
        glu_done, sig_ready, glu_prod = sem("glu_done"), sem("sig_ready"), sem("glu_prod")
        logits_done, gate_sub, gate_exp, mask_ready, pos_done, cum_ready = (
            sem(n) for n in ("logits_done", "gate_sub", "gate_exp", "mask_ready", "pos_done", "cum_ready"))
        sel_built, sel_ready, sw_turned, sw_ready, gathered, xg_ready = (
            sem(n) for n in ("sel_built", "sel_ready", "sw_turned", "sw_ready", "gathered", "xg_ready"))
        gu_done, sil_ready, hid_ready, hid_turned, hidT_ready, down_done, y_ready, scattered, x_added = (
            sem(n) for n in ("gu_done", "sil_ready", "hid_ready", "hid_turned", "hidT_ready", "down_done",
                             "y_ready", "scattered", "x_added"))
        qkv_done, qkv_kept, v_kept, qk_turned, qkT_ready = (
            sem(n) for n in ("qkv_done", "qkv_kept", "v_kept", "qk_turned", "qkT_ready"))
        lam_sum, lam_exp = sem("lam_sum"), sem("lam_exp")
        scores_done, peak_ready, exp_ready, att_ready, att_turned, attT_ready, av_done = (
            sem(n) for n in ("scores_done", "peak_ready", "exp_ready", "att_ready", "att_turned", "attT_ready", "av_done"))
        osq, ovar, oroot, o_ready, o_turned, oT_ready, wo_done = (
            sem(n) for n in ("osq", "ovar", "oroot", "o_ready", "o_turned", "oT_ready", "wo_done"))
        final_ready = sem("final_ready")

        win = [ring[:, u, :].rearrange("p (k n) -> p k n", k=KD) for u in range(UNITS)]
        gu = [ring[:, u, :].rearrange("p (e g k f) -> p e g k f", e=QE, g=2, k=2) for u in range(4)]
        dn = [ring[:, 4 + u, :].rearrange("p (e n) -> p e n", e=QE) for u in range(2)]

        def qround(l, q):
            return l * (NQ + 1) + 1 + q

        MOST = 2 * MAXPASS * NQ

        def passes_of(eng, l, q):
            return (eng.value_load(cum[l][0:1, bass.ds(q + NQ, 1)], min_val=0, max_val=MOST),
                    eng.value_load(cum[l][0:1, bass.ds(q, 1)], min_val=1, max_val=MAXPASS))

        def passes_through(eng, l):
            return eng.value_load(cum[l][0:1, 2 * NQ:2 * NQ + 1], min_val=0, max_val=MOST)

        def stack(copy, n):
            quad, j = n // 4, n % 4
            ups = ps[:, 0:4, :].rearrange("p b n -> p (b n)").rearrange("p (c m s) -> p c m s", c=KD, s=SB)
            dst = U4[32 * j:32 * j + 32, :, :].rearrange("p (c a) m -> p c a m", a=4)[:, :, quad, :]
            return copy(dst, ups[32 * quad:32 * quad + 32, :, :, SB - 1 - j])

        block = ctx.enter_context(nc.Block())

        @block.sync
        def _(sp):
            sp.dma_start(con[:], a["con"]).then_inc(s_con, 16)
            sp.dma_start(x[:], a["x"].rearrange("b (a p) d -> p (b a) d", p=P)).then_inc(s_x, 16)

            def columns(u, w, c0, kp):
                src = w.rearrange("(p k) n -> p k n" if kp else "(k p) n -> p k n", k=KD)
                for half in range(2):
                    sp.dma_start(win[u][:, 4 * half:4 * half + 4, :],
                                 src[:, 4 * half:4 * half + 4, c0:c0 + 512]).then_inc(landed[u], 16)

            for u in range(2):
                columns(u, a["ssm_w_in"][0], 512 * u, True)
            columns(2, a["ssm_w_glu"][0], 0, False)
            sp.wait_ge(v_done, 8)
            sp.wait_ge(w1T_ready, 16)
            sp.wait_ge(f_done, 8)
            sp.wait_ge(w2_ready, 4)
            for u in range(3, 6):
                columns(u, a["ssm_w_glu"][0], 512 * (u - 2), False)

            def quartet(l, q):
                def experts(name):
                    w = a[name][l].rearrange("g e r c -> (g e) (r c)")
                    return w[bass.ds(q * QE, QE), :]

                base = l + 1 + before_q
                for u in range(4):
                    sp.wait_ge(used[u], base)
                    for g, name in enumerate(("moe_w_gate", "moe_w_up")):
                        src = experts(name).rearrange("e (p n) -> p e n", p=P)[:, :, 512 * u:512 * u + 512]
                        sp.dma_start(gu[u][:, :, g, :, :].rearrange("p e k f -> p e (k f)"), src).then_inc(landed[u], 16)
                for u in range(2):
                    sp.wait_ge(used[4 + u], base)
                    src = experts("moe_w_down").rearrange("e (k p n) -> p k e n", k=2, p=P)
                    for half in range(2):
                        sp.dma_start(dn[u][:, 2 * half:2 * half + 2, :],
                                     src[:, u, 2 * half:2 * half + 2, :]).then_inc(landed[4 + u], 16)

            for l in range(2):
                before_q = 0 if l == 0 else total
                quartet(l, 0)
                if l == 0:
                    sp.wait_ge(g_ready, 16)
                    sp.wait_ge(mixed, 4)
                    sp.dma_start(wo, a["attn_w_o"][0].rearrange("(k p) n -> p k n", p=P)).then_inc(s_wo, 16)
                sp.wait_ge(cum_ready, l + 1)
                with sp.Fori(1, NQ) as q:
                    before_q, _ = passes_of(sp, l, q)
                    quartet(l, q)
                total = passes_through(sp, l)
                if l == 0:
                    for u in range(UNITS):
                        sp.wait_ge(used[u], total + 1)
                        columns(u, a["attn_w_qkv"][0], 512 * u, True)
            for tt in range(TT):
                sp.wait_ge(final_ready, tt + 1)
                sp.dma_start(out[0, tt * P:(tt + 1) * P, :], xr[:, tt, :, :].rearrange("p k q -> p (k q)")).then_inc(out_done, 16)
            sp.wait_ge(out_done, 32)

        @block.gpsimd
        def _(pool):
            def gain(i, src):
                pool.dma_start(gains[:, i % 2, :], src.partition_broadcast(P)).then_inc(s_gain, 16)

            pool.memset(part(4096, 8192), 0.0).then_inc(cleared, 1)
            pool.memset(X[:, 0, :, :], 0.0).then_inc(cleared, 1)
            pool.memset(pre[:, 8192:10240], 0.0).then_inc(cleared, 1)
            pool.memset(pre[:, 0:2048], 0.0).then_inc(cleared, 1)
            gs = [a["norm_mix_g"][0], a["norm_ffn_g"][0], a["norm_mix_g"][1], a["norm_ffn_g"][1], a["final_norm_g"]]
            for i, g in enumerate(gs):
                if i >= 1:
                    pool.wait_ge(s_gain, 16 * i)
                if i >= 2:
                    pool.wait_ge(normed, 2 * (i - 1))
                gain(i, g)
            pool.wait_ge(s_gain, 16 * len(gs))

        @block.scalar
        def _(act):
            def dma(dst, src, s):
                act.dma_start(dst, src).then_inc(s, 16)

            dma(lam[:, 0, :], a["ssm_lam_re"][0].rearrange("(r g) p -> r (g p)", g=2), s_lam)
            dma(lam[:, 1, :], a["ssm_lam_im"][0].rearrange("(r g) p -> r (g p)", g=2), s_lam)
            dma(small[0:32, 0:2], a["ssm_log_dt"][0].rearrange("(r g) -> r g", g=2), s_lam)
            dma(drep[0:32, 0:32], a["ssm_d"][0].rearrange("(r c) -> r c", c=PC), s_lam)
            for i, n in enumerate(("re", "im")):
                dma(Bn[:, i, :, :], a["ssm_b_" + n][0].rearrange("(r g) p h -> (g p) r h", g=2), s_bc)
                dma(Cn[:, i, :, :], a["ssm_c_" + n][0].rearrange("(c g) h p -> (g h) c p", g=8), s_bc)
            for l in range(2):
                dma(wr[:, l, :, 0:NG], a["moe_w_router_group"][l].rearrange("(p k) n -> p k n", k=KD), s_router)
                dma(wr[:, l, :, NG:], a["moe_w_router_expert"][l].rearrange("(p k) g e -> p k (g e)", k=KD), s_router)
                dma(rb[:, l, 0:NG], a["moe_b_router_group"][l].partition_broadcast(P), s_router)
                dma(rb[:, l, NG:], a["moe_b_router_expert"][l].rearrange("g e -> (g e)").partition_broadcast(P), s_router)

            def norm(i):
                for tt in range(TT):
                    act.activation(xr[:, tt, :, :].rearrange("p k q -> p (k q)"), x[:, tt, :], ACT.Square,
                                   accum_out=small[:, 8 + tt:9 + tt]).then_inc(squares, 1)
                act.wait_ge(var_ready, i + 1)
                act.activation(small[:, 12:14], small[:, 10:12], ACT.Sqrt).then_inc(root_ready, 1)
                if i < 4:
                    act.wait_ge(hT_psum, i + 1)
                    for b in range(4):
                        act.copy(hT[:, 2 * b:2 * b + 2, :].rearrange("p k t -> p (k t)"), ps[:, b, :]).then_inc(hT_ready, 1)

            act.wait_ge(s_lam, 64)
            act.activation(small[0:32, 2:4], small[0:32, 0:2], ACT.Exp).then_inc(dt_ready, 1)
            act.wait_ge(er_ready, 1)
            act.activation(lam[:, 4, :], lam[:, 2, :], ACT.Exp).then_inc(sin_ready, 1)
            act.wait_ge(arg_ready, 1)
            act.activation(lam[:, 5, :], lam[:, 5, :], ACT.Sin).then_inc(sin_ready, 1)
            act.activation(lam[:, 6, :], lam[:, 6, :], ACT.Sin).then_inc(sin_ready, 1)
            act.wait_ge(s_x, 16)
            act.wait_ge(lam_psum, 5)
            norm(0)
            act.wait_ge(c_psum, 1)
            for i in range(2):
                act.copy(Cc[:, i, :, :].rearrange("p r c -> p (r c)"), ps[:, 4 + i, :]).then_inc(c_ready, 1)

            act.wait_ge(u_done, 8)
            for n in range(8):
                stack(act.copy, n).then_inc(u4_act, 1)
            for o in range(PAIRS // OCT):
                act.wait_ge(w1_turned, o + 1)
                if o >= 1:
                    act.wait_ge(v_done, 2 * o)
                for b in range(4):
                    act.copy(W1T[:, b // 2, 4 * (b % 2):4 * (b % 2) + 4, :].rearrange("p r c -> p (r c)"),
                             ps[:, b, :]).then_inc(w1T_ready, 1)
                act.wait_ge(v_done, 2 * o + 2)
                for b in range(2):
                    src = ps[:, 4 + b, :].rearrange("p (r i m) -> p m i r", r=4, i=2)
                    for i in range(2):
                        act.copy(X[:, 1:M + 1, i, OCT * o + 4 * b:OCT * o + 4 * b + 4], src[:, :, i, :]).then_inc(v_ready, 1)
            act.wait_ge(y_done, PAIRS)
            for n in range(16):
                quad, s = n // 4, n % 4
                src = ps[32 * s:32 * s + 32, 0:4, :].rearrange("p b (c a m) -> p b c a m", c=2, a=4)
                src = src.rearrange("p b c a m -> p (b c) a m")[:, :, quad, :]
                dst = gT[32 * quad:32 * quad + 32, :, :].rearrange("p c (m s) -> p c m s", s=SB)[:, :, :, s]
                act.activation(dst, src, ACT.Gelu_apprx_tanh).then_inc(g_ready, 1)
            for n in range(4):
                act.wait_ge(glu_done, n + 1)
                if n >= 1:
                    act.wait_ge(mixed, n)
                act.activation(sig[:, 0, :], ps[:, 2 * (n % 2) + 1, :], ACT.Sigmoid).then_inc(sig_ready, 1)

            def moe(l):
                act.wait_ge(gate_sub, 2 * l + 1)
                act.activation(rt[:, 8:16], rt[:, 8:16], ACT.Exp).then_inc(gate_exp, 1)
                act.wait_ge(gate_sub, 2 * l + 2)
                act.activation(rt[:, 128:144], rt[:, 128:144], ACT.Exp).then_inc(gate_exp, 1)
                act.wait_ge(cum_ready, l + 1)
                with act.Fori(0, NQ) as q:
                    n0, passes = passes_of(act, l, q)
                    with act.Fori(0, passes) as p:
                        n = n0 + p
                        act.wait_ge(sw_turned, n + 2)
                        act.copy(swT, ps[:, 3, 0:256]).then_inc(sw_ready, 1)
                        act.wait_ge(gathered, n + 2)
                        act.copy(xg[:, 4:8, :].rearrange("p k s -> p (k s)"), ps[:, 1, :]).then_inc(xg_ready, 1)
                        act.wait_ge(gu_done, n + 1)
                        act.activation(sil, ps[:, 2, 0:256], ACT.Silu).then_inc(sil_ready, 1)
                        act.wait_ge(down_done, n + 1)
                        act.copy(yy[:, 0:512], ps[:, 4, :]).then_inc(y_ready, 1)
                total = passes_through(act, l)
                act.wait_ge(x_added, 2 * total + 1)

            act.wait_ge(mixed, 4)
            norm(1)
            moe(0)
            for n, name in enumerate(("q1", "k1", "q2", "k2")):
                dma(lam4[:, n, :], a["attn_lambda_" + name][0].partition_broadcast(P), s_att)
            dma(subg, a["attn_subln_g"][0].partition_broadcast(P), s_att)
            norm(2)
            act.wait_ge(lam_sum, 1)
            act.activation(asm[:, 2:4], asm[:, 0:2], ACT.Exp).then_inc(lam_exp, 1)
            for tt in range(TT):
                for c in range(2):
                    act.wait_ge(qkv_done, 6 * tt + 5 + c)
                    act.copy(vv[:, tt, 512 * c:512 * c + 512], ps[:, 4 + c, :]).then_inc(v_kept, 1)
                for c in range(4):
                    act.wait_ge(qk_turned, 4 * tt + c + 1)
                    act.copy(qk[:, 4 * c:4 * c + 4, tt * P:(tt + 1) * P],
                             ps[:, 6 + c % 2, :].rearrange("p (h t) -> p h t", h=4)).then_inc(qkT_ready, 1)

            def soft(i):
                keys = P * (i // H + 1)
                act.wait_ge(peak_ready, i + 1)
                if i >= 2:
                    act.wait_ge(att_ready, i - 1)
                for j in range(2):
                    act.activation(Pb[:, i % 2, j, 0:keys], ps[:, 2 * (i % 2) + j, 0:keys], ACT.Exp,
                                   bias=asm[:, 8 + 2 * (i % 2) + j:9 + 2 * (i % 2) + j], scale=DH ** -0.5,
                                   accum_out=asm[:, 12 + 2 * (i % 2) + j:13 + 2 * (i % 2) + j]).then_inc(exp_ready, 1)

            act.wait_ge(qkv_kept, 8)
            soft(0)
            for i in range(2 * H):
                if i + 1 < 2 * H:
                    soft(i + 1)
                keys = P * (i // H + 1)
                act.wait_ge(att_turned, i + 1)
                if i >= 1:
                    act.wait_ge(av_done, i)
                act.copy(atT[:, 0:keys], ps[:, 4, 0:keys]).then_inc(attT_ready, 1)
                if i % H == H - 1:
                    act.wait_ge(av_done, i + 1)
                    b = i // H
                    for c in range(2):
                        act.copy(osb[:, b, 512 * c:512 * c + 512], ps[:, 6 + c, :]).then_inc(osq, 1)
            for b in range(2):
                act.wait_ge(ovar, b + 1)
                act.activation(asm[:, 32 + 8 * b:40 + 8 * b], asm[:, 16 + 8 * b:24 + 8 * b], ACT.Sqrt).then_inc(oroot, 1)
            for b in range(2):
                act.wait_ge(o_turned, b + 1)
                for c in range(2):
                    act.copy(oT[:, 4 * c:4 * c + 4, b * P:(b + 1) * P],
                             ps[:, 4 + c, :].rearrange("p (h t) -> p h t", h=4)).then_inc(oT_ready, 1)
            act.wait_ge(mixed, 8)
            norm(3)
            moe(1)
            norm(4)

        @block.vector
        def _(dve):
            count = [0]

            def link(ins):
                count[0] += 1
                ins.then_inc(dstep, 1)
                dve.wait_ge(dstep, count[0])

            TTo, TS, STT, RED = dve.tensor_tensor, dve.tensor_scalar, dve.scalar_tensor_tensor, dve.tensor_reduce

            def norm(i):
                dve.wait_ge(squares, 2 * i + 2)
                TS(small[:, 10:12], small[:, 8:10], 1.0 / D, EPS, ALU.mult, ALU.add).then_inc(var_ready, 1)
                dve.wait_ge(root_ready, i + 1)
                link(dve.reciprocal(small[:, 14:16], small[:, 12:14]))
                dve.wait_ge(s_gain, 16 * (i + 1))
                for tt in range(TT):
                    if i < 4:
                        STT(xr[:, tt, :, :], x[:, tt, :].rearrange("p (q k) -> p k q", k=KD), small[:, 14 + tt:15 + tt],
                            gains[:, i % 2, :].rearrange("p (q k) -> p k q", k=KD), ALU.mult, ALU.mult).then_inc(normed, 1)
                    else:
                        STT(xr[:, tt, :, :].rearrange("p k q -> p (k q)"), x[:, tt, :], small[:, 14 + tt:15 + tt],
                            gains[:, i % 2, :], ALU.mult, ALU.mult).then_inc(final_ready, 1)

            for first in (state, hidT_ready, x_added, y_ready):
                dve.sem_inc(first, 1)
            L = lambda n: lam[:, n, :]
            V = lambda n: lam2[:, n, :]
            dve.wait_ge(dt_ready, 1)
            dtb = spread(small[0:32, 2:4], 2, 64)
            two = lambda v: v.rearrange("p (g c) -> p g c", g=2)
            TTo(two(L(2)), two(L(0)), dtb, ALU.mult).then_inc(er_ready, 1)
            link(TTo(two(L(3)), two(L(1)), dtb, ALU.mult))
            MAGIC = 1.5 * 2.0 ** 23
            link(TS(V(0), L(3), 1.0 / (2 * math.pi), MAGIC, ALU.mult, ALU.add))
            link(TS(V(0), V(0), -MAGIC, None, ALU.add))
            C1 = 6.28125
            C2 = float(np.float32(np.round((2 * math.pi - C1) * 2.0 ** 22) / 2.0 ** 22))
            C3 = 2 * math.pi - C1 - C2
            link(STT(V(1), V(0), -C1, L(3), ALU.mult, ALU.add))
            link(STT(V(1), V(0), -C2, V(1), ALU.mult, ALU.add))
            link(STT(V(1), V(0), -C3, V(1), ALU.mult, ALU.add))
            PI_IN = 3.1415925
            link(TS(L(6), V(1), PI_IN, -PI_IN, ALU.min, ALU.max))
            link(STT(V(2), L(6), -1.0, L(6), ALU.mult, ALU.max))
            link(TS(L(5), V(2), -1.0, math.pi / 2, ALU.mult, ALU.add))
            dve.sem_inc(arg_ready, 1)
            link(TTo(V(0), L(0), L(0), ALU.mult))
            link(TTo(V(1), L(1), L(1), ALU.mult))
            link(TTo(V(0), V(0), V(1), ALU.add))
            link(dve.reciprocal(V(0), V(0)))
            dve.wait_ge(sin_ready, 3)
            link(TTo(V(1), L(4), L(5), ALU.mult))
            link(TTo(V(2), L(4), L(6), ALU.mult))
            link(TS(V(3), V(1), -1.0, None, ALU.add))
            link(TTo(V(4), V(3), L(0), ALU.mult))
            link(TTo(V(5), V(2), L(1), ALU.mult))
            link(TTo(V(4), V(4), V(5), ALU.add))
            link(TTo(V(5), V(2), L(0), ALU.mult))
            link(TTo(V(6), V(3), L(1), ALU.mult))
            link(TTo(V(5), V(5), V(6), ALU.subtract))
            link(TTo(V(3), V(4), V(0), ALU.mult))
            link(TTo(V(4), V(5), V(0), ALU.mult))
            link(dve.tensor_copy(V(5).rearrange("p (j c) -> p j c", j=4), spread(drep[0:32, 0:32], 1, 4)))
            dve.sem_inc(lam_ready, 1)
            dve.wait_ge(lam_psum, 5)
            TP = ps[:, 6, 0:160].rearrange("p (n r) -> p n r", n=5)
            dve.memset(Pw[:, 0, 0, :], 1.0)
            dve.memset(Pw[:, 1:3, 0, :], 0.0)
            dve.tensor_copy(Pw[:, 0, 1, :], TP[:, 0, :])
            dve.tensor_copy(Pw[:, 1, 1, :], TP[:, 1, :])
            dve.tensor_copy(sc2[:], TP[:, 2:4, :])
            link(dve.tensor_copy(dcol, TP[:, 4, :]))
            sq = step[:, :, :, :].rearrange("p n i r -> p (n i) r")

            def cmul(lo, n, by, base):
                r = lambda i: Pw[:, i, base:base + n, :]
                b = lambda i: spread(Pw[:, i, by, :], 1, n)
                TTo(sq[:, 0:n, :], r(0), b(0), ALU.mult)
                link(TTo(sq[:, 2:2 + n, :], r(1), b(1), ALU.mult))
                link(TTo(Pw[:, 0, lo:lo + n, :], sq[:, 0:n, :], sq[:, 2:2 + n, :], ALU.subtract))
                TTo(sq[:, 0:n, :], r(0), b(1), ALU.mult)
                link(TTo(sq[:, 2:2 + n, :], r(1), b(0), ALU.mult))
                link(TTo(Pw[:, 1, lo:lo + n, :], sq[:, 0:n, :], sq[:, 2:2 + n, :], ALU.add))

            cmul(2, 1, 1, 1)
            cmul(3, 2, 2, 1)
            link(TS(Pw[:, 2, 1:5, :], Pw[:, 1, 1:5, :], -1.0, None, ALU.mult))
            dve.tensor_copy(LA[:, 0, :], Pw[:, 0, 4, :])
            dve.tensor_copy(LA[:, 1, :], Pw[:, 0, 4, :])
            dve.tensor_copy(LB[:, 0, :], Pw[:, 2, 4, :])
            link(dve.tensor_copy(LB[:, 1, :], Pw[:, 1, 4, :]))
            norm(0)
            dve.wait_ge(s_bc, 64)
            r16 = lambda v: v.rearrange("p (r c) -> p r c", r=PAIRS)
            for i in range(2):
                TTo(r16(t1), Bn[:, i, :, :], spread(sc2[:, 0, :], 2, 16), ALU.mult)
                link(TTo(r16(t2), Bn[:, 1 - i, :, :], spread(sc2[:, 1, :], 2, 16), ALU.mult))
                link(TTo(Bb[:, i, :, :], r16(t1), r16(t2), ALU.add if i else ALU.subtract))
            dve.wait_ge(c_ready, 2)
            dve.wait_ge(cleared, 4)
            for g in range(2):
                h = slice(64 * g, 64 * g + 64)
                dve.tensor_copy(Cb[h, 0, :, 16 * g:16 * g + 16], Cc[h, 0, :, :])
                link(TS(Cb[h, 1, :, 16 * g:16 * g + 16], Cc[h, 1, :, :], -1.0, None, ALU.mult))
            dve.wait_ge(u_done, 8)
            for n in range(8, 16):
                stack(dve.tensor_copy, n).then_inc(u4_dve, 1)
            v4 = lambda v: v.rearrange("p (r j c) -> p r j c", r=OCT, j=SB)
            for o in range(PAIRS // OCT):
                pr = slice(OCT * o, OCT * o + OCT)
                pw = lambda i, lo: spread(Pw[:, i, lo:lo + 4, pr].rearrange("p j r -> p r j"), 3, 16)
                bb = lambda i: spread(Bb[:, i, pr, :], 2, SB)
                if o >= 1:
                    dve.wait_ge(w1_turned, o)
                    dve.wait_ge(f_done, 2 * o)
                for i in range(2):
                    TTo(v4(t1), pw(0, 0), bb(i), ALU.mult)
                    link(TTo(v4(t2), pw(1, 0), bb(1 - i), ALU.mult))
                    for g in range(2):
                        h = slice(64 * g, 64 * g + 64)
                        ins = TTo(W1[h, i, :, :, 16 * g:16 * g + 16], v4(t1)[h], v4(t2)[h], ALU.add if i else ALU.subtract)
                        if g == 0:
                            ins.then_inc(dstep, 1)
                            count[0] += 1
                    link(ins)
                dve.sem_inc(w1_ready, 1)
                cc = lambda i: spread(Cc[:, i, pr, :], 2, SB)
                for i in range(2):
                    TTo(v4(t1), pw(0 if i == 0 else 2, 1), cc(0), ALU.mult)
                    link(TTo(v4(t2), pw(1 if i == 0 else 0, 1), cc(1), ALU.mult))
                    for g in range(2):
                        h = slice(64 * g, 64 * g + 64)
                        dst = W2[h, i, pr, :].rearrange("p r (s c) -> p r s c", s=SB)[:, :, :, 16 * g:16 * g + 16]
                        ins = TTo(dst, v4(t1)[h], v4(t2)[h], ALU.subtract)
                        if g == 0:
                            ins.then_inc(dstep, 1)
                            count[0] += 1
                    link(ins)
                dve.sem_inc(w2_ready, 1)
                dve.wait_ge(f_done, 2 * o + 2)
                for r in range(OCT):
                    STT(Fw[:, OCT * o + r, :], con[:, C_SKIP:C_SKIP + P], dcol[:, OCT * o + r:OCT * o + r + 1],
                        ps[:, 6 + r // 4, P * (r % 4):P * (r % 4) + P], ALU.mult, ALU.add).then_inc(f_ready, 1)
            dve.wait_ge(v_ready, 16)
            UNR = 8
            with dve.Fori(0, M // UNR) as mb:
                for d in range(UNR):
                    m = mb * UNR + d
                    xm = X[:, bass.ds(m, 1), :, :].rearrange("p m i r -> p (m i) r")
                    xn = X[:, bass.ds(m + 1, 1), :, :].rearrange("p m i r -> p (m i) r")
                    dve.wait_ge(state, m + 1)
                    TTo(step[:, 0, :, :], LA[:], xm, ALU.mult).then_inc(prod_a, 1)
                    TTo(step[:, 1, 0, :], LB[:, 0, :], X[:, bass.ds(m, 1), 1, :].rearrange("p m r -> p (m r)"), ALU.mult).then_inc(prod_b, 1)
                    TTo(step[:, 1, 1, :], LB[:, 1, :], X[:, bass.ds(m, 1), 0, :].rearrange("p m r -> p (m r)"), ALU.mult).then_inc(prod_b, 1)
                    dve.wait_ge(prod_a, m + 1)
                    TTo(step[:, 2, :, :], step[:, 0, :, :], xn, ALU.add).then_inc(summed, 1)
                    dve.wait_ge(prod_b, 2 * m + 2)
                    dve.wait_ge(summed, m + 1)
                    TTo(xn, step[:, 2, :, :], step[:, 1, :, :], ALU.add).then_inc(state, 1)
            for n in range(4):
                tt, c = n // 2, n % 2
                dve.wait_ge(sig_ready, n + 1)
                link(TTo(sig[:, 1, :], ps[:, 2 * (n % 2), :], sig[:, 0, :], ALU.mult))
                TTo(x[:, tt, 512 * c:512 * c + 512], x[:, tt, 512 * c:512 * c + 512], sig[:, 1, :], ALU.add).then_inc(mixed, 1)

            def first_best(dst, v, n, best, tmp, least):
                link(RED(best, v, AX.X, ALU.max))
                link(TTo(tmp, v, spread(best, 2, n), ALU.is_equal))
                link(STT(tmp, tmp, -16.0, spread(con[:, C_SLOT:C_SLOT + n], 1, TT), ALU.mult, ALU.add))
                link(RED(least, tmp, AX.X, ALU.min))
                link(TTo(dst, tmp, spread(least, 2, n), ALU.is_equal))

            def moe(l):
                r = lambda off, n: rt[:, off:off + TT * n].rearrange("p (a n) -> p a n", a=TT)
                c2 = lambda off: rt[:, off:off + TT]
                r48 = lambda off: rt[:, off:off + 64].rearrange("p (a g e) -> p a g e", a=TT, g=NG)
                dve.wait_ge(s_router, 128)
                dve.wait_ge(logits_done, l + 1)
                link(dve.tensor_copy(lg, ps[:, 4, 0:72].rearrange("p (a n) -> p a n", a=TT)))
                gl, el = lg[:, :, 0:NG], lg[:, :, NG:].rearrange("p a (g e) -> p a g e", g=NG)
                link(RED(c2(0), gl, AX.X, ALU.max))
                TTo(r(8, 4), gl, spread(c2(0), 2, NG), ALU.subtract).then_inc(gate_sub, 1)
                link(TTo(r(16, 4), gl, spread(rb[:, l, 0:NG], 1, TT), ALU.add))
                first_best(r(24, 4), r(16, 4), NG, c2(2), r(32, 4), c2(4))
                goh = r(24, 4)
                dve.wait_ge(gate_exp, 2 * l + 1)
                link(RED(c2(40), r(8, 4), AX.X, ALU.add))
                link(dve.reciprocal(c2(42), c2(40)))
                link(TTo(r(32, 4), r(8, 4), goh, ALU.mult))
                link(RED(c2(44), r(32, 4), AX.X, ALU.add))
                link(TTo(c2(46), c2(44), c2(42), ALU.mult))
                gb = spread(goh, 3, NE)
                link(TTo(r48(192), el, gb, ALU.mult))
                link(RED(r(64, 8), r48(192).rearrange("p a g e -> p a e g"), AX.X, ALU.add))
                for tt in range(TT):
                    b48 = rb[:, l, NG:].rearrange("p (g e) -> p g e", g=NG)
                    link(TTo(r48(192)[:, tt], b48, spread(goh[:, tt, :], 2, NE), ALU.mult))
                link(RED(r(80, 8), r48(192).rearrange("p a g e -> p a e g"), AX.X, ALU.add))
                link(RED(c2(0), r(64, 8), AX.X, ALU.max))
                TTo(r(128, 8), r(64, 8), spread(c2(0), 2, NE), ALU.subtract).then_inc(gate_sub, 1)
                dve.wait_ge(gate_exp, 2 * l + 2)
                link(RED(c2(2), r(128, 8), AX.X, ALU.add))
                link(dve.reciprocal(c2(4), c2(2)))
                link(TTo(r(64, 8), r(128, 8), spread(c2(4), 2, NE), ALU.mult))
                link(TTo(r(96, 8), r(64, 8), r(80, 8), ALU.add))
                first_best(r(112, 8), r(96, 8), NE, c2(2), r(144, 8), c2(4))
                link(STT(r(96, 8), r(112, 8), NO, r(96, 8), ALU.mult, ALU.add))
                first_best(r(160, 8), r(96, 8), NE, c2(2), r(144, 8), c2(4))
                link(TTo(r(112, 8), r(112, 8), r(160, 8), ALU.add))
                link(TTo(r(64, 8), r(64, 8), r(112, 8), ALU.mult))
                link(RED(c2(2), r(64, 8), AX.X, ALU.add))
                link(dve.reciprocal(c2(4), c2(2)))
                link(TTo(c2(4), c2(4), c2(46), ALU.mult))
                link(TTo(r(64, 8), r(64, 8), spread(c2(4), 2, NE), ALU.mult))
                for tt in range(TT):
                    ge = lambda v: v[:, tt, :].rearrange("p (g e) -> p g e", g=NG)
                    gs = spread(goh[:, tt, :], 2, NE)
                    link(TTo(ge(msk), gs, spread(r(112, 8)[:, tt, :], 1, NG), ALU.mult))
                    link(TTo(ge(comb), gs, spread(r(64, 8)[:, tt, :], 1, NG), ALU.mult))
                dve.sem_inc(mask_ready, 1)
                dve.wait_ge(pos_done, l + 1)
                link(STT(slot1, ps[:, 5, 0:64].rearrange("p (a e) -> p a e", a=TT), 1.0, msk, ALU.add, ALU.mult))
                link(RED(rt[:, 0:8], ps[:, 5, 64:96].rearrange("p (q e) -> p q e", q=NQ), AX.X, ALU.max))
                link(TTo(rt[:, 64:120].rearrange("p (q s) -> p q s", q=NQ), spread(rt[:, 0:8], 2, 7),
                         con[:, C_STEP:C_STEP + 56].rearrange("p (q s) -> p q s", q=NQ), ALU.is_gt))
                link(RED(rt[:, 8:16], rt[:, 64:120].rearrange("p (q s) -> p q s", q=NQ), AX.X, ALU.add))
                link(TS(rt[:, 8:16], rt[:, 8:16], 1.0, None, ALU.add))
                link(TTo(rt[:, 128:200].rearrange("p (q s) -> p q s", q=9), spread(rt[:, 8:16], 1, 9),
                         con[:, C_UPTO:C_UPTO + 72].rearrange("p (q s) -> p q s", q=9), ALU.mult))
                link(RED(rt[:, 16:25], rt[:, 128:200].rearrange("p (q s) -> p q s", q=9), AX.X, ALU.add))
                if l == 1:
                    link(TS(rt[:, 16:25], rt[:, 16:25], small[:, 20:21], None, ALU.add))
                link(dve.tensor_copy(cum[l][:, 0:17], rt[:, 8:25]))
                if l == 0:
                    link(dve.tensor_copy(small[:, 20:21], rt[:, 24:25]))
                dve.sem_inc(cum_ready, 1)
                sel4 = lambda v: v.rearrange("p a (e s) -> p a e s", e=QE)
                with dve.Fori(0, NQ) as q:
                    n0, passes = passes_of(dve, l, q)
                    with dve.Fori(0, passes) as p:
                        n = n0 + p
                        p32 = p * SLOTS
                        dve.wait_ge(gathered, n + 1)
                        for tt in range(TT):
                            TTo(sel4(sel)[:, tt], spread(slot1[:, tt, bass.ds(q * QE, QE)], 2, SLOTS),
                                spread(con[:, bass.ds(p32 + C_SLOT, SLOTS)], 1, QE), ALU.is_equal).then_inc(sel_built, 1)
                        dve.wait_ge(sel_built, 2 * n + 2)
                        dve.wait_ge(sw_turned, n + 1)
                        for tt in range(TT):
                            TTo(sel4(scw)[:, tt], sel4(sel)[:, tt],
                                spread(comb[:, tt, bass.ds(q * QE, QE)], 2, SLOTS), ALU.mult).then_inc(sel_ready, 1)
                        dve.wait_ge(gathered, n + 2)
                        dve.tensor_copy(xg[:, 0:4, :].rearrange("p k s -> p (k s)"), ps[:, 0, :]).then_inc(xg_ready, 1)
                        dve.wait_ge(sil_ready, n + 1)
                        TTo(hid, ps[:, 2, 256:512], sil, ALU.mult).then_inc(hid_ready, 1)
                        dve.wait_ge(hid_turned, n + 1)
                        dve.tensor_copy(hidT, ps[:, 3, 256:512]).then_inc(hidT_ready, 1)
                        dve.wait_ge(down_done, n + 1)
                        dve.tensor_copy(yy[:, 512:1024], ps[:, 5, :]).then_inc(y_ready, 1)
                        for tt in range(TT):
                            dve.wait_ge(scattered, 2 * n + 1 + tt)
                            b = 6 if tt else 0
                            TTo(x[:, tt, :], x[:, tt, :], ps[:, b:b + 2, :].rearrange("p b n -> p (b n)"), ALU.add).then_inc(x_added, 1)

            norm(1)
            moe(0)
            norm(2)
            lambda_init = 0.8 - 0.6 * math.exp(-0.3)
            dve.wait_ge(s_att, 80)
            l4 = lam4.rearrange("p (n i) c -> p n i c", i=2)
            link(TTo(rope1[:, 0:128].rearrange("p (n c) -> p n c", n=2), l4[:, :, 0, :], l4[:, :, 1, :], ALU.mult))
            RED(asm[:, 0:2], rope1[:, 0:128].rearrange("p (n c) -> p n c", n=2), AX.X, ALU.add).then_inc(lam_sum, 1)
            dve.wait_ge(lam_exp, 1)
            link(TTo(asm[:, 4:5], asm[:, 3:4], asm[:, 2:3], ALU.subtract))
            link(TS(asm[:, 4:5], asm[:, 4:5], -lambda_init, None, ALU.add))
            link(TS(subg, subg, 1.0 - lambda_init, None, ALU.mult))
            for tt in range(TT):
                cs = con[:, C_ROPE + 128 * tt:C_ROPE + 128 * tt + 64]
                sn = con[:, C_ROPE + 128 * tt + 64:C_ROPE + 128 * tt + 128]
                for c in range(4):
                    dve.wait_ge(qkv_done, 6 * tt + c + 1)
                    if 4 * tt + c:
                        dve.wait_ge(qkv_kept, 4 * tt + c)
                    if tt:
                        dve.wait_ge(qk_turned, c + 1)
                    src = ps[:, c, :].rearrange("p (h n) -> p h n", h=8)
                    ra, rc = (v.rearrange("p (h n) -> p h n", h=8) for v in (rope1, rope2))
                    TTo(ra, src, spread(cs, 1, 8), ALU.mult).then_inc(dstep, 1)
                    TTo(rc[:, :, 0:32], src[:, :, 32:64], spread(sn[:, 0:32], 1, 8), ALU.mult).then_inc(dstep, 1)
                    count[0] += 2
                    link(TTo(rc[:, :, 32:64], src[:, :, 0:32], spread(sn[:, 32:64], 1, 8), ALU.mult))
                    TTo(nat[:, 512 * c:512 * c + 512], rope1, rope2, ALU.add).then_inc(qkv_kept, 1)

            def peak(i):
                keys = P * (i // H + 1)
                b = 2 * (i % 2)
                dve.wait_ge(scores_done, i + 1)
                link(dve.memset(ps[0:CHUNK, b:b + 2, keys - CHUNK:keys], NO))
                if i >= 2:
                    dve.wait_ge(exp_ready, 2 * i - 2)
                link(RED(asm[:, 6:8], ps[:, b:b + 2, 0:keys], AX.X, ALU.max))
                TS(asm[:, 8 + b:10 + b], asm[:, 6:8], -(DH ** -0.5), None, ALU.mult).then_inc(peak_ready, 1)

            peak(0)
            for i in range(2 * H):
                if i + 1 < 2 * H:
                    peak(i + 1)
                keys = P * (i // H + 1)
                d = 2 * (i % 2)
                dve.wait_ge(exp_ready, 2 * i + 2)
                if i >= 1:
                    dve.wait_ge(att_ready, i)
                link(dve.reciprocal(asm[:, 48:50], asm[:, 12 + d:14 + d]))
                link(TTo(asm[:, 50:51], asm[:, 49:50], asm[:, 4:5], ALU.mult))
                if i >= 1:
                    dve.wait_ge(att_turned, i)
                link(TS(at[:, 0:keys], Pb[:, i % 2, 1, 0:keys], asm[:, 50:51], None, ALU.mult))
                STT(at[:, 0:keys], Pb[:, i % 2, 0, 0:keys], asm[:, 48:49], at[:, 0:keys], ALU.mult, ALU.add).then_inc(att_ready, 1)
            for b in range(2):
                dve.wait_ge(osq, 2 * b + 2)
                hv = osb[:, b, :].rearrange("p (h e) -> p h e", h=H)
                sqv = xr[:, b, :, :]
                link(TTo(sqv, hv, hv, ALU.mult))
                link(RED(asm[:, 16 + 8 * b:24 + 8 * b], sqv, AX.X, ALU.add))
                TS(asm[:, 16 + 8 * b:24 + 8 * b], asm[:, 16 + 8 * b:24 + 8 * b], 1.0 / P, EPS, ALU.mult, ALU.add).then_inc(ovar, 1)
            for b in range(2):
                hv = osb[:, b, :].rearrange("p (h e) -> p h e", h=H)
                dve.wait_ge(oroot, b + 1)
                link(dve.reciprocal(asm[:, 32 + 8 * b:40 + 8 * b], asm[:, 32 + 8 * b:40 + 8 * b]))
                link(TTo(hv, hv, spread(asm[:, 32 + 8 * b:40 + 8 * b], 2, P), ALU.mult))
                TTo(hv, hv, spread(subg, 1, H), ALU.mult).then_inc(o_ready, 1)
            for n in range(4):
                b, c = n // 2, n % 2
                dve.wait_ge(wo_done, n + 1)
                TTo(x[:, b, 512 * c:512 * c + 512], x[:, b, 512 * c:512 * c + 512], ps[:, n, :], ALU.add).then_inc(mixed, 1)
            norm(3)
            moe(1)
            norm(4)

        @block.tensor
        def _(pe):
            mm = pe.matmul

            def turn(i):
                pe.wait_ge(normed, 2 * i + 2)
                for k in range(KD):
                    for tt in range(TT):
                        ins = pe.transpose(ps[:, k // 2, 256 * (k % 2) + P * tt:256 * (k % 2) + P * tt + P], xr[:, tt, k, :], ident)
                ins.then_inc(hT_psum, 1)

            for first in (gathered, sw_turned):
                pe.sem_inc(first, 1)
            pe.wait_ge(s_con, 16)
            pe.wait_ge(lam_ready, 1)
            for n, v in enumerate((1, 2, 3, 4, 5)):
                pe.transpose(ps[:, 6, 32 * n:32 * n + 32], lam2[:, v, :], ident[0:32, 0:32]).then_inc(lam_psum, 1)
            turn(0)
            pe.wait_ge(s_bc, 64)
            idg = ident.rearrange("p (r g h) -> p r g h", g=2, h=16)
            for i in range(2):
                for c in range(KD):
                    for g in range(2):
                        ins = mm(ps[64 * g:64 * g + 64, 4 + i, 64 * c:64 * c + 64], Cn[:, i, c, :], idg[:, :, g, :],
                                 start=True, stop=True)
            ins.then_inc(c_psum, 1)
            pe.wait_ge(hT_ready, 4)
            for c in range(KD):
                if c % 4 == 0:
                    pe.wait_ge(landed[c // 4], 32)
                for k in range(KD):
                    ins = mm(ps[:, c // 2, 256 * (c % 2):256 * (c % 2) + 256], win[c // 4][:, k, P * (c % 4):P * (c % 4) + P],
                             hT[:, k, :], start=(k == 0), stop=(k == KD - 1))
                ins.then_inc(u_done, 1)
            pe.wait_ge(u_done, 8)
            for u in range(2):
                pe.sem_inc(used[u], 1)
            zeros = con[:, C_ZERO:C_ZERO + 96]
            for o in range(PAIRS // OCT):
                pe.wait_ge(w1_ready, o + 1)
                if o == 0:
                    pe.wait_ge(u4_act, 8)
                    pe.wait_ge(u4_dve, 8)
                    pe.wait_ge(c_ready, 2)
                else:
                    pe.wait_ge(w1T_ready, 4 * o)
                for i in range(2):
                    for r in range(OCT):
                        ins = pe.transpose(ps[:, 2 * i + r // 4, P * (r % 4):P * (r % 4) + P],
                                           W1[:, i, r, :, :].rearrange("p j c -> p (j c)"), ident)
                ins.then_inc(w1_turned, 1)
                pe.wait_ge(w2_ready, o + 1)
                for r in range(OCT):
                    if r % 4 == 0 and o >= 1:
                        pe.wait_ge(f_ready, OCT * o)
                    R = OCT * o + r
                    fb = ps[:, 6 + r // 4, P * (r % 4):P * (r % 4) + P]
                    for j in range(SB):
                        q = slice(32 * j, 32 * j + 32)
                        if j < 3:
                            mm(fb[q, 0:32 * (3 - j)], W1[:, 0, r, 0, :], zeros[:, 0:32 * (3 - j)], start=True, stop=True)
                        for i in range(2):
                            ins = mm(fb[q, 32 * (3 - j):32 * (4 - j)], W1[:, i, r, 0, :], Cb[:, i, R, :],
                                     start=(i == 0), stop=(i == 1))
                        if j:
                            for i in range(2):
                                ins = mm(fb[q, 32 * (4 - j):P], W1[:, i, r, 0, :], W2[:, i, R, 0:32 * j],
                                         start=(i == 0), stop=(i == 1))
                    if r % 4 == 3:
                        ins.then_inc(f_done, 1)
                pe.wait_ge(w1T_ready, 4 * o + 4)
                for r in range(OCT):
                    if r % 4 == 0 and o >= 1:
                        pe.wait_ge(v_ready, 4 * o)
                    for i in range(2):
                        ins = mm(ps[:, 4 + r // 4, P * (r % 4) + 64 * i:P * (r % 4) + 64 * i + 64], W1T[:, i, r, :],
                                 U4[:, OCT * o + r, :], start=True, stop=True)
                    if r % 4 == 3:
                        ins.then_inc(v_done, 1)
            pe.wait_ge(f_ready, PAIRS)
            pe.wait_ge(state, M + 1)
            for r in range(PAIRS):
                dst = ps[:, r // 8, 64 * (r % 8):64 * (r % 8) + 64]
                mm(dst, Fw[:, r, :], U4[:, r, :], start=True, stop=False)
                for i in range(2):
                    ins = mm(dst, W2[:, i, r, :], X[:, 0:M, i, r], start=False, stop=(i == 1))
                ins.then_inc(y_done, 1)
            pe.wait_ge(g_ready, 16)
            for n in range(4):
                tt, c = n // 2, n % 2
                if n >= 2:
                    pe.wait_ge(mixed, n - 1)
                for half in range(2):
                    u = 2 + 2 * half + c
                    pe.wait_ge(landed[u], 32)
                    for k in range(KD):
                        ins = mm(ps[:, 2 * (n % 2) + half, :], gT[:, k, tt * P:(tt + 1) * P], win[u][:, k, :],
                                 start=(k == 0), stop=(k == KD - 1))
                    if n >= 2:
                        if half == 0:
                            ins.then_inc(used[u], 1)
                ins.then_inc(glu_done, 1)
                if n == 3:
                    pe.wait_ge(glu_done, 4)
                    for u in (4, 5):
                        pe.sem_inc(used[u], 1)

            def moe(l):
                pe.wait_ge(hT_ready, 8 * (l + 1))
                pe.wait_ge(s_router, 128)
                for tt in range(TT):
                    for k in range(KD):
                        ins = mm(ps[:, 4, 36 * tt:36 * tt + 36], hT[:, k, tt * P:(tt + 1) * P], wr[:, l, k, :],
                                 start=(k == 0), stop=(k == KD - 1))
                ins.then_inc(logits_done, 1)
                pe.wait_ge(mask_ready, l + 1)
                mm(ps[:, 5, 0:32], before, msk[:, 0, :], start=True, stop=True)
                mm(ps[:, 5, 32:64], before, msk[:, 1, :], start=True, stop=False)
                mm(ps[:, 5, 32:64], ones, msk[:, 0, :], start=False, stop=True)
                mm(ps[:, 5, 64:96], ones, msk[:, 0, :], start=True, stop=False)
                mm(ps[:, 5, 64:96], ones, msk[:, 1, :], start=False, stop=True).then_inc(pos_done, 1)
                pe.wait_ge(cum_ready, l + 1)
                with pe.Fori(0, NQ) as q:
                    n0, passes = passes_of(pe, l, q)
                    rounds = (q + (qround(l, 0) + 1)) * 32
                    with pe.Fori(0, passes) as p:
                        n = n0 + p
                        pe.wait_ge(sel_ready, 2 * n + 2)
                        pe.wait_ge(hidT_ready, n + 1)
                        for tt in range(TT):
                            ins = pe.transpose(ps[:, 3, P * tt:P * tt + P], scw[:, tt, :], ident)
                        ins.then_inc(sw_turned, 1)
                        pe.wait_ge(x_added, 2 * n + 1)
                        for k in range(KD):
                            for tt in range(TT):
                                ins = mm(ps[:, k // 4, P * (k % 4):P * (k % 4) + P], xr[:, tt, k, :], sel[:, tt, :],
                                         start=(tt == 0), stop=(tt == TT - 1))
                        ins.then_inc(gathered, 1)
                        pe.wait_ge(xg_ready, 2 * n + 2)
                        for k in range(KD):
                            if k % 2 == 0:
                                pe.wait_ge(landed[k // 2], rounds)
                            for e in range(QE):
                                s = slice(32 * e, 32 * e + 32)
                                ins = mm(ps[s, 2, :], xg[:, k, s], gu[k // 2][:, e, :, k % 2, :],
                                         start=(k == 0), stop=(k == KD - 1))
                            if k % 2 == 1 and k < KD - 1:
                                ins.then_inc(used[k // 2], 1)
                        ins.then_inc(gu_done, 1)
                        pe.wait_ge(hid_ready, n + 1)
                        pe.wait_ge(gu_done, n + 1)
                        pe.wait_ge(sw_ready, n + 1)
                        pe.transpose(ps[:, 3, 256:384], hid[:, 0:P], ident).then_inc(used[3], 1)
                        pe.transpose(ps[:, 3, 384:512], hid[:, P:2 * P], ident).then_inc(hid_turned, 1)
                        pe.wait_ge(hidT_ready, n + 2)
                        pe.wait_ge(y_ready, 2 * n + 1)
                        for k in range(2):
                            pe.wait_ge(landed[4 + k], rounds)
                            for half in range(2):
                                for e in range(QE):
                                    s = slice(32 * e, 32 * e + 32)
                                    ins = mm(ps[s, 4 + half, :], hidT[:, P * k + 32 * e:P * k + 32 * e + 32],
                                             dn[k][:, e, 512 * half:512 * half + 512], start=(k == 0), stop=(k == 1))
                            if k == 0:
                                ins.then_inc(used[4], 1)
                        ins.then_inc(down_done, 1)
                        pe.wait_ge(y_ready, 2 * n + 3)
                        for tt in range(TT):
                            for half in range(2):
                                ins = mm(ps[:, (6 if tt else 0) + half, :], swT[:, P * tt:P * tt + P],
                                         yy[:, 512 * half:512 * half + 512], start=True, stop=True)
                                if tt == 0 and half == 0:
                                    ins.then_inc(used[5], 1)
                            ins.then_inc(scattered, 1)

            turn(1)
            moe(0)
            turn(2)
            pe.wait_ge(hT_ready, 12)
            for tt in range(TT):
                for c in range(6):
                    pe.wait_ge(landed[c], 32 * (NQ + 2))
                    if tt:
                        if c < 4:
                            pe.wait_ge(qkv_kept, c + 1)
                        else:
                            pe.wait_ge(v_kept, c - 3)
                    for k in range(KD):
                        ins = mm(ps[:, c, :], hT[:, k, tt * P:(tt + 1) * P], win[c][:, k, :], start=(k == 0), stop=(k == KD - 1))
                    ins.then_inc(qkv_done, 1)
                for c in range(4):
                    pe.wait_ge(qkv_kept, 4 * tt + c + 1)
                    if 4 * tt + c >= 2:
                        pe.wait_ge(qkT_ready, 4 * tt + c - 1)
                    for h in range(4):
                        ins = pe.transpose(ps[:, 6 + c % 2, P * h:P * h + P], nat[:, 512 * c + P * h:512 * c + P * h + P], ident)
                    ins.then_inc(qk_turned, 1)
            pe.wait_ge(qkv_done, 12)
            for u in range(UNITS):
                pe.sem_inc(used[u], 1)

            def scores(i):
                b, h = i // H, i % H
                keys = P * (b + 1)
                if i == 0:
                    pe.wait_ge(qkT_ready, 8)
                    pe.wait_ge(v_kept, 4)
                if i >= 2:
                    pe.wait_ge(exp_ready, 2 * i - 2)
                for j in range(2):
                    s = slice(64 * j, 64 * j + 64)
                    ins = mm(ps[:, 2 * (i % 2) + j, 0:keys], qk[s, h, b * P:(b + 1) * P], qk[s, 8 + h, 0:keys], start=True, stop=True)
                ins.then_inc(scores_done, 1)

            scores(0)
            for i in range(2 * H):
                b, h = i // H, i % H
                if i + 1 < 2 * H:
                    scores(i + 1)
                pe.wait_ge(att_ready, i + 1)
                if i >= 1:
                    pe.wait_ge(attT_ready, i)
                for k in range(b + 1):
                    ins = pe.transpose(ps[:, 4, P * k:P * k + P], at[:, P * k:P * k + P], ident)
                ins.then_inc(att_turned, 1)
                pe.wait_ge(attT_ready, i + 1)
                if i == H:
                    pe.wait_ge(osq, 2)
                for k in range(b + 1):
                    ins = mm(ps[:, 6 + h // 4, P * (h % 4):P * (h % 4) + P], atT[:, P * k:P * k + P], vv[:, k, P * h:P * h + P],
                             start=(k == 0), stop=(k == b))
                ins.then_inc(av_done, 1)
            for b in range(2):
                pe.wait_ge(o_ready, b + 1)
                if b:
                    pe.wait_ge(oT_ready, 2)
                for h in range(H):
                    ins = pe.transpose(ps[:, 4 + h // 4, P * (h % 4):P * (h % 4) + P], osb[:, b, P * h:P * h + P], ident)
                ins.then_inc(o_turned, 1)
            pe.wait_ge(s_wo, 16)
            for n in range(4):
                b, c = n // 2, n % 2
                pe.wait_ge(oT_ready, 2 * b + 2)
                for k in range(KD):
                    ins = mm(ps[:, n, :], oT[:, k, b * P:(b + 1) * P], wo[:, k, 512 * c:512 * c + 512], start=(k == 0), stop=(k == KD - 1))
                ins.then_inc(wo_done, 1)
            turn(3)
            moe(1)


_INS = ['x', 'norm_mix_g', 'norm_ffn_g', 'final_norm_g', 'ssm_w_in', 'ssm_lam_re', 'ssm_lam_im', 'ssm_log_dt',
        'ssm_b_re', 'ssm_b_im', 'ssm_c_re', 'ssm_c_im', 'ssm_d', 'ssm_w_glu', 'attn_w_qkv', 'attn_lambda_q1',
        'attn_lambda_k1', 'attn_lambda_q2', 'attn_lambda_k2', 'attn_subln_g', 'attn_w_o', 'moe_w_router_group',
        'moe_b_router_group', 'moe_w_router_expert', 'moe_b_router_expert', 'moe_w_gate', 'moe_w_up', 'moe_w_down']


def kernel(**inputs):
    import concourse.bacc as bacc
    from concourse.bass_utils import run_bass_kernel_spmd as run

    nc = bacc.Bacc("TRN2", target_bir_lowering=False, num_devices=1)
    arrays = {"in_con": constants()}
    for name in _INS:
        arrays["in_" + name] = np.ascontiguousarray(inputs[name])
    aps = {n[3:]: nc.dram_tensor(n, v.shape, mybir.dt.from_np(v.dtype), kind="ExternalInput").ap() for n, v in arrays.items()}
    out = nc.dram_tensor("out", (1, T, D), F32, kind="ExternalOutput").ap()
    build(nc, aps, out)
    return run(nc, [arrays], core_ids=[0]).results[0]["out"]
```

```python
import math
from contextlib import ExitStack

import numpy as np
import concourse.bass as bass
from concourse import mybir

F32 = mybir.dt.float32
I32 = mybir.dt.int32
BF16 = mybir.dt.bfloat16
ALU = mybir.AluOpType
ACT = mybir.ActivationFunctionType
AX = mybir.AxisListType

P = 128
D = 1024
T = 256
TT = T // P
KD = D // P
EPS = 1e-6
SB = 4
M = T // SB
PAIRS = 32
PC = 32
OCT = 8
H = 8
DH = 64
CHUNK = 64
NG, NE, FE = 4, 8, 256
E = NG * NE
QE = 4
NQ = E // QE
SLOTS = 32
MAXPASS = T // SLOTS
UNIT = 4096
UNITS = 6
NO = -1.0e30

C_ID = 0
C_BEFORE = C_ID + P
C_ONES = C_BEFORE + P
C_SLOT = C_ONES + P
C_SKIP = C_SLOT + T + SLOTS
C_ROPE = C_SKIP + PC
C_STEP = C_ROPE + TT * 4 * 32
C_UPTO = C_STEP + NQ * 7
C_TURN = C_UPTO + 9 * 8
C_N = C_TURN + 1


def constants():
    c = np.zeros((P, C_N), np.float32)
    i = np.arange(P)
    c[:, C_ID:C_ID + P] = np.eye(P)
    c[:, C_BEFORE:C_BEFORE + P] = i[:, None] < i[None, :]
    c[:, C_ONES:C_ONES + P] = 1.0
    c[:, C_SLOT:C_SKIP] = np.arange(1, T + SLOTS + 1)
    c[:, C_SKIP:C_SKIP + PC] = i[:, None] % PC == np.arange(PC)[None, :]
    inv = np.float32(10000.0) ** (-np.arange(0, DH, 2, dtype=np.float32) / np.float32(DH))
    ang = np.arange(T, dtype=np.float32)[:, None] * inv[None, :]
    cos, sin = np.cos(ang).astype(np.float32), np.sin(ang).astype(np.float32)
    rope = np.concatenate([cos, cos, -sin, sin], axis=1).reshape(TT, P, 128)
    for tt in range(TT):
        c[:, C_ROPE + 128 * tt:C_ROPE + 128 * (tt + 1)] = rope[tt]
    c[:, C_STEP:C_STEP + NQ * 7] = np.tile(SLOTS * np.arange(1, 8), NQ)
    c[:, C_UPTO:C_UPTO + 72] = (np.arange(8)[None, :] < np.arange(9)[:, None]).reshape(-1)
    c[:, C_TURN] = math.pi / 2
    return c


def spread(ap, axis, n):
    a = ap.unsqueeze(axis)
    shape = list(a.shape)
    shape[axis] = n
    return a.to_broadcast(shape)


def build(nc, a, out):
    with ExitStack() as ctx:
        ctx.enter_context(nc.allow_non_contiguous_dma(reason="short runs of the small parameters"))

        def sb(name, shape, dt=F32):
            return ctx.enter_context(nc.sbuf_tensor(name, shape, dt))

        def sem(name):
            return ctx.enter_context(nc.semaphore(name))

        ring = sb("ring", [P, UNITS, UNIT])
        x = sb("x", [P, TT, D])
        xr = sb("xr", [P, TT, KD, P])
        hT = sb("hT", [P, KD, T])
        gains = sb("gains", [P, 2, D])
        con = sb("con", [P, C_N])
        wr = sb("wr", [P, 2, KD, NG + E])
        rb = sb("rb", [P, 2, NG + E])
        small = sb("small", [P, 64])
        cum = [sb(f"cum{l}", [P, 17], I32) for l in range(2)]
        work = sb("work", [P, 18560])
        ps = ctx.enter_context(nc.psum_tensor("ps", [P, 8, 512], F32))

        ident = con[:, C_ID:C_ID + P]
        before = con[:, C_BEFORE:C_BEFORE + P]
        ones = con[:, C_ONES:C_ONES + P]

        def part(off, n):
            return work[:, off:off + n]

        Fw = part(0, 4096).rearrange("p (r c) -> p r c", r=PAIRS)
        W2 = part(4096, 8192).rearrange("p (i r c) -> p i r c", i=2, r=PAIRS)
        X = part(12288, (M + 1) * 64).rearrange("p (m i r) -> p m i r", i=2, r=PAIRS)
        o = 12288 + (M + 1) * 64
        Pw = part(o, 3 * 5 * PAIRS).rearrange("p (i j r) -> p i j r", i=3, j=5)
        o += 480
        LB = part(o, 64).rearrange("p (i r) -> p i r", i=2)
        o += 64
        LA = part(o, 64).rearrange("p (i r) -> p i r", i=2)
        o += 64
        sc2 = part(o, 64).rearrange("p (i r) -> p i r", i=2)
        o += 64
        dcol = part(o, 8)
        o += 8
        skip = part(o, 256).rearrange("p (q c) -> p q c", q=KD)
        o += 256
        step = part(o, 256).rearrange("p (n i r) -> p n i r", n=4, i=2)
        o += 256
        drep = part(o, 128)
        o += 128
        assert o <= 18560
        U4 = hT[:].rearrange("p k t -> p (k t)").rearrange("p (r m) -> p r m", r=PAIRS)
        gT = xr[:].rearrange("p a k q -> p (a k q)").rearrange("p (c t) -> p c t", c=KD)
        pre = ring[:, 3:6, :].rearrange("p u n -> p (u n)")
        W1 = pre[:, 0:2048].rearrange("p (i r j c) -> p i r j c", i=2, r=OCT, j=SB)
        W1T = pre[:, 2048:4096].rearrange("p (i r c) -> p i r c", i=2, r=OCT)
        Bn = pre[:, 4096:5120].rearrange("p (i r c) -> p i r c", i=2, r=PAIRS)
        Bb = pre[:, 5120:6144].rearrange("p (i r c) -> p i r c", i=2, r=PAIRS)
        Cn = pre[:, 6144:7168].rearrange("p (i c s) -> p i c s", i=2, c=KD)
        Cc = pre[:, 7168:8192].rearrange("p (i r c) -> p i r c", i=2, r=PAIRS)
        Cb = pre[:, 8192:10240].rearrange("p (i r c) -> p i r c", i=2, r=PAIRS)
        t1 = pre[:, 10240:10752]
        t2 = pre[:, 10752:11264]
        lam = pre[0:32, 11264:12288].rearrange("p (n c) -> p n c", c=P)
        lam2 = work[0:32, 12352:13376].rearrange("p (n c) -> p n c", c=P)
        t3 = xr[:, 0, 0:4, :].rearrange("p k q -> p (k q)")
        t4 = xr[:, 0, 4:8, :].rearrange("p k q -> p (k q)")
        sig = part(12288, 1024).rearrange("p (n c) -> p n c", n=2)
        o = 0
        xg = part(o, 1024).rearrange("p (k s) -> p k s", k=KD)
        o += 1024
        sel = part(o, 128).bitcast(BF16).rearrange("p (a s) -> p a s", a=TT)
        o += 128
        scw = part(o, 256).rearrange("p (a s) -> p a s", a=TT)
        o += 256
        sil = part(o, 256)
        o += 256
        hid = part(o, 256)
        o += 256
        hidT = part(o, 256)
        o += 256
        swT = part(o, 256)
        o += 256
        kept = part(o, (MAXPASS + 1) * 512).rearrange("p (n c) -> p n c", n=MAXPASS + 1)
        o += (MAXPASS + 1) * 512
        lgT = sil
        lowest = part(o, 1024)
        o += 1024
        parts = [v.bitcast(BF16).rearrange("p (a k q) -> p a k q", a=TT, k=KD)
                 for v in (hT[:, 0:4, :].rearrange("p k t -> p (k t)"), hT[:, 4:8, :].rearrange("p k t -> p (k t)"), lowest)]
        yy = part(o, 1024)
        o += 1024
        lg = part(o, 72).rearrange("p (a n) -> p a n", a=TT)
        o += 72
        slot1 = part(o, 72).rearrange("p (a e) -> p a e", a=TT)
        o += 72
        comb = part(o, 72).rearrange("p (a e) -> p a e", a=TT)
        o += 72
        msk = part(o, 64).rearrange("p (a e) -> p a e", a=TT)
        o += 64
        rt = part(o, 512)
        o += 512
        assert o <= 10208
        wo = part(10208, 8192).rearrange("p (k n) -> p k n", k=KD)
        qk = part(0, 4096).rearrange("p (h t) -> p h t", h=16)
        vv = part(4096, 2048).rearrange("p (a n) -> p a n", a=TT)
        nat = part(6144, 1024).rearrange("p (b n) -> p b n", b=2)
        osb = [part(7168, 1024), part(6144, 1024)]
        oT = part(0, 2048).rearrange("p (k t) -> p k t", k=KD)
        rope1 = part(8192, 512)
        rope2 = part(8704, 512)
        osq2 = part(8192, 1024)
        at = part(9216, 512)
        pv_rest = part(9728, 480)
        lam4 = pv_rest[:, 0:256].rearrange("p (n c) -> p n c", n=4)
        soft_row = pv_rest[:, 0:128].rearrange("p (b n) -> p b n", b=2)
        subg = pv_rest[:, 256:384]
        asm = pv_rest[:, 384:480]
        Pb = xr[:].rearrange("p a k q -> p a (k q)").rearrange("p b (i n) -> p b i n", i=2)
        atT = gains[:, 0, :].rearrange("p (b n) -> p b n", b=2)
        groups = [(0, 0, 4, 4, 6, 7, 0), (0, 4, 4, 4, 6, 7, 0),
                  (1, 0, 2, 0, 4, 6, 0), (1, 2, 2, 2, 4, 6, 256), (1, 4, 2, 0, 4, 7, 0), (1, 6, 2, 2, 4, 7, 256)]
        exps = [8, 16, 20, 24, 28, 32]

        s_con, s_x, s_lam, s_bc, s_router, s_gain0, s_gain, s_att, s_wo = (
            sem(n) for n in ("con_in", "x_in", "lam_in", "bc_in", "router_in", "gain0_in", "gain_in", "att_in", "wo_in"))
        landed = [sem(f"landed{u}") for u in range(UNITS)]
        used = [sem(f"used{u}") for u in range(UNITS)]
        out_done = sem("out_done")
        dstep, pstep = sem("dve_steps"), sem("pool_steps")
        squares, var_ready, root_ready, normed = (sem(n) for n in ("squares", "var_ready", "root_ready", "normed"))
        hT_psum, hT_ready = sem("hT_psum"), sem("hT_ready")
        mixed = sem("mixed")
        dt_ready, er_ready, arg_ready, sin_ready = (sem(n) for n in ("dt_ready", "er_ready", "arg_ready", "sin_ready"))
        lam_ready, lam_psum, c_psum, c_ready = (sem(n) for n in ("lam_ready", "lam_psum", "c_psum", "c_ready"))
        cleared = sem("cleared")
        u_done, u4_act, u4_dve = sem("u_done"), sem("u4_act"), sem("u4_dve")
        w1_ready, w2_ready, w1_turned, w1T_ready = (sem(n) for n in ("w1_ready", "w2_ready", "w1_turned", "w1T_ready"))
        part_ready, rest_ready = sem("part_ready"), sem("rest_ready")
        k_done, k_ready, f_ready, v_done, v_ready = (sem(n) for n in ("k_done", "k_ready", "f_ready", "v_done", "v_ready"))
        bbar_ready, pow_ready, w1_first = sem("bbar_ready"), sem("pow_ready"), sem("w1_first")
        drep_ready, prod_a, prod_b, summed, state = (sem(n) for n in ("drep_ready", "prod_a", "prod_b", "summed", "state"))
        y_done, g_ready = sem("y_done"), sem("g_ready")
        glu_done, sig_ready, glu_prod = sem("glu_done"), sem("sig_ready"), sem("glu_prod")
        logits_turned, logits_kept = sem("logits_turned"), sem("logits_kept")
        logits_done, gate_sub, gate_exp, mask_ready, pos_done, cum_ready = (
            sem(n) for n in ("logits_done", "gate_sub", "gate_exp", "mask_ready", "pos_done", "cum_ready"))
        sel_built, sel_ready, sw_turned, sw_ready, gathered, xg_ready = (
            sem(n) for n in ("sel_built", "sel_ready", "sw_turned", "sw_ready", "gathered", "xg_ready"))
        hidT_kept, down_ready, back_ready = sem("hidT_kept"), sem("down_ready"), sem("back_ready")
        gu_done, sil_ready, hid_ready, hid_turned, down_done, y_ready, scattered, x_added = (
            sem(n) for n in ("gu_done", "sil_ready", "hid_ready", "hid_turned", "down_done",
                             "y_ready", "scattered", "x_added"))
        qkv_done, qkv_kept, v_kept, qk_turned, qkT_ready = (
            sem(n) for n in ("qkv_done", "qkv_kept", "v_kept", "qk_turned", "qkT_ready"))
        lam_sum, lam_exp = sem("lam_sum"), sem("lam_exp")
        scores_done, peak_ready, exp_ready, att_ready, att_turned, attT_ready, av_done = (
            sem(n) for n in ("scores_done", "peak_ready", "exp_ready", "att_ready", "att_turned", "attT_ready", "av_done"))
        osq, ovar, oroot, o_ready, o_turned, oT_ready, wo_done = (
            sem(n) for n in ("osq", "ovar", "oroot", "o_ready", "o_turned", "oT_ready", "wo_done"))
        final_ready = sem("final_ready")

        win = [ring[:, u, :].rearrange("p (k n) -> p k n", k=KD) for u in range(UNITS)]
        gu = [ring[:, u, :].rearrange("p (e g k f) -> p e g k f", e=QE, g=2, k=2) for u in range(4)]
        dn = [ring[:, 4 + u, :].rearrange("p (e n) -> p e n", e=QE) for u in range(2)]

        def qround(l, q):
            return l * (NQ + 1) + 1 + q

        MOST = 2 * MAXPASS * NQ

        def passes_of(eng, l, q):
            return (eng.value_load(cum[l][0:1, bass.ds(q + NQ, 1)], min_val=0, max_val=MOST),
                    eng.value_load(cum[l][0:1, bass.ds(q, 1)], min_val=1, max_val=MAXPASS))

        def passes_through(eng, l):
            return eng.value_load(cum[l][0:1, 2 * NQ:2 * NQ + 1], min_val=0, max_val=MOST)

        def stack(copy, n):
            quad, j = n // 4, n % 4
            ups = ps[:, 0:4, :].rearrange("p b n -> p (b n)").rearrange("p (c m s) -> p c m s", c=KD, s=SB)
            dst = U4[32 * j:32 * j + 32, :, :].rearrange("p (c a) m -> p c a m", a=4)[:, :, quad, :]
            return copy(dst, ups[32 * quad:32 * quad + 32, :, :, SB - 1 - j])

        block = ctx.enter_context(nc.Block())

        @block.sync
        def _(sp):
            sp.dma_start(con[:], a["con"]).then_inc(s_con, 16)
            sp.dma_start(x[:], a["x"].rearrange("b (a p) d -> p (b a) d", p=P)).then_inc(s_x, 16)

            def columns(u, w, c0, kp):
                src = w.rearrange("(p k) n -> p k n" if kp else "(k p) n -> p k n", k=KD)
                for half in range(2):
                    sp.dma_start(win[u][:, 4 * half:4 * half + 4, :],
                                 src[:, 4 * half:4 * half + 4, c0:c0 + 512]).then_inc(landed[u], 16)

            sp.dma_start(gains[:, 0, :], a["norm_mix_g"][0].partition_broadcast(P)).then_inc(s_gain0, 16)
            for u in range(2):
                columns(u, a["ssm_w_in"][0], 512 * u, True)
            columns(2, a["ssm_w_glu"][0], 0, False)
            sp.wait_ge(v_done, 8)
            sp.wait_ge(w1T_ready, 16)
            sp.wait_ge(k_done, 4)
            for u in range(3, 6):
                columns(u, a["ssm_w_glu"][0], 512 * (u - 2), False)

            def quartet(l, q):
                def experts(name):
                    w = a[name][l].rearrange("g e r c -> (g e) (r c)")
                    return w[bass.ds(q * QE, QE), :]

                base = l + 1 + before_q
                for u in range(4):
                    sp.wait_ge(used[u], base)
                    for g, name in enumerate(("moe_w_gate", "moe_w_up")):
                        src = experts(name).rearrange("e (p n) -> p e n", p=P)[:, :, 512 * u:512 * u + 512]
                        sp.dma_start(gu[u][:, :, g, :, :].rearrange("p e k f -> p e (k f)"), src).then_inc(landed[u], 16)
                for u in range(2):
                    sp.wait_ge(used[4 + u], base)
                    src = experts("moe_w_down").rearrange("e (k p n) -> p k e n", k=2, p=P)
                    for half in range(2):
                        sp.dma_start(dn[u][:, 2 * half:2 * half + 2, :],
                                     src[:, u, 2 * half:2 * half + 2, :]).then_inc(landed[4 + u], 16)

            for l in range(2):
                before_q = 0 if l == 0 else total
                quartet(l, 0)
                if l == 0:
                    sp.wait_ge(g_ready, 64)
                    sp.wait_ge(mixed, 4)
                    sp.dma_start(wo, a["attn_w_o"][0].rearrange("(k p) n -> p k n", p=P)).then_inc(s_wo, 16)
                sp.wait_ge(cum_ready, l + 1)
                with sp.Fori(1, NQ) as q:
                    before_q, _ = passes_of(sp, l, q)
                    quartet(l, q)
                total = passes_through(sp, l)
                if l == 0:
                    for u in range(UNITS):
                        sp.wait_ge(used[u], total + 1)
                        columns(u, a["attn_w_qkv"][0], 512 * u, True)
            for tt in range(TT):
                sp.wait_ge(final_ready, tt + 1)
                sp.dma_start(out[0, tt * P:(tt + 1) * P, :], xr[:, tt, :, :].rearrange("p k q -> p (k q)")).then_inc(out_done, 16)
            sp.wait_ge(out_done, 32)

        @block.gpsimd
        def _(pool):
            def gain(i, src):
                pool.dma_start(gains[:, i % 2, :], src.partition_broadcast(P)).then_inc(s_gain, 16)

            def pool_link(ins, n):
                ins.then_inc(pstep, 1)
                pool.wait_ge(pstep, n)

            pool.memset(part(0, 12288), 0.0).then_inc(cleared, 1)
            pool.memset(X[:, 0, :, :], 0.0).then_inc(cleared, 1)
            pool.memset(pre[:, 8192:10240], 0.0).then_inc(cleared, 1)
            pool.memset(pre[:, 0:2048], 0.0).then_inc(cleared, 1)
            gain(1, a["norm_ffn_g"][0])
            pool.wait_ge(cleared, 4)
            pool.wait_ge(hT_psum, 1)
            pool.wait_ge(pow_ready, 1)
            pool.wait_ge(c_ready, 2)
            v4 = lambda v: v.rearrange("p (r j c) -> p r j c", r=OCT, j=SB)
            n = 0
            for o in range(PAIRS // OCT):
                pr = slice(OCT * o, OCT * o + OCT)
                pw = lambda i: spread(Pw[:, i, 1:5, pr].rearrange("p j r -> p r j"), 3, 16)
                cc = lambda i: spread(Cc[:, i, pr, :], 2, SB)
                for i in range(2):
                    pool.tensor_tensor(v4(t3), pw(0 if i == 0 else 2), cc(0), ALU.mult).then_inc(pstep, 1)
                    pool_link(pool.tensor_tensor(v4(t4), pw(1 if i == 0 else 0), cc(1), ALU.mult), n + 2)
                    for g in range(2):
                        h = slice(64 * g, 64 * g + 64)
                        dst = W2[h, i, pr, :].rearrange("p r (s c) -> p r s c", s=SB)[:, :, :, 16 * g:16 * g + 16]
                        ins = pool.tensor_tensor(dst, v4(t3)[h], v4(t4)[h], ALU.subtract)
                        if g == 0:
                            ins.then_inc(pstep, 1)
                    pool_link(ins, n + 4)
                    n += 4
                pool.sem_inc(w2_ready, 1)
            def split(l):
                for i in range(2):
                    pool.wait_ge(part_ready, 3 * l + i + 1)
                    pool.tensor_tensor(xr[:], xr[:], parts[i], ALU.subtract).then_inc(rest_ready, 1)

            split(0)
            for i, g in ((2, a["norm_mix_g"][1]), (3, a["norm_ffn_g"][1]), (4, a["final_norm_g"])):
                pool.wait_ge(s_gain, 16 * (i - 1))
                pool.wait_ge(normed, 2 * (i - 1))
                if i == 4:
                    pool.wait_ge(mixed, 8)
                gain(i, g)
            split(1)
            pool.wait_ge(s_gain, 64)

        @block.scalar
        def _(act):
            def dma(dst, src, s):
                act.dma_start(dst, src).then_inc(s, 16)

            dma(lam[:, 0, :], a["ssm_lam_re"][0].rearrange("(r g) p -> r (g p)", g=2), s_lam)
            dma(lam[:, 1, :], a["ssm_lam_im"][0].rearrange("(r g) p -> r (g p)", g=2), s_lam)
            dma(small[0:32, 0:2], a["ssm_log_dt"][0].rearrange("(r g) -> r g", g=2), s_lam)
            dma(drep[0:8, :], a["ssm_d"][0].rearrange("(c p) -> c p", p=P), s_lam)
            for i, n in enumerate(("re", "im")):
                dma(Bn[:, i, :, :], a["ssm_b_" + n][0].rearrange("(r g) p h -> (g p) r h", g=2), s_bc)
                dma(Cn[:, i, :, :], a["ssm_c_" + n][0].rearrange("(c g) h p -> (g h) c p", g=8), s_bc)
            for l in range(2):
                dma(wr[:, l, :, 0:NG], a["moe_w_router_group"][l].rearrange("(p k) n -> p k n", k=KD), s_router)
                dma(wr[:, l, :, NG:], a["moe_w_router_expert"][l].rearrange("(p k) g e -> p k (g e)", k=KD), s_router)
                dma(rb[:, l, 0:NG], a["moe_b_router_group"][l].partition_broadcast(P), s_router)
                dma(rb[:, l, NG:], a["moe_b_router_expert"][l].rearrange("g e -> (g e)").partition_broadcast(P), s_router)

            def norm(i):
                for tt in range(TT):
                    act.activation(xr[:, tt, :, :].rearrange("p k q -> p (k q)"), x[:, tt, :], ACT.Square,
                                   accum_out=small[:, 8 + tt:9 + tt]).then_inc(squares, 1)
                act.wait_ge(var_ready, i + 1)
                act.activation(small[:, 12:14], small[:, 10:12], ACT.Sqrt).then_inc(root_ready, 1)
                if i < 4:
                    act.wait_ge(hT_psum, i + 1)
                    for b in range(4):
                        act.copy(hT[:, 2 * b:2 * b + 2, :].rearrange("p k t -> p (k t)"), ps[:, b, :]).then_inc(hT_ready, 1)

            act.wait_ge(s_x, 16)
            norm(0)
            act.wait_ge(s_lam, 64)
            act.activation(small[0:32, 2:4], small[0:32, 0:2], ACT.Exp).then_inc(dt_ready, 1)
            act.wait_ge(er_ready, 1)
            act.activation(lam[:, 4, :], lam[:, 2, :], ACT.Exp).then_inc(sin_ready, 1)
            act.wait_ge(arg_ready, 1)
            act.activation(lam[:, 5, :], lam[:, 5, :], ACT.Sin).then_inc(sin_ready, 1)
            act.activation(lam[:, 6, :], lam[:, 6, :], ACT.Sin).then_inc(sin_ready, 1)
            act.wait_ge(c_psum, 1)
            for i in range(2):
                act.copy(Cc[:, i, :, :].rearrange("p r c -> p (r c)"), ps[:, 4 + i, :]).then_inc(c_ready, 1)

            act.wait_ge(u_done, 8)
            for n in range(8):
                stack(act.copy, n).then_inc(u4_act, 1)
            act.wait_ge(bbar_ready, 1)
            act.wait_ge(cleared, 4)
            for o in range(PAIRS // OCT):
                if o >= 1:
                    act.wait_ge(w1_turned, o)
                    act.wait_ge(k_done, o)
                for i in range(2):
                    for g in range(2):
                        h = slice(64 * g, 64 * g + 64)
                        act.copy(W1[h, i, :, 0, 16 * g:16 * g + 16], Bb[h, i, OCT * o:OCT * o + OCT, :]).then_inc(w1_first, 1)
                act.wait_ge(w1_turned, o + 1)
                if o >= 1:
                    act.wait_ge(v_done, 2 * o)
                for b in range(4):
                    act.copy(W1T[:, b // 2, 4 * (b % 2):4 * (b % 2) + 4, :].rearrange("p r c -> p (r c)"),
                             ps[:, b, :]).then_inc(w1T_ready, 1)
                act.wait_ge(v_done, 2 * o + 2)
                for b in range(2):
                    src = ps[:, 4 + b, :].rearrange("p (r i m) -> p m i r", r=4, i=2)
                    for i in range(2):
                        act.copy(X[:, 1:M + 1, i, OCT * o + 4 * b:OCT * o + 4 * b + 4], src[:, :, i, :]).then_inc(v_ready, 1)
            act.wait_ge(k_ready, 1)
            for j in range(SB):
                for r in range(4):
                    kps = ps[32 * r:32 * r + 32, 6:8, :].rearrange("p b n -> p (b n)").rearrange("p (q n) -> p q n", q=KD)
                    dst = Fw[32 * j:32 * j + 32, :, :].rearrange("p (q a) n -> p q a n", a=4)[:, :, r, 32 * (3 - j):P]
                    act.copy(dst, kps[:, :, 0:32 * (j + 1)]).then_inc(f_ready, 1)
            for b in range(4):
                act.wait_ge(y_done, 8 * b + 8)
                for n in range(16):
                    quad, s = n // 4, n % 4
                    src = ps[32 * s:32 * s + 32, b, :].rearrange("p (c a m) -> p c a m", c=2, a=4)[:, :, quad, :]
                    dst = gT[32 * quad:32 * quad + 32, 2 * b:2 * b + 2, :].rearrange("p c (m s) -> p c m s", s=SB)[:, :, :, s]
                    act.activation(dst, src, ACT.Gelu_apprx_tanh).then_inc(g_ready, 1)
            for n in range(4):
                act.wait_ge(glu_done, n + 1)
                if n >= 1:
                    act.wait_ge(mixed, n)
                act.activation(sig[:, 0, :], ps[:, 5 + 2 * (n % 2), :], ACT.Sigmoid).then_inc(sig_ready, 1)

            def moe(l):
                act.wait_ge(logits_turned, l + 1)
                act.copy(lgT[0:NG + E, :], ps[0:NG + E, 4, 0:T]).then_inc(logits_kept, 1)
                act.copy(parts[0], xr[:]).then_inc(part_ready, 1)
                act.wait_ge(gate_sub, 2 * l + 1)
                act.activation(rt[:, 8:16], rt[:, 8:16], ACT.Exp).then_inc(gate_exp, 1)
                act.wait_ge(gate_sub, 2 * l + 2)
                act.activation(rt[:, 128:144], rt[:, 128:144], ACT.Exp).then_inc(gate_exp, 1)
                for i in range(2):
                    act.wait_ge(rest_ready, 2 * l + i + 1)
                    act.copy(parts[i + 1], xr[:]).then_inc(part_ready, 1)
                act.wait_ge(cum_ready, l + 1)
                with act.Fori(0, NQ) as q:
                    n0, passes = passes_of(act, l, q)
                    with act.Fori(0, passes) as p:
                        n = n0 + p
                        act.wait_ge(sw_turned, n + 1)
                        act.copy(kept[:, bass.ds(p, 1), 256:512].rearrange("p n c -> p (n c)"), ps[:, 3, 0:256]).then_inc(sw_ready, 1)
                        act.wait_ge(gathered, 2 * n + 2)
                        act.copy(xg[:, 4:8, :].rearrange("p k s -> p (k s)"), ps[:, 1, :]).then_inc(xg_ready, 1)
                        act.wait_ge(gu_done, n + 1)
                        act.activation(sil, ps[:, 2, 0:256], ACT.Silu).then_inc(sil_ready, 1)
                    with act.Fori(0, passes) as p:
                        n = n0 + p
                        act.wait_ge(sw_ready, n + 1)
                        act.wait_ge(scattered, 2 * n + 1)
                        act.copy(swT, kept[:, bass.ds(p, 1), 256:512].rearrange("p n c -> p (n c)")).then_inc(back_ready, 1)
                        act.wait_ge(down_done, n + 2)
                        act.copy(yy[:, 0:512], ps[:, 4, :]).then_inc(y_ready, 1)
                total = passes_through(act, l)
                act.wait_ge(x_added, 2 * total + 2)

            act.wait_ge(mixed, 4)
            norm(1)
            moe(0)
            for n, name in enumerate(("q1", "k1", "q2", "k2")):
                dma(lam4[:, n, :], a["attn_lambda_" + name][0].partition_broadcast(P), s_att)
            dma(subg, a["attn_subln_g"][0].partition_broadcast(P), s_att)
            norm(2)
            act.wait_ge(lam_sum, 1)
            act.activation(asm[:, 2:4], asm[:, 0:2], ACT.Exp).then_inc(lam_exp, 1)
            def keep_v(tt):
                for c in range(4, 6):
                    act.wait_ge(qkv_done, 6 * tt + c + 1)
                    act.copy(vv[:, tt, 512 * c - 2048:512 * c - 1536], ps[:, c if tt == 0 else c % 2, :]).then_inc(v_kept, 1)

            def keep_qk(tt, c):
                act.wait_ge(qk_turned, 4 * tt + c + 1)
                act.copy(qk[:, 4 * c:4 * c + 4, tt * P:(tt + 1) * P],
                         ps[:, (6 if tt == 0 else 2) + c % 2, :].rearrange("p (h t) -> p h t", h=4)).then_inc(qkT_ready, 1)

            def soft(g):
                b, _, heads, sbank, _, _, _ = groups[g]
                keys = P * (b + 1)
                row = soft_row[:, g % 2, :]
                act.wait_ge(peak_ready, g + 1)
                if g >= 2:
                    act.wait_ge(att_ready, g - 1)
                for j in range(2):
                    for h in range(heads):
                        n = heads * j + h
                        act.activation(Pb[:, g % 2, j, keys * h:keys * h + keys], ps[:, sbank + j, keys * h:keys * h + keys],
                                       ACT.Exp, bias=row[:, 8 + n:9 + n], scale=DH ** -0.5,
                                       accum_out=row[:, 16 + n:17 + n]).then_inc(exp_ready, 1)

            def keep_att(g):
                act.wait_ge(att_turned, g + 1)
                if g >= 2:
                    act.wait_ge(av_done, g - 1)
                act.copy(atT[:, g % 2, :], ps[:, groups[g][4], :]).then_inc(attT_ready, 1)

            def keep_o(n):
                act.wait_ge(av_done, (1, 2, 4, 6)[n])
                act.copy(osb[n // 2][:, 512 * (n % 2):512 * (n % 2) + 512], ps[:, (7, 7, 6, 7)[n], :]).then_inc(osq, 1)

            def root_o(b):
                act.wait_ge(ovar, b + 1)
                act.activation(asm[:, 32 + 8 * b:40 + 8 * b], asm[:, 16 + 8 * b:24 + 8 * b], ACT.Sqrt).then_inc(oroot, 1)

            def keep_oT(b, c, bank):
                act.wait_ge(o_turned, 2 * b + c + 1)
                act.copy(oT[:, 4 * c:4 * c + 4, b * P:(b + 1) * P],
                         ps[:, bank, :].rearrange("p (h t) -> p h t", h=4)).then_inc(oT_ready, 1)

            for c in range(4):
                keep_qk(0, c)
            keep_v(0)
            soft(0)
            soft(1)
            keep_att(0)
            keep_o(0)
            keep_qk(1, 0)
            keep_att(1)
            keep_o(1)
            for c in range(1, 4):
                keep_qk(1, c)
            root_o(0)
            keep_v(1)
            soft(2)
            soft(3)
            keep_att(2)
            keep_oT(0, 0, 5)
            soft(4)
            keep_att(3)
            keep_oT(0, 1, 5)
            keep_o(2)
            soft(5)
            keep_att(4)
            keep_att(5)
            keep_o(3)
            root_o(1)
            keep_oT(1, 0, 4)
            keep_oT(1, 1, 5)
            act.wait_ge(mixed, 8)
            norm(3)
            moe(1)
            norm(4)

        @block.vector
        def _(dve):
            count = [0]

            def link(ins):
                count[0] += 1
                ins.then_inc(dstep, 1)
                dve.wait_ge(dstep, count[0])

            TTo, TS, STT, RED = dve.tensor_tensor, dve.tensor_scalar, dve.scalar_tensor_tensor, dve.tensor_reduce

            def norm(i):
                dve.wait_ge(squares, 2 * i + 2)
                TS(small[:, 10:12], small[:, 8:10], 1.0 / D, EPS, ALU.mult, ALU.add).then_inc(var_ready, 1)
                dve.wait_ge(root_ready, i + 1)
                link(dve.reciprocal(small[:, 14:16], small[:, 12:14]))
                if i == 0:
                    dve.wait_ge(s_gain0, 16)
                else:
                    dve.wait_ge(s_gain, 16 * i)
                for tt in range(TT):
                    if i < 4:
                        STT(xr[:, tt, :, :], x[:, tt, :].rearrange("p (q k) -> p k q", k=KD), small[:, 14 + tt:15 + tt],
                            gains[:, i % 2, :].rearrange("p (q k) -> p k q", k=KD), ALU.mult, ALU.mult).then_inc(normed, 1)
                    else:
                        STT(xr[:, tt, :, :].rearrange("p k q -> p (k q)"), x[:, tt, :], small[:, 14 + tt:15 + tt],
                            gains[:, i % 2, :], ALU.mult, ALU.mult).then_inc(final_ready, 1)

            for first in (state, x_added, x_added, y_ready, sel_ready, hidT_kept):
                dve.sem_inc(first, 1)
            norm(0)
            L = lambda n: lam[:, n, :]
            V = lambda n: lam2[:, n, :]
            dve.wait_ge(dt_ready, 1)
            dtb = spread(small[0:32, 2:4], 2, 64)
            two = lambda v: v.rearrange("p (g c) -> p g c", g=2)
            TTo(two(L(2)), two(L(0)), dtb, ALU.mult).then_inc(er_ready, 1)
            link(TTo(two(L(3)), two(L(1)), dtb, ALU.mult))
            MAGIC = 1.5 * 2.0 ** 23
            link(TS(V(0), L(3), 1.0 / (2 * math.pi), MAGIC, ALU.mult, ALU.add))
            link(TS(V(0), V(0), -MAGIC, None, ALU.add))
            C1 = 6.28125
            C2 = float(np.float32(np.round((2 * math.pi - C1) * 2.0 ** 22) / 2.0 ** 22))
            C3 = 2 * math.pi - C1 - C2
            link(STT(V(1), V(0), -C1, L(3), ALU.mult, ALU.add))
            link(STT(V(1), V(0), -C2, V(1), ALU.mult, ALU.add))
            link(STT(V(1), V(0), -C3, V(1), ALU.mult, ALU.add))
            PI_IN = 3.1415925
            link(TS(L(6), V(1), PI_IN, -PI_IN, ALU.min, ALU.max))
            link(STT(V(2), L(6), -1.0, L(6), ALU.mult, ALU.max))
            link(TS(L(5), V(2), -1.0, math.pi / 2, ALU.mult, ALU.add))
            dve.sem_inc(arg_ready, 1)
            link(TTo(V(0), L(0), L(0), ALU.mult))
            link(TTo(V(1), L(1), L(1), ALU.mult))
            link(TTo(V(0), V(0), V(1), ALU.add))
            link(dve.reciprocal(V(0), V(0)))
            dve.wait_ge(sin_ready, 3)
            link(TTo(V(1), L(4), L(5), ALU.mult))
            link(TTo(V(2), L(4), L(6), ALU.mult))
            link(TS(V(3), V(1), -1.0, None, ALU.add))
            link(TTo(V(4), V(3), L(0), ALU.mult))
            link(TTo(V(5), V(2), L(1), ALU.mult))
            link(TTo(V(4), V(4), V(5), ALU.add))
            link(TTo(V(5), V(2), L(0), ALU.mult))
            link(TTo(V(6), V(3), L(1), ALU.mult))
            link(TTo(V(5), V(5), V(6), ALU.subtract))
            link(TTo(V(3), V(4), V(0), ALU.mult))
            link(TTo(V(4), V(5), V(0), ALU.mult))
            dve.sem_inc(lam_ready, 1)
            dve.wait_ge(lam_psum, 5)
            TP = ps[:, 6, 0:128].rearrange("p (n r) -> p n r", n=4)
            dve.memset(Pw[:, 0, 0, :], 1.0)
            dve.memset(Pw[:, 1:3, 0, :], 0.0)
            dve.tensor_copy(Pw[:, 0, 1, :], TP[:, 0, :])
            dve.tensor_copy(Pw[:, 1, 1, :], TP[:, 1, :])
            dve.tensor_copy(sc2[:], TP[:, 2:4, :])
            link(dve.tensor_copy(dcol, ps[:, 6, 128:136]))
            TTo(skip, spread(con[:, C_SKIP:C_SKIP + PC], 1, KD), spread(dcol, 2, PC), ALU.mult)
            sq = step[:, :, :, :].rearrange("p n i r -> p (n i) r")

            def cmul(lo, n, by, base):
                r = lambda i: Pw[:, i, base:base + n, :]
                b = lambda i: spread(Pw[:, i, by, :], 1, n)
                TTo(sq[:, 0:n, :], r(0), b(0), ALU.mult)
                link(TTo(sq[:, 2:2 + n, :], r(1), b(1), ALU.mult))
                link(TTo(Pw[:, 0, lo:lo + n, :], sq[:, 0:n, :], sq[:, 2:2 + n, :], ALU.subtract))
                TTo(sq[:, 0:n, :], r(0), b(1), ALU.mult)
                link(TTo(sq[:, 2:2 + n, :], r(1), b(0), ALU.mult))
                link(TTo(Pw[:, 1, lo:lo + n, :], sq[:, 0:n, :], sq[:, 2:2 + n, :], ALU.add))

            cmul(2, 1, 1, 1)
            cmul(3, 2, 2, 1)
            link(TS(Pw[:, 2, 1:5, :], Pw[:, 1, 1:5, :], -1.0, None, ALU.mult))
            dve.tensor_copy(LA[:, 0, :], Pw[:, 0, 4, :])
            dve.tensor_copy(LA[:, 1, :], Pw[:, 0, 4, :])
            dve.tensor_copy(LB[:, 0, :], Pw[:, 2, 4, :])
            link(dve.tensor_copy(LB[:, 1, :], Pw[:, 1, 4, :]))
            dve.sem_inc(pow_ready, 1)
            dve.wait_ge(s_bc, 64)
            r16 = lambda v: v.rearrange("p (r c) -> p r c", r=PAIRS)
            for i in range(2):
                TTo(r16(t1), Bn[:, i, :, :], spread(sc2[:, 0, :], 2, 16), ALU.mult)
                link(TTo(r16(t2), Bn[:, 1 - i, :, :], spread(sc2[:, 1, :], 2, 16), ALU.mult))
                link(TTo(Bb[:, i, :, :], r16(t1), r16(t2), ALU.add if i else ALU.subtract))
            dve.sem_inc(bbar_ready, 1)
            dve.wait_ge(c_ready, 2)
            dve.wait_ge(cleared, 4)
            for g in range(2):
                h = slice(64 * g, 64 * g + 64)
                dve.tensor_copy(Cb[h, 0, :, 16 * g:16 * g + 16], Cc[h, 0, :, :])
                link(TS(Cb[h, 1, :, 16 * g:16 * g + 16], Cc[h, 1, :, :], -1.0, None, ALU.mult))
            dve.wait_ge(u_done, 8)
            for n in range(8, 16):
                stack(dve.tensor_copy, n).then_inc(u4_dve, 1)
            v3 = lambda v: v[:, 0:OCT * 48].rearrange("p (r j c) -> p r j c", r=OCT, j=3)
            for o in range(PAIRS // OCT):
                pr = slice(OCT * o, OCT * o + OCT)
                pw = lambda i: spread(Pw[:, i, 1:4, pr].rearrange("p j r -> p r j"), 3, 16)
                bb = lambda i: spread(Bb[:, i, pr, :], 2, 3)
                if o >= 1:
                    dve.wait_ge(w1_turned, o)
                for i in range(2):
                    TTo(v3(t1), pw(0), bb(i), ALU.mult)
                    link(TTo(v3(t2), pw(1), bb(1 - i), ALU.mult))
                    for g in range(2):
                        h = slice(64 * g, 64 * g + 64)
                        ins = TTo(W1[h, i, :, 1:4, 16 * g:16 * g + 16], v3(t1)[h], v3(t2)[h], ALU.add if i else ALU.subtract)
                        if g == 0:
                            ins.then_inc(dstep, 1)
                            count[0] += 1
                    link(ins)
                dve.sem_inc(w1_ready, 1)
            dve.wait_ge(k_done, 4)
            taps = ps[:, 6:8, :].rearrange("p b n -> p (b n)").rearrange("p (q n) -> p q n", q=KD)[:, :, 0:PC]
            TTo(taps, taps, skip, ALU.add).then_inc(k_ready, 1)
            dve.wait_ge(v_ready, 16)
            for m in range(M):
                dve.wait_ge(state, m + 1)
                TTo(step[:, 0, :, :], LA[:], X[:, m, :, :], ALU.mult).then_inc(prod_a, 1)
                TTo(step[:, 1, 0, :], LB[:, 0, :], X[:, m, 1, :], ALU.mult).then_inc(prod_b, 1)
                TTo(step[:, 1, 1, :], LB[:, 1, :], X[:, m, 0, :], ALU.mult).then_inc(prod_b, 1)
                dve.wait_ge(prod_a, m + 1)
                TTo(step[:, 2, :, :], step[:, 0, :, :], X[:, m + 1, :, :], ALU.add).then_inc(summed, 1)
                dve.wait_ge(prod_b, 2 * m + 2)
                dve.wait_ge(summed, m + 1)
                TTo(X[:, m + 1, :, :], step[:, 2, :, :], step[:, 1, :, :], ALU.add).then_inc(state, 1)
            for n in range(4):
                tt, c = n // 2, n % 2
                dve.wait_ge(sig_ready, n + 1)
                link(TTo(sig[:, 1, :], ps[:, 4 + 2 * (n % 2), :], sig[:, 0, :], ALU.mult))
                TTo(x[:, tt, 512 * c:512 * c + 512], x[:, tt, 512 * c:512 * c + 512], sig[:, 1, :], ALU.add).then_inc(mixed, 1)

            def first_best(dst, v, n, best, tmp, least):
                link(RED(best, v, AX.X, ALU.max))
                link(TTo(tmp, v, spread(best, 2, n), ALU.is_equal))
                link(STT(tmp, tmp, -16.0, spread(con[:, C_SLOT:C_SLOT + n], 1, TT), ALU.mult, ALU.add))
                link(RED(least, tmp, AX.X, ALU.min))
                link(TTo(dst, tmp, spread(least, 2, n), ALU.is_equal))

            def moe(l):
                r = lambda off, n: rt[:, off:off + TT * n].rearrange("p (a n) -> p a n", a=TT)
                c2 = lambda off: rt[:, off:off + TT]
                r48 = lambda off: rt[:, off:off + 64].rearrange("p (a g e) -> p a g e", a=TT, g=NG)
                dve.wait_ge(s_router, 128)
                dve.wait_ge(logits_done, l + 1)
                link(dve.tensor_copy(lg, ps[:, 5, 0:72].rearrange("p (a n) -> p a n", a=TT)))
                gl, el = lg[:, :, 0:NG], lg[:, :, NG:].rearrange("p a (g e) -> p a g e", g=NG)
                link(RED(c2(0), gl, AX.X, ALU.max))
                TTo(r(8, 4), gl, spread(c2(0), 2, NG), ALU.subtract).then_inc(gate_sub, 1)
                link(TTo(r(16, 4), gl, spread(rb[:, l, 0:NG], 1, TT), ALU.add))
                first_best(r(24, 4), r(16, 4), NG, c2(2), r(32, 4), c2(4))
                goh = r(24, 4)
                dve.wait_ge(gate_exp, 2 * l + 1)
                link(RED(c2(40), r(8, 4), AX.X, ALU.add))
                link(dve.reciprocal(c2(42), c2(40)))
                link(TTo(r(32, 4), r(8, 4), goh, ALU.mult))
                link(RED(c2(44), r(32, 4), AX.X, ALU.add))
                link(TTo(c2(46), c2(44), c2(42), ALU.mult))
                gb = spread(goh, 3, NE)
                link(TTo(r48(192), el, gb, ALU.mult))
                link(RED(r(64, 8), r48(192).rearrange("p a g e -> p a e g"), AX.X, ALU.add))
                for tt in range(TT):
                    b48 = rb[:, l, NG:].rearrange("p (g e) -> p g e", g=NG)
                    link(TTo(r48(192)[:, tt], b48, spread(goh[:, tt, :], 2, NE), ALU.mult))
                link(RED(r(80, 8), r48(192).rearrange("p a g e -> p a e g"), AX.X, ALU.add))
                link(RED(c2(0), r(64, 8), AX.X, ALU.max))
                TTo(r(128, 8), r(64, 8), spread(c2(0), 2, NE), ALU.subtract).then_inc(gate_sub, 1)
                dve.wait_ge(gate_exp, 2 * l + 2)
                link(RED(c2(2), r(128, 8), AX.X, ALU.add))
                link(dve.reciprocal(c2(4), c2(2)))
                link(TTo(r(64, 8), r(128, 8), spread(c2(4), 2, NE), ALU.mult))
                link(TTo(r(96, 8), r(64, 8), r(80, 8), ALU.add))
                first_best(r(112, 8), r(96, 8), NE, c2(2), r(144, 8), c2(4))
                link(STT(r(96, 8), r(112, 8), NO, r(96, 8), ALU.mult, ALU.add))
                first_best(r(160, 8), r(96, 8), NE, c2(2), r(144, 8), c2(4))
                link(TTo(r(112, 8), r(112, 8), r(160, 8), ALU.add))
                link(TTo(r(64, 8), r(64, 8), r(112, 8), ALU.mult))
                link(RED(c2(2), r(64, 8), AX.X, ALU.add))
                link(dve.reciprocal(c2(4), c2(2)))
                link(TTo(c2(4), c2(4), c2(46), ALU.mult))
                link(TTo(r(64, 8), r(64, 8), spread(c2(4), 2, NE), ALU.mult))
                for tt in range(TT):
                    ge = lambda v: v[:, tt, :].rearrange("p (g e) -> p g e", g=NG)
                    gs = spread(goh[:, tt, :], 2, NE)
                    link(TTo(ge(msk), gs, spread(r(112, 8)[:, tt, :], 1, NG), ALU.mult))
                    link(TTo(ge(comb[:, :, 0:E]), gs, spread(r(64, 8)[:, tt, :], 1, NG), ALU.mult))
                dve.sem_inc(mask_ready, 1)
                dve.wait_ge(pos_done, l + 1)
                link(STT(slot1[:, :, 0:E], ps[:, 5, 128:192].rearrange("p (a e) -> p a e", a=TT), 1.0, msk, ALU.add, ALU.mult))
                link(RED(rt[:, 0:8], ps[:, 5, 192:224].rearrange("p (q e) -> p q e", q=NQ), AX.X, ALU.max))
                link(TTo(rt[:, 64:120].rearrange("p (q s) -> p q s", q=NQ), spread(rt[:, 0:8], 2, 7),
                         con[:, C_STEP:C_STEP + 56].rearrange("p (q s) -> p q s", q=NQ), ALU.is_gt))
                link(RED(rt[:, 8:16], rt[:, 64:120].rearrange("p (q s) -> p q s", q=NQ), AX.X, ALU.add))
                link(TS(rt[:, 8:16], rt[:, 8:16], 1.0, None, ALU.add))
                link(TTo(rt[:, 128:200].rearrange("p (q s) -> p q s", q=9), spread(rt[:, 8:16], 1, 9),
                         con[:, C_UPTO:C_UPTO + 72].rearrange("p (q s) -> p q s", q=9), ALU.mult))
                link(RED(rt[:, 16:25], rt[:, 128:200].rearrange("p (q s) -> p q s", q=9), AX.X, ALU.add))
                if l == 1:
                    link(TS(rt[:, 16:25], rt[:, 16:25], small[:, 20:21], None, ALU.add))
                link(dve.tensor_copy(cum[l][:, 0:17], rt[:, 8:25]))
                if l == 0:
                    link(dve.tensor_copy(small[:, 20:21], rt[:, 24:25]))
                dve.sem_inc(cum_ready, 1)
                sel4 = lambda v: v.rearrange("p a (e s) -> p a e s", e=QE)


                strip = lambda q: bass.ds(q * QE, QE)
                slots = lambda p: bass.ds(p * SLOTS + C_SLOT, SLOTS)

                def choose(q, p, builds):
                    for tt in range(TT):
                        TTo(sel4(sel)[:, tt], spread(slot1[:, tt, strip(q)], 2, SLOTS),
                            spread(con[:, slots(p)], 1, QE), ALU.is_equal).then_inc(sel_built, 1)
                    dve.wait_ge(sel_built, 2 * builds)
                    for tt in range(TT):
                        TTo(sel4(scw)[:, tt], sel4(sel)[:, tt],
                            spread(comb[:, tt, strip(q)], 2, SLOTS), ALU.mult).then_inc(sel_ready, 1)

                start = 0 if l == 0 else passes_through(dve, 0) + (NQ + 1) * l
                dve.wait_ge(sel_ready, 2 * start + 1)
                choose(0, 0, start + 1)
                with dve.Fori(0, NQ) as q:
                    n0, passes = passes_of(dve, l, q)
                    built = n0 + q + (NQ + 1) * l
                    with dve.Fori(0, passes) as p:
                        n = n0 + p
                        dve.wait_ge(gathered, 2 * n + 1)
                        dve.tensor_copy(xg[:, 0:4, :].rearrange("p k s -> p (k s)"), ps[:, 0, :]).then_inc(xg_ready, 1)
                        dve.wait_ge(gathered, 2 * n + 2)
                        choose(q, p + 1, built + p + 2)
                        dve.wait_ge(sil_ready, n + 1)
                        TTo(hid, ps[:, 2, 256:512], sil, ALU.mult).then_inc(hid_ready, 1)
                        dve.wait_ge(hid_turned, n + 1)
                        dve.tensor_copy(kept[:, bass.ds(p, 1), 0:256].rearrange("p n c -> p (n c)"), ps[:, 3, 256:512]).then_inc(hidT_kept, 1)
                    dve.wait_ge(hidT_kept, n0 + 2)
                    dve.wait_ge(down_done, n0 + 1)
                    dve.tensor_copy(hidT, kept[:, 0, 0:256]).then_inc(down_ready, 1)
                    dve.wait_ge(sel_ready, 2 * (built + passes) + 3)
                    choose(q + 1, 0, built + passes + 2)
                    with dve.Fori(0, passes) as p:
                        n = n0 + p
                        dve.wait_ge(down_done, n + 2)
                        dve.tensor_copy(yy[:, 512:1024], ps[:, 5, :]).then_inc(y_ready, 1)
                        dve.tensor_copy(hidT, kept[:, bass.ds(p + 1, 1), 0:256].rearrange("p n c -> p (n c)")).then_inc(down_ready, 1)
                        for tt in range(TT):
                            dve.wait_ge(scattered, 2 * n + 2 + tt)
                            b = 6 if tt else 0
                            TTo(x[:, tt, :], x[:, tt, :], ps[:, b:b + 2, :].rearrange("p b n -> p (b n)"), ALU.add).then_inc(x_added, 1)

            norm(1)
            moe(0)
            norm(2)
            lambda_init = 0.8 - 0.6 * math.exp(-0.3)
            dve.wait_ge(s_att, 80)
            l4 = lam4.rearrange("p (n i) c -> p n i c", i=2)
            link(TTo(rope1[:, 0:128].rearrange("p (n c) -> p n c", n=2), l4[:, :, 0, :], l4[:, :, 1, :], ALU.mult))
            RED(asm[:, 0:2], rope1[:, 0:128].rearrange("p (n c) -> p n c", n=2), AX.X, ALU.add).then_inc(lam_sum, 1)
            dve.wait_ge(lam_exp, 1)
            link(TTo(asm[:, 4:5], asm[:, 3:4], asm[:, 2:3], ALU.subtract))
            link(TS(asm[:, 4:5], asm[:, 4:5], -lambda_init, None, ALU.add))
            link(TS(subg, subg, 1.0 - lambda_init, None, ALU.mult))
            def rotate(tt, c):
                cs = con[:, C_ROPE + 128 * tt:C_ROPE + 128 * tt + 64]
                sn = con[:, C_ROPE + 128 * tt + 64:C_ROPE + 128 * tt + 128]
                i = 4 * tt + c
                dve.wait_ge(qkv_done, 6 * tt + c + 1)
                if i:
                    dve.wait_ge(qkv_kept, i)
                if i >= 2:
                    dve.wait_ge(qk_turned, i - 1)
                src = ps[:, c if tt == 0 else c % 2, :].rearrange("p (h n) -> p h n", h=8)
                ra, rc = (v.rearrange("p (h n) -> p h n", h=8) for v in (rope1, rope2))
                TTo(ra, src, spread(cs, 1, 8), ALU.mult).then_inc(dstep, 1)
                TTo(rc[:, :, 0:32], src[:, :, 32:64], spread(sn[:, 0:32], 1, 8), ALU.mult).then_inc(dstep, 1)
                count[0] += 2
                link(TTo(rc[:, :, 32:64], src[:, :, 0:32], spread(sn[:, 32:64], 1, 8), ALU.mult))
                TTo(nat[:, c % 2, :], rope1, rope2, ALU.add).then_inc(qkv_kept, 1)

            def peak(g):
                b, _, heads, sbank, _, _, _ = groups[g]
                keys = P * (b + 1)
                row = soft_row[:, g % 2, :]
                dve.wait_ge(scores_done, g + 1)
                sv = ps[:, sbank:sbank + 2, :].rearrange("p j (h n) -> p j h n", h=heads)
                for j in range(2):
                    ins = dve.memset(sv[0:CHUNK, j, :, keys - CHUNK:keys], NO)
                link(ins)
                link(RED(row[:, 0:2 * heads].rearrange("p (j h) -> p j h", j=2), sv, AX.X, ALU.max))
                TS(row[:, 8:8 + 2 * heads], row[:, 0:2 * heads], -(DH ** -0.5), None, ALU.mult).then_inc(peak_ready, 1)

            def combine(g):
                b, _, heads, _, _, _, _ = groups[g]
                keys = P * (b + 1)
                row = soft_row[:, g % 2, :]
                dve.wait_ge(exp_ready, exps[g])
                link(dve.reciprocal(row[:, 24:24 + 2 * heads], row[:, 16:16 + 2 * heads]))
                link(TS(row[:, 32:32 + heads], row[:, 24 + heads:24 + 2 * heads], asm[:, 4:5], None, ALU.mult))
                if g >= 1:
                    dve.wait_ge(att_turned, g)
                for h in range(heads):
                    k = slice(keys * h, keys * h + keys)
                    ins = TS(at[:, k], Pb[:, g % 2, 1, k], row[:, 32 + h:33 + h], None, ALU.mult)
                link(ins)
                for h in range(heads):
                    k = slice(keys * h, keys * h + keys)
                    ins = STT(at[:, k], Pb[:, g % 2, 0, k], row[:, 24 + h:25 + h], at[:, k], ALU.mult, ALU.add)
                ins.then_inc(att_ready, 1)

            def norm_o(b):
                hv = osb[b].rearrange("p (h e) -> p h e", h=H)
                sqv = osq2.rearrange("p (h e) -> p h e", h=H)
                dve.wait_ge(osq, 2 * b + 2)
                dve.wait_ge(qkv_kept, 8)
                link(TTo(sqv, hv, hv, ALU.mult))
                link(RED(asm[:, 16 + 8 * b:24 + 8 * b], sqv, AX.X, ALU.add))
                TS(asm[:, 16 + 8 * b:24 + 8 * b], asm[:, 16 + 8 * b:24 + 8 * b], 1.0 / P, EPS, ALU.mult, ALU.add).then_inc(ovar, 1)
                dve.wait_ge(oroot, b + 1)
                link(dve.reciprocal(asm[:, 32 + 8 * b:40 + 8 * b], asm[:, 32 + 8 * b:40 + 8 * b]))
                link(TTo(hv, hv, spread(asm[:, 32 + 8 * b:40 + 8 * b], 2, P), ALU.mult))
                TTo(hv, hv, spread(subg, 1, H), ALU.mult).then_inc(o_ready, 1)

            def add_mix(n, bank):
                b, c = n // 2, n % 2
                dve.wait_ge(wo_done, n + 1)
                TTo(x[:, b, 512 * c:512 * c + 512], x[:, b, 512 * c:512 * c + 512], ps[:, bank, :], ALU.add).then_inc(mixed, 1)

            for c in range(4):
                rotate(0, c)
            peak(0)
            rotate(1, 0)
            peak(1)
            combine(0)
            rotate(1, 1)
            combine(1)
            rotate(1, 2)
            rotate(1, 3)
            norm_o(0)
            peak(2)
            peak(3)
            combine(2)
            peak(4)
            combine(3)
            add_mix(0, 5)
            peak(5)
            combine(4)
            add_mix(1, 5)
            combine(5)
            norm_o(1)
            add_mix(2, 0)
            add_mix(3, 1)
            norm(3)
            moe(1)
            norm(4)

        @block.tensor
        def _(pe):
            mm = pe.matmul

            def turn(i):
                pe.wait_ge(normed, 2 * i + 2)
                for k in range(KD):
                    for tt in range(TT):
                        ins = pe.transpose(ps[:, k // 2, 256 * (k % 2) + P * tt:256 * (k % 2) + P * tt + P], xr[:, tt, k, :], ident)
                ins.then_inc(hT_psum, 1)

            for first in (down_done, scattered):
                pe.sem_inc(first, 1)
            pe.wait_ge(s_con, 16)
            turn(0)
            pe.wait_ge(lam_ready, 1)
            for n, v in enumerate((1, 2, 3, 4)):
                pe.transpose(ps[:, 6, 32 * n:32 * n + 32], lam2[:, v, :], ident[0:32, 0:32]).then_inc(lam_psum, 1)
            pe.transpose(ps[:, 6, 128:136], drep[0:8, :], ident[0:8, 0:8]).then_inc(lam_psum, 1)
            pe.wait_ge(s_bc, 64)
            idg = ident.rearrange("p (r g h) -> p r g h", g=2, h=16)
            for i in range(2):
                for c in range(KD):
                    for g in range(2):
                        ins = mm(ps[64 * g:64 * g + 64, 4 + i, 64 * c:64 * c + 64], Cn[:, i, c, :], idg[:, :, g, :],
                                 start=True, stop=True)
            ins.then_inc(c_psum, 1)
            pe.wait_ge(hT_ready, 4)
            for c in range(KD):
                if c % 4 == 0:
                    pe.wait_ge(landed[c // 4], 32)
                for k in range(KD):
                    ins = mm(ps[:, c // 2, 256 * (c % 2):256 * (c % 2) + 256], win[c // 4][:, k, P * (c % 4):P * (c % 4) + P],
                             hT[:, k, :], start=(k == 0), stop=(k == KD - 1))
                ins.then_inc(u_done, 1)
            pe.wait_ge(u_done, 8)
            for u in range(2):
                pe.sem_inc(used[u], 1)
            for o in range(PAIRS // OCT):
                pe.wait_ge(w1_ready, o + 1)
                pe.wait_ge(w1_first, 4 * o + 4)
                if o == 0:
                    pe.wait_ge(u4_act, 8)
                    pe.wait_ge(u4_dve, 8)
                    pe.wait_ge(c_ready, 2)
                else:
                    pe.wait_ge(w1T_ready, 4 * o)
                for i in range(2):
                    for r in range(OCT):
                        ins = pe.transpose(ps[:, 2 * i + r // 4, P * (r % 4):P * (r % 4) + P],
                                           W1[:, i, r, :, :].rearrange("p j c -> p (j c)"), ident)
                ins.then_inc(w1_turned, 1)
                for r in range(OCT):
                    if r % 4 == 0 and o >= 1:
                        pe.wait_ge(v_ready, 4 * o)
                    if r == 0:
                        pe.wait_ge(w1T_ready, 4 * o + 4)
                    for i in range(2):
                        ins = mm(ps[:, 4 + r // 4, P * (r % 4) + 64 * i:P * (r % 4) + 64 * i + 64], W1T[:, i, r, :],
                                 U4[:, OCT * o + r, :], start=True, stop=True)
                    if r % 4 == 3:
                        ins.then_inc(v_done, 1)
                pe.wait_ge(w2_ready, o + 1)
                for r in range(OCT):
                    pair = OCT * o + r
                    q = slice(32 * (pair % 4), 32 * (pair % 4) + 32)
                    at0 = P * (pair // 4 % 4)
                    for lo, hi, taps in ((0, PC, Cb), (PC, P, W2)):
                        for i in range(2):
                            ins = mm(ps[q, 6 + pair // 16, at0 + lo:at0 + hi], W1[:, i, r, 0, :], taps[:, i, pair, 0:hi - lo],
                                     start=(i == 0), stop=(i == 1))
                ins.then_inc(k_done, 1)
            def y(pair):
                return ps[:, pair // 8, 64 * (pair % 8):64 * (pair % 8) + 64]

            pe.wait_ge(f_ready, 16)
            for r in range(PAIRS):
                mm(y(r), Fw[:, r, :], U4[:, r, :], start=(r % 8 == 0), stop=False, skip_group_check=True)
            pe.wait_ge(state, M + 1)
            for r in range(PAIRS):
                for i in range(2):
                    ins = mm(y(r), W2[:, i, r, :], X[:, 0:M, i, r], start=False, stop=(i == 1), skip_group_check=True)
                ins.then_inc(y_done, 1)
            for n in range(4):
                tt, c = n // 2, n % 2
                if n >= 2:
                    pe.wait_ge(mixed, n - 1)
                for half in range(2):
                    u = 2 + 2 * half + c
                    pe.wait_ge(landed[u], 32)
                    for k in range(KD):
                        if n == 0 and half == 0 and k % 2 == 0:
                            pe.wait_ge(g_ready, 8 * k + 16)
                        ins = mm(ps[:, 4 + 2 * (n % 2) + half, :], gT[:, k, tt * P:(tt + 1) * P], win[u][:, k, :],
                                 start=(k == 0), stop=(k == KD - 1))
                    if n >= 2:
                        if half == 0:
                            ins.then_inc(used[u], 1)
                ins.then_inc(glu_done, 1)
                if n == 3:
                    pe.wait_ge(glu_done, 4)
                    for u in (4, 5):
                        pe.sem_inc(used[u], 1)

            def moe(l):
                pe.wait_ge(hT_ready, 8 * (l + 1))
                pe.wait_ge(s_router, 128)
                for k in range(KD):
                    ins = mm(ps[0:NG + E, 4, 0:T], wr[:, l, k, :], hT[:, k, :], start=(k == 0), stop=(k == KD - 1))
                ins.then_inc(logits_turned, 1)
                pe.wait_ge(logits_kept, l + 1)
                for tt in range(TT):
                    ins = pe.transpose(ps[:, 5, 36 * tt:36 * tt + 36], lgT[0:NG + E, tt * P:(tt + 1) * P], ident[0:NG + E, 0:NG + E])
                ins.then_inc(logits_done, 1)
                pe.wait_ge(mask_ready, l + 1)
                mm(ps[:, 5, 128:160], before, msk[:, 0, :], start=True, stop=True)
                mm(ps[:, 5, 160:192], before, msk[:, 1, :], start=True, stop=False)
                mm(ps[:, 5, 160:192], ones, msk[:, 0, :], start=False, stop=True)
                mm(ps[:, 5, 192:224], ones, msk[:, 0, :], start=True, stop=False)
                mm(ps[:, 5, 192:224], ones, msk[:, 1, :], start=False, stop=True).then_inc(pos_done, 1)
                pe.wait_ge(cum_ready, l + 1)
                pe.wait_ge(part_ready, 3 * l + 3)
                with pe.Fori(0, NQ) as q:
                    n0, passes = passes_of(pe, l, q)
                    rounds = (q + (qround(l, 0) + 1)) * 32
                    with pe.Fori(0, passes) as p:
                        n = n0 + p
                        pe.wait_ge(sel_ready, 2 * (n + q) + (2 * (NQ + 1) * l + 3))
                        pe.wait_ge(hidT_kept, n + 1)
                        for tt in range(TT):
                            ins = pe.transpose(ps[:, 3, P * tt:P * tt + P], scw[:, tt, :], ident)
                        ins.then_inc(sw_turned, 1)
                        pe.wait_ge(x_added, 2 * n0 + 1)
                        for k in range(KD):
                            for tt in range(TT):
                                for i in range(3):
                                    ins = mm(ps[:, k // 4, P * (k % 4):P * (k % 4) + P], parts[i][:, tt, k, :], sel[:, tt, :],
                                             start=(tt == 0 and i == 0), stop=(tt == TT - 1 and i == 2))
                            if k % 4 == 3:
                                ins.then_inc(gathered, 1)
                        pe.wait_ge(xg_ready, 2 * n + 2)
                        for k in range(KD):
                            if k % 2 == 0:
                                pe.wait_ge(landed[k // 2], rounds)
                            for e in range(QE):
                                s = slice(32 * e, 32 * e + 32)
                                ins = mm(ps[s, 2, :], xg[:, k, s], gu[k // 2][:, e, :, k % 2, :],
                                         start=(k == 0), stop=(k == KD - 1))
                            if k % 2 == 1 and k < KD - 1:
                                ins.then_inc(used[k // 2], 1)
                        ins.then_inc(gu_done, 1)
                        pe.wait_ge(gu_done, n + 1)
                        pe.wait_ge(hid_ready, n + 1)
                        pe.wait_ge(sw_ready, n + 1)
                        pe.transpose(ps[:, 3, 256:384], hid[:, 0:P], ident).then_inc(used[3], 1)
                        pe.transpose(ps[:, 3, 384:512], hid[:, P:2 * P], ident).then_inc(hid_turned, 1)
                    with pe.Fori(0, passes) as p:
                        n = n0 + p
                        pe.wait_ge(down_ready, n + 1 + (q + NQ * l))
                        pe.wait_ge(y_ready, 2 * n + 1)
                        for k in range(2):
                            pe.wait_ge(landed[4 + k], rounds)
                            for half in range(2):
                                for e in range(QE):
                                    s = slice(32 * e, 32 * e + 32)
                                    ins = mm(ps[s, 4 + half, :], hidT[:, P * k + 32 * e:P * k + 32 * e + 32],
                                             dn[k][:, e, 512 * half:512 * half + 512], start=(k == 0), stop=(k == 1))
                            if k == 0:
                                ins.then_inc(used[4], 1)
                        ins.then_inc(down_done, 1)
                        pe.wait_ge(back_ready, n + 1)
                        pe.wait_ge(y_ready, 2 * n + 3)
                        pe.wait_ge(x_added, 2 * n + 2)
                        for tt in range(TT):
                            for half in range(2):
                                ins = mm(ps[:, (6 if tt else 0) + half, :], swT[:, P * tt:P * tt + P],
                                         yy[:, 512 * half:512 * half + 512], start=True, stop=True)
                                if tt == 0 and half == 0:
                                    ins.then_inc(used[5], 1)
                            ins.then_inc(scattered, 1)

            turn(1)
            moe(0)
            turn(2)
            def project(tt, c):
                pe.wait_ge(landed[c], 32 * (NQ + 2))
                if tt:
                    if c in (0, 1):
                        pe.wait_ge(qkv_kept, 2)
                    elif c in (2, 3):
                        pe.wait_ge(qkv_kept, 3 + c)
                    else:
                        pe.wait_ge(qkv_kept, 3 + c)
                for k in range(KD):
                    ins = mm(ps[:, c if tt == 0 else c % 2, :], hT[:, k, tt * P:(tt + 1) * P], win[c][:, k, :],
                             start=(k == 0), stop=(k == KD - 1))
                ins.then_inc(qkv_done, 1)

            def turn_qk(tt, c):
                i = 4 * tt + c
                pe.wait_ge(qkv_kept, i + 1)
                if i in (2, 3, 6, 7):
                    pe.wait_ge(qkT_ready, i - 1)
                for h in range(4):
                    ins = pe.transpose(ps[:, (6 if tt == 0 else 2) + c % 2, P * h:P * h + P], nat[:, c % 2, P * h:P * h + P], ident)
                ins.then_inc(qk_turned, 1)

            def scores(g):
                b, h0, heads, sbank, _, _, _ = groups[g]
                keys = P * (b + 1)
                pe.wait_ge(qkT_ready, 4 * (b + 1))
                if g in (1, 4, 5):
                    pe.wait_ge(exp_ready, exps[0 if g == 1 else g - 2])
                for h in range(heads):
                    for j in range(2):
                        s = slice(64 * j, 64 * j + 64)
                        ins = mm(ps[:, sbank + j, keys * h:keys * h + keys], qk[s, h0 + h, b * P:(b + 1) * P],
                                 qk[s, 8 + h0 + h, 0:keys], start=True, stop=True)
                ins.then_inc(scores_done, 1)

            def turn_att(g):
                pe.wait_ge(att_ready, g + 1)
                if g:
                    pe.wait_ge(attT_ready, g)
                for n in range(4):
                    ins = pe.transpose(ps[:, groups[g][4], P * n:P * n + P], at[:, P * n:P * n + P], ident)
                ins.then_inc(att_turned, 1)

            def values(g):
                b, h0, heads, _, _, obank, col = groups[g]
                pe.wait_ge(attT_ready, g + 1)
                pe.wait_ge(v_kept, 2 * b + 2)
                if g == 1:
                    pe.wait_ge(osq, 1)
                if g >= 2:
                    pe.wait_ge(osq, 2)
                for h in range(heads):
                    for k in range(b + 1):
                        n = (b + 1) * h + k
                        ins = mm(ps[:, obank, col + P * h:col + P * h + P], atT[:, g % 2, P * n:P * n + P],
                                 vv[:, k, P * (h0 + h):P * (h0 + h) + P], start=(k == 0), stop=(k == b))
                ins.then_inc(av_done, 1)

            def turn_o(b, c, bank):
                pe.wait_ge(o_ready, b + 1)
                if b == 0 and c == 1:
                    pe.wait_ge(oT_ready, 1)
                for h in range(4):
                    ins = pe.transpose(ps[:, bank, P * h:P * h + P], osb[b][:, 512 * c + P * h:512 * c + P * h + P], ident)
                ins.then_inc(o_turned, 1)

            def out_proj(n, bank):
                b, c = n // 2, n % 2
                pe.wait_ge(s_wo, 16)
                pe.wait_ge(oT_ready, 2 * b + 2)
                if n:
                    pe.wait_ge(mixed, 4 + min(n, 2))
                for k in range(KD):
                    ins = mm(ps[:, bank, :], oT[:, k, b * P:(b + 1) * P], wo[:, k, 512 * c:512 * c + 512],
                             start=(k == 0), stop=(k == KD - 1))
                ins.then_inc(wo_done, 1)

            pe.wait_ge(hT_ready, 12)
            project(0, 0)
            project(0, 1)
            turn_qk(0, 0)
            project(0, 2)
            turn_qk(0, 1)
            project(0, 3)
            turn_qk(0, 2)
            project(0, 4)
            turn_qk(0, 3)
            project(0, 5)
            pe.wait_ge(v_kept, 2)
            scores(0)
            project(1, 0)
            scores(1)
            project(1, 1)
            turn_att(0)
            turn_qk(1, 0)
            values(0)
            project(1, 2)
            turn_att(1)
            turn_qk(1, 1)
            values(1)
            project(1, 3)
            turn_qk(1, 2)
            project(1, 4)
            turn_qk(1, 3)
            project(1, 5)
            pe.wait_ge(qkv_done, 12)
            for u in range(UNITS):
                pe.sem_inc(used[u], 1)
            pe.wait_ge(v_kept, 4)
            scores(2)
            scores(3)
            turn_att(2)
            turn_o(0, 0, 5)
            values(2)
            scores(4)
            turn_att(3)
            turn_o(0, 1, 5)
            values(3)
            out_proj(0, 5)
            scores(5)
            turn_att(4)
            values(4)
            out_proj(1, 5)
            turn_att(5)
            values(5)
            turn_o(1, 0, 4)
            turn_o(1, 1, 5)
            out_proj(2, 0)
            out_proj(3, 1)
            turn(3)
            moe(1)


_INS = ['x', 'norm_mix_g', 'norm_ffn_g', 'final_norm_g', 'ssm_w_in', 'ssm_lam_re', 'ssm_lam_im', 'ssm_log_dt',
        'ssm_b_re', 'ssm_b_im', 'ssm_c_re', 'ssm_c_im', 'ssm_d', 'ssm_w_glu', 'attn_w_qkv', 'attn_lambda_q1',
        'attn_lambda_k1', 'attn_lambda_q2', 'attn_lambda_k2', 'attn_subln_g', 'attn_w_o', 'moe_w_router_group',
        'moe_b_router_group', 'moe_w_router_expert', 'moe_b_router_expert', 'moe_w_gate', 'moe_w_up', 'moe_w_down']


def kernel(**inputs):
    import concourse.bacc as bacc
    from concourse.bass_utils import run_bass_kernel_spmd as run

    nc = bacc.Bacc("TRN2", target_bir_lowering=False, num_devices=1)
    arrays = {"in_con": constants()}
    for name in _INS:
        arrays["in_" + name] = np.ascontiguousarray(inputs[name])
    aps = {n[3:]: nc.dram_tensor(n, v.shape, mybir.dt.from_np(v.dtype), kind="ExternalInput").ap() for n, v in arrays.items()}
    out = nc.dram_tensor("out", (1, T, D), F32, kind="ExternalOutput").ap()
    build(nc, aps, out)
    return run(nc, [arrays], core_ids=[0]).results[0]["out"]
```

```python
import math
from contextlib import ExitStack

import numpy as np
import concourse.bass as bass
from concourse import mybir

F32 = mybir.dt.float32
I32 = mybir.dt.int32
BF16 = mybir.dt.bfloat16
ALU = mybir.AluOpType
ACT = mybir.ActivationFunctionType
AX = mybir.AxisListType

P = 128
D = 1024
T = 256
TT = T // P
KD = D // P
EPS = 1e-6
SB = 4
M = T // SB
PAIRS = 32
PC = 32
OCT = 8
H = 8
DH = 64
CHUNK = 64
NG, NE, FE = 4, 8, 256
E = NG * NE
QE = 4
NQ = E // QE
SLOTS = 32
MAXPASS = T // SLOTS
UNIT = 4096
UNITS = 6
NO = -1.0e30

C_ID = 0
C_BEFORE = C_ID + P
C_ONES = C_BEFORE + P
C_SLOT = C_ONES + P
C_SKIP = C_SLOT + T + SLOTS
C_ROPE = C_SKIP + PC
C_STEP = C_ROPE + TT * 4 * 32
C_UPTO = C_STEP + NQ * 7
C_TURN = C_UPTO + 9 * 8
C_N = C_TURN + 1


def constants():
    c = np.zeros((P, C_N), np.float32)
    i = np.arange(P)
    c[:, C_ID:C_ID + P] = np.eye(P)
    c[:, C_BEFORE:C_BEFORE + P] = i[:, None] < i[None, :]
    c[:, C_ONES:C_ONES + P] = 1.0
    c[:, C_SLOT:C_SKIP] = np.arange(1, T + SLOTS + 1)
    c[:, C_SKIP:C_SKIP + PC] = i[:, None] % PC == np.arange(PC)[None, :]
    inv = np.float32(10000.0) ** (-np.arange(0, DH, 2, dtype=np.float32) / np.float32(DH))
    ang = np.arange(T, dtype=np.float32)[:, None] * inv[None, :]
    cos, sin = np.cos(ang).astype(np.float32), np.sin(ang).astype(np.float32)
    rope = np.concatenate([cos, cos, -sin, sin], axis=1).reshape(TT, P, 128)
    for tt in range(TT):
        c[:, C_ROPE + 128 * tt:C_ROPE + 128 * (tt + 1)] = rope[tt]
    c[:, C_STEP:C_STEP + NQ * 7] = np.tile(SLOTS * np.arange(1, 8), NQ)
    c[:, C_UPTO:C_UPTO + 72] = (np.arange(8)[None, :] < np.arange(9)[:, None]).reshape(-1)
    c[:, C_TURN] = math.pi / 2
    return c


def spread(ap, axis, n):
    a = ap.unsqueeze(axis)
    shape = list(a.shape)
    shape[axis] = n
    return a.to_broadcast(shape)


def build(nc, a, out):
    with ExitStack() as ctx:
        ctx.enter_context(nc.allow_non_contiguous_dma(reason="short runs of the small parameters"))

        def sb(name, shape, dt=F32):
            return ctx.enter_context(nc.sbuf_tensor(name, shape, dt))

        def sem(name):
            return ctx.enter_context(nc.semaphore(name))

        ring = sb("ring", [P, UNITS, UNIT])
        x = sb("x", [P, TT, D])
        xr = sb("xr", [P, TT, KD, P])
        hT = sb("hT", [P, KD, T])
        gains = sb("gains", [P, 2, D])
        con = sb("con", [P, C_N])
        wr = sb("wr", [P, 2, KD, NG + E])
        rb = sb("rb", [P, 2, NG + E])
        small = sb("small", [P, 64])
        cum = [sb(f"cum{l}", [P, 17], I32) for l in range(2)]
        work = sb("work", [P, 18560])
        ps = ctx.enter_context(nc.psum_tensor("ps", [P, 8, 512], F32))

        ident = con[:, C_ID:C_ID + P]
        before = con[:, C_BEFORE:C_BEFORE + P]
        ones = con[:, C_ONES:C_ONES + P]

        def part(off, n):
            return work[:, off:off + n]

        Fw = part(0, 4096).rearrange("p (r c) -> p r c", r=PAIRS)
        W2 = part(4096, 8192).rearrange("p (i r c) -> p i r c", i=2, r=PAIRS)
        X = part(12288, 64 * M).rearrange("p (o i r m) -> p o i r m", o=PAIRS // OCT, i=2, r=OCT)
        o = 12288 + 64 * M
        Pw = part(o, 3 * 5 * PAIRS).rearrange("p (i j r) -> p i j r", i=3, j=5)
        o += 480
        sc2 = part(o, 64).rearrange("p (i r) -> p i r", i=2)
        o += 64
        dcol = part(o, 8)
        o += 8
        turns = part(o, 576).rearrange("p (i n r) -> p i n r", i=2, n=9)
        o += 576
        turns8 = part(o, 512).rearrange("p (i n r) -> p i n r", i=2, n=8)
        o += 512
        turns2 = part(o, 128).rearrange("p (i n r) -> p i n r", i=2, n=2)
        o += 128
        skip = part(o, 256).rearrange("p (q c) -> p q c", q=KD)
        o += 256
        drep = part(o, 128)
        o += 128
        assert o <= 18560
        U4 = gains[:].rearrange("p a n -> p (a n)").rearrange("p (r m) -> p r m", r=PAIRS)
        gT = xr[:].rearrange("p a k q -> p (a k q)").rearrange("p (c t) -> p c t", c=KD)
        pre = ring[:, 3:6, :].rearrange("p u n -> p (u n)")
        W1 = pre[:, 0:2048].rearrange("p (i r j c) -> p i r j c", i=2, r=OCT, j=SB)
        W1T = pre[:, 2048:4096].rearrange("p (i r c) -> p i r c", i=2, r=OCT)
        Bn = pre[:, 4096:5120].rearrange("p (i r c) -> p i r c", i=2, r=PAIRS)
        Bb = pre[:, 5120:6144].rearrange("p (i r c) -> p i r c", i=2, r=PAIRS)
        Cn = pre[:, 6144:7168].rearrange("p (i c s) -> p i c s", i=2, c=KD)
        Cc = pre[:, 7168:8192].rearrange("p (i r c) -> p i r c", i=2, r=PAIRS)
        Cb = pre[:, 8192:10240].rearrange("p (i r c) -> p i r c", i=2, r=PAIRS)
        t1 = pre[:, 10240:10752]
        t2 = pre[:, 10752:11264]
        table = ring[:, 2, :].rearrange("p (i r m) -> p i r m", i=2, r=PAIRS)
        lam = pre[0:32, 11264:12288].rearrange("p (n c) -> p n c", c=P)
        lam2 = work[0:32, 12352:13376].rearrange("p (n c) -> p n c", c=P)
        t3 = xr[:, 0, 0:4, :].rearrange("p k q -> p (k q)")
        t4 = xr[:, 0, 4:8, :].rearrange("p k q -> p (k q)")
        decay = ([pre[:, 6144 + 512 * n:6656 + 512 * n] for n in range(2)] +
                 [xr[:, 1, 4 * n:4 * n + 4, :].rearrange("p k q -> p (k q)") for n in range(2)])
        rot1, rot2 = pre[:, 4096:5120], pre[:, 11264:12288]
        sig = part(0, 1024).rearrange("p (n c) -> p n c", n=2)
        o = 0
        xg = part(o, 1024).rearrange("p (k s) -> p k s", k=KD)
        o += 1024
        sel = part(o, 128).bitcast(BF16).rearrange("p (a s) -> p a s", a=TT)
        o += 128
        scw = part(o, 256).rearrange("p (a s) -> p a s", a=TT)
        o += 256
        sil = part(o, 256)
        o += 256
        hid = part(o, 256)
        o += 256
        hidT = part(o, 256)
        o += 256
        swT = part(o, 256)
        o += 256
        kept = part(o, (MAXPASS + 1) * 512).rearrange("p (n c) -> p n c", n=MAXPASS + 1)
        o += (MAXPASS + 1) * 512
        lgT = sil
        lowest = part(o, 1024)
        o += 1024
        parts = [v.bitcast(BF16).rearrange("p (a k q) -> p a k q", a=TT, k=KD)
                 for v in (hT[:, 0:4, :].rearrange("p k t -> p (k t)"), hT[:, 4:8, :].rearrange("p k t -> p (k t)"), lowest)]
        yy = part(o, 1024)
        o += 1024
        lg = part(o, 72).rearrange("p (a n) -> p a n", a=TT)
        o += 72
        slot1 = part(o, 72).rearrange("p (a e) -> p a e", a=TT)
        o += 72
        comb = part(o, 72).rearrange("p (a e) -> p a e", a=TT)
        o += 72
        msk = part(o, 64).rearrange("p (a e) -> p a e", a=TT)
        o += 64
        rt = part(o, 512)
        o += 512
        assert o <= 10208
        wo = part(10208, 8192).rearrange("p (k n) -> p k n", k=KD)
        qk = part(0, 4096).rearrange("p (h t) -> p h t", h=16)
        vv = part(4096, 2048).rearrange("p (a n) -> p a n", a=TT)
        nat = part(6144, 1024).rearrange("p (b n) -> p b n", b=2)
        osb = [part(7168, 1024), part(6144, 1024)]
        oT = part(0, 2048).rearrange("p (k t) -> p k t", k=KD)
        rope1 = part(8192, 512)
        rope2 = part(8704, 512)
        osq2 = part(8192, 1024)
        at = part(9216, 512)
        pv_rest = part(9728, 480)
        lam4 = pv_rest[:, 0:256].rearrange("p (n c) -> p n c", n=4)
        soft_row = pv_rest[:, 0:128].rearrange("p (b n) -> p b n", b=2)
        subg = pv_rest[:, 256:384]
        asm = pv_rest[:, 384:480]
        Pb = xr[:].rearrange("p a k q -> p a (k q)").rearrange("p b (i n) -> p b i n", i=2)
        atT = gains[:, 0, :].rearrange("p (b n) -> p b n", b=2)
        groups = [(0, 0, 4, 4, 6, 7, 0), (0, 4, 4, 4, 6, 7, 0),
                  (1, 0, 2, 0, 4, 6, 0), (1, 2, 2, 2, 4, 6, 256), (1, 4, 2, 0, 4, 7, 0), (1, 6, 2, 2, 4, 7, 256)]
        exps = [8, 16, 20, 24, 28, 32]

        s_con, s_x, s_lam, s_bc, s_router, s_gain0, s_gain, s_att, s_wo = (
            sem(n) for n in ("con_in", "x_in", "lam_in", "bc_in", "router_in", "gain0_in", "gain_in", "att_in", "wo_in"))
        landed = [sem(f"landed{u}") for u in range(UNITS + 2)]
        used = [sem(f"used{u}") for u in range(UNITS)]
        out_done = sem("out_done")
        dstep, pstep = sem("dve_steps"), sem("pool_steps")
        squares, var_ready, root_ready, normed = (sem(n) for n in ("squares", "var_ready", "root_ready", "normed"))
        hT_psum, hT_ready = sem("hT_psum"), sem("hT_ready")
        mixed = sem("mixed")
        dt_ready, er_ready, arg_ready, sin_ready = (sem(n) for n in ("dt_ready", "er_ready", "arg_ready", "sin_ready"))
        lam_ready, lam_psum, c_psum, c_ready = (sem(n) for n in ("lam_ready", "lam_psum", "c_psum", "c_ready"))
        cleared = sem("cleared")
        u_done, u4_ready = sem("u_done"), sem("u4_ready")
        w1_ready, w2_ready, w1_turned, w1T_ready = (sem(n) for n in ("w1_ready", "w2_ready", "w1_turned", "w1T_ready"))
        part_ready, rest_ready = sem("part_ready"), sem("rest_ready")
        k_done, k_ready, f_ready, v_done, v_ready = (sem(n) for n in ("k_done", "k_ready", "f_ready", "v_done", "v_ready"))
        bbar_ready, pow_ready, w1_first = sem("bbar_ready"), sem("pow_ready"), sem("w1_first")
        turns_ready, table_ready, decay_ready = (sem(n) for n in ("turns_ready", "table_ready", "decay_ready"))
        scanned, state, last_state = (sem(n) for n in ("scanned", "state", "last_state"))
        y_done, g_ready = sem("y_done"), sem("g_ready")
        glu_done, sig_ready, glu_prod = sem("glu_done"), sem("sig_ready"), sem("glu_prod")
        logits_turned, logits_kept = sem("logits_turned"), sem("logits_kept")
        logits_done, gate_sub, gate_exp, mask_ready, pos_done, cum_ready = (
            sem(n) for n in ("logits_done", "gate_sub", "gate_exp", "mask_ready", "pos_done", "cum_ready"))
        sel_built, sel_ready, sw_turned, sw_ready, gathered, xg_ready = (
            sem(n) for n in ("sel_built", "sel_ready", "sw_turned", "sw_ready", "gathered", "xg_ready"))
        hidT_kept, down_ready, back_ready = sem("hidT_kept"), sem("down_ready"), sem("back_ready")
        gu_done, sil_ready, hid_ready, hid_turned, down_done, y_ready, scattered, x_added = (
            sem(n) for n in ("gu_done", "sil_ready", "hid_ready", "hid_turned", "down_done",
                             "y_ready", "scattered", "x_added"))
        qkv_done, qkv_kept, v_kept, qk_turned, qkT_ready = (
            sem(n) for n in ("qkv_done", "qkv_kept", "v_kept", "qk_turned", "qkT_ready"))
        lam_sum, lam_exp = sem("lam_sum"), sem("lam_exp")
        scores_done, peak_ready, exp_ready, att_ready, att_turned, attT_ready, av_done = (
            sem(n) for n in ("scores_done", "peak_ready", "exp_ready", "att_ready", "att_turned", "attT_ready", "av_done"))
        osq, ovar, oroot, o_ready, o_turned, oT_ready, wo_done = (
            sem(n) for n in ("osq", "ovar", "oroot", "o_ready", "o_turned", "oT_ready", "wo_done"))
        final_ready = sem("final_ready")

        win = [ring[:, u, :].rearrange("p (k n) -> p k n", k=KD) for u in range(UNITS)]
        gu = [ring[:, u, :].rearrange("p (e g k f) -> p e g k f", e=QE, g=2, k=2) for u in range(4)]
        dn = [[v.rearrange("p (e n) -> p e n", e=QE) for v in place]
              for place in ([ring[:, 4, :], ring[:, 5, :]], [part(10208, UNIT), part(10208 + UNIT, UNIT)])]

        def down_at(l, odd):
            place = 1 - (l + odd) % 2
            return dn[place], landed[4 + 2 * place:6 + 2 * place], place

        def qround(l, q):
            return l * (NQ + 1) + 1 + q

        MOST = 2 * MAXPASS * NQ

        def passes_of(eng, l, q):
            return (eng.value_load(cum[l][0:1, bass.ds(q + NQ, 1)], min_val=0, max_val=MOST),
                    eng.value_load(cum[l][0:1, bass.ds(q, 1)], min_val=1, max_val=MAXPASS))

        def passes_through(eng, l):
            return eng.value_load(cum[l][0:1, 2 * NQ:2 * NQ + 1], min_val=0, max_val=MOST)

        def stack(copy, half, n):
            quad, j = n // 4, n % 4
            ups = ps[:, 2 * half:2 * half + 2, :].rearrange("p b n -> p (b n)").rearrange("p (c m s) -> p c m s", c=KD // 2, s=SB)
            dst = U4[32 * j:32 * j + 32, :, :].rearrange("p (c a) m -> p c a m", a=4)[:, 4 * half:4 * half + 4, quad, :]
            return copy(dst, ups[32 * quad:32 * quad + 32, :, :, SB - 1 - j])

        def table_of(o):
            pr = slice(OCT * o, OCT * o + OCT)
            high = lambda i: spread(turns8[:, i, :, pr].rearrange("p n r -> p r n"), 3, 8)
            low = lambda i: spread(turns[:, i, 0:8, pr].rearrange("p n r -> p r n"), 2, 8)
            place = lambda i: table[:, i, pr, :].rearrange("p r (h l) -> p r h l", h=8)
            return high, low, place

        block = ctx.enter_context(nc.Block())

        @block.sync
        def _(sp):
            sp.dma_start(x[:], a["x"].rearrange("b (a p) d -> p (b a) d", p=P)).then_inc(s_x, 16)
            sp.dma_start(con[:], a["con"]).then_inc(s_con, 16)

            def columns(u, w, c0, kp):
                src = w.rearrange("(p k) n -> p k n" if kp else "(k p) n -> p k n", k=KD)
                for half in range(2):
                    sp.dma_start(win[u][:, 4 * half:4 * half + 4, :],
                                 src[:, 4 * half:4 * half + 4, c0:c0 + 512]).then_inc(landed[u], 16)

            sp.dma_start(gains[:, 0, :], a["norm_mix_g"][0].partition_broadcast(P)).then_inc(s_gain0, 16)
            columns(0, a["ssm_w_in"][0], 0, True)
            for i, n in enumerate(("re", "im")):
                sp.dma_start(Bn[:, i, :, :], a["ssm_b_" + n][0].rearrange("(r g) p h -> (g p) r h", g=2)).then_inc(s_bc, 16)
                sp.dma_start(Cn[:, i, :, :], a["ssm_c_" + n][0].rearrange("(c g) h p -> (g h) c p", g=8)).then_inc(s_bc, 16)
            columns(1, a["ssm_w_in"][0], 512, True)
            for l in range(2):
                sp.dma_start(wr[:, l, :, 0:NG], a["moe_w_router_group"][l].rearrange("(p k) n -> p k n", k=KD)).then_inc(s_router, 16)
                sp.dma_start(wr[:, l, :, NG:], a["moe_w_router_expert"][l].rearrange("(p k) g e -> p k (g e)", k=KD)).then_inc(s_router, 16)
                sp.dma_start(rb[:, l, 0:NG], a["moe_b_router_group"][l].partition_broadcast(P)).then_inc(s_router, 16)
                sp.dma_start(rb[:, l, NG:], a["moe_b_router_expert"][l].rearrange("g e -> (g e)").partition_broadcast(P)).then_inc(s_router, 16)
            def experts(name, l, q):
                w = a[name][l].rearrange("g e r c -> (g e) (r c)")
                return w[bass.ds(q * QE, QE), :]

            def gate_up(l, q, u):
                for g, name in enumerate(("moe_w_gate", "moe_w_up")):
                    src = experts(name, l, q).rearrange("e (p n) -> p e n", p=P)[:, :, 512 * u:512 * u + 512]
                    sp.dma_start(gu[u][:, :, g, :, :].rearrange("p e k f -> p e (k f)"), src).then_inc(landed[u], 16)

            def down(l, q, odd, u):
                dst, here, _ = down_at(l, odd)
                src = experts("moe_w_down", l, q).rearrange("e (k p n) -> p k e n", k=2, p=P)
                for half in range(2):
                    sp.dma_start(dst[u][:, 2 * half:2 * half + 2, :],
                                 src[:, u, 2 * half:2 * half + 2, :]).then_inc(here[u], 16)

            def gate_ups(l, q):
                before_q, _ = passes_of(sp, l, q)
                for u in range(4):
                    sp.wait_ge(used[u], 1 + before_q)
                    gate_up(l, q, u)

            for u in range(2):
                sp.wait_ge(used[u], 1)
                gate_up(0, 0, u)
            sp.wait_ge(v_done, 8)
            sp.wait_ge(w1T_ready, 16)
            sp.wait_ge(k_done, 4)
            columns(3, a["ssm_w_glu"][0], 512, False)
            sp.wait_ge(state, 3)
            sp.wait_ge(last_state, 1)
            for u in (2, 4, 5):
                columns(u, a["ssm_w_glu"][0], 512 * (u - 2), False)

            for l in range(2):
                if l == 0:
                    sp.wait_ge(y_done, PAIRS)
                    for u in range(2):
                        down(0, 0, 0, u)
                    for u in range(2, 4):
                        sp.wait_ge(used[u], 1)
                        gate_up(0, 0, u)
                    for u in range(2):
                        sp.wait_ge(used[4 + u], 1)
                        down(0, 1, 1, u)
                else:
                    for u in range(4):
                        sp.wait_ge(qkv_done, 7 + u)
                        gate_up(1, 0, u)
                    for u in range(2):
                        sp.wait_ge(qkv_done, 11 + u)
                        down(1, 0, 0, u)
                    sp.wait_ge(wo_done, 4)
                    for u in range(2):
                        down(1, 1, 1, u)
                sp.wait_ge(cum_ready, l + 1)
                gate_ups(l, 1)
                with sp.Fori(1, NQ // 2) as h:
                    for odd in range(2):
                        q = 2 * h + odd
                        through, _ = passes_of(sp, l, q - 1)
                        gate_first = l == 0 and odd == 1
                        if gate_first:
                            gate_ups(l, q)
                        sp.wait_ge(down_done, through + 1)
                        for u in range(2):
                            down(l, q, odd, u)
                        if not gate_first:
                            gate_ups(l, q)
                if l == 0:
                    total = passes_through(sp, 0)
                    for u in range(UNITS):
                        if u < 4:
                            sp.wait_ge(used[u], total + 1)
                        elif u == 4:
                            sp.wait_ge(down_done, total + 1)
                            sp.wait_ge(s_att, 80)
                        columns(u, a["attn_w_qkv"][0], 512 * u, True)
                    sp.dma_start(wo, a["attn_w_o"][0].rearrange("(k p) n -> p k n", p=P)).then_inc(s_wo, 16)
            for tt in range(TT):
                sp.wait_ge(final_ready, tt + 1)
                sp.dma_start(out[0, tt * P:(tt + 1) * P, :], xr[:, tt, :, :].rearrange("p k q -> p (k q)")).then_inc(out_done, 16)
            sp.wait_ge(out_done, 32)

        @block.gpsimd
        def _(pool):
            def gain(i, src):
                pool.dma_start(gains[:, i % 2, :], src.partition_broadcast(P)).then_inc(s_gain, 16)

            def pool_link(ins, n):
                ins.then_inc(pstep, 1)
                pool.wait_ge(pstep, n)

            pool.memset(part(0, 12288), 0.0).then_inc(cleared, 1)
            pool.memset(pre[:, 8192:10240], 0.0).then_inc(cleared, 1)
            pool.memset(pre[:, 0:2048], 0.0).then_inc(cleared, 1)
            pool.wait_ge(cleared, 3)
            pool.wait_ge(hT_psum, 1)
            pool.wait_ge(pow_ready, 1)
            pool.wait_ge(c_ready, 2)
            for v in decay:
                pool.memset(v.rearrange("p (r m) -> p r m", r=OCT)[:, :, 0:1], 0.0).then_inc(cleared, 1)
            v4 = lambda v: v.rearrange("p (r j c) -> p r j c", r=OCT, j=SB)
            v8 = lambda v: v.rearrange("p (r h l) -> p r h l", r=OCT, h=8)
            n = 0
            for o in range(PAIRS // OCT):
                pr = slice(OCT * o, OCT * o + OCT)
                pw = lambda i: spread(Pw[:, i, 1:5, pr].rearrange("p j r -> p r j"), 3, 16)
                cc = lambda i: spread(Cc[:, i, pr, :], 2, SB)
                for i in range(2):
                    pool.tensor_tensor(v4(t3), pw(0 if i == 0 else 2), cc(0), ALU.mult).then_inc(pstep, 1)
                    pool_link(pool.tensor_tensor(v4(t4), pw(1 if i == 0 else 0), cc(1), ALU.mult), n + 2)
                    for g in range(2):
                        h = slice(64 * g, 64 * g + 64)
                        dst = W2[h, i, pr, :].rearrange("p r (s c) -> p r s c", s=SB)[:, :, :, 16 * g:16 * g + 16]
                        ins = pool.tensor_tensor(dst, v4(t3)[h], v4(t4)[h], ALU.subtract)
                        if g == 0:
                            ins.then_inc(pstep, 1)
                    pool_link(ins, n + 4)
                    n += 4
                pool.sem_inc(w2_ready, 1)
                if o >= 2:
                    pool.wait_ge(turns_ready, 1)
                    high, low, place = table_of(o)
                    for i, op in enumerate((ALU.subtract, ALU.add)):
                        pool.tensor_tensor(v8(t3), high(0), low(i), ALU.mult).then_inc(pstep, 1)
                        pool_link(pool.tensor_tensor(v8(t4), high(1), low(1 - i), ALU.mult), n + 2)
                        pool_link(pool.tensor_tensor(place(i), v8(t3), v8(t4), op), n + 3)
                        n += 3
                    pool.sem_inc(table_ready, 1)
            full = hT[:].rearrange("p k t -> p (k t)").rearrange("p (n r m) -> p n r m", n=4, r=OCT)[:, :, :, 1:M]
            pool.wait_ge(u_done, 8)
            for o in range(3):
                pr = slice(OCT * o, OCT * o + OCT)
                z = X[:, o, :, :, 1:M]
                sin = table[:, 1, pr, 1:M]
                pool.wait_ge(scanned, o + 1)
                pool.tensor_tensor(full[:, 0:2], z, spread(table[:, 0, pr, 1:M], 1, 2), ALU.mult).then_inc(pstep, 1)
                pool.tensor_tensor(full[:, 2], z[:, 1], sin, ALU.mult).then_inc(pstep, 1)
                pool_link(pool.tensor_tensor(full[:, 3], z[:, 0], sin, ALU.mult), n + 3)
                pool.tensor_tensor(z[:, 0], full[:, 0], full[:, 2], ALU.subtract).then_inc(pstep, 1)
                pool_link(pool.tensor_tensor(z[:, 1], full[:, 1], full[:, 3], ALU.add), n + 5)
                n += 5
                pool.sem_inc(state, 1)
            pool.wait_ge(y_done, PAIRS)
            gain(1, a["norm_ffn_g"][0])

            def split(l):
                for i in range(2):
                    pool.wait_ge(part_ready, 3 * l + i + 1)
                    pool.tensor_tensor(xr[:], xr[:], parts[i], ALU.subtract).then_inc(rest_ready, 1)

            split(0)
            for i, g in ((2, a["norm_mix_g"][1]), (3, a["norm_ffn_g"][1]), (4, a["final_norm_g"])):
                pool.wait_ge(s_gain, 16 * (i - 1))
                pool.wait_ge(normed, 2 * (i - 1))
                if i == 4:
                    pool.wait_ge(mixed, 8)
                gain(i, g)
            split(1)
            pool.wait_ge(s_gain, 64)

        @block.scalar
        def _(act):
            def dma(dst, src, s):
                act.dma_start(dst, src).then_inc(s, 16)

            dma(lam[:, 0, :], a["ssm_lam_re"][0].rearrange("(r g) p -> r (g p)", g=2), s_lam)
            dma(lam[:, 1, :], a["ssm_lam_im"][0].rearrange("(r g) p -> r (g p)", g=2), s_lam)
            dma(small[0:32, 0:2], a["ssm_log_dt"][0].rearrange("(r g) -> r g", g=2), s_lam)
            dma(drep[0:8, :], a["ssm_d"][0].rearrange("(c p) -> c p", p=P), s_lam)

            def norm(i, added, first, both):
                if i > 0:
                    act.activation(small[:, 40:41], con[:, C_TURN:C_TURN + 1], ACT.Sqrt)
                for tt in range(TT):
                    act.wait_ge(added, both if tt else first)
                    act.activation(xr[:, tt, :, :].rearrange("p k q -> p (k q)"), x[:, tt, :], ACT.Square,
                                   accum_out=small[:, 8 + tt:9 + tt]).then_inc(squares, 1)
                act.wait_ge(var_ready, i + 1)
                act.activation(small[:, 12:14], small[:, 10:12], ACT.Sqrt).then_inc(root_ready, 1)
                if i < 4:
                    act.wait_ge(hT_psum, i + 1)
                    for b in range(4):
                        act.copy(hT[:, 2 * b:2 * b + 2, :].rearrange("p k t -> p (k t)"), ps[:, b, :]).then_inc(hT_ready, 1)

            norm(0, s_x, 16, 16)
            act.wait_ge(s_con, 16)
            act.wait_ge(s_lam, 64)
            act.activation(small[0:32, 2:4], small[0:32, 0:2], ACT.Exp).then_inc(dt_ready, 1)
            act.wait_ge(er_ready, 1)
            act.activation(lam[:, 4, :], lam[:, 2, :], ACT.Exp).then_inc(sin_ready, 1)
            act.wait_ge(arg_ready, 1)
            act.activation(lam[:, 5, :], lam[:, 5, :], ACT.Sin).then_inc(sin_ready, 1)
            act.activation(lam[:, 6, :], lam[:, 6, :], ACT.Sin).then_inc(sin_ready, 1)
            act.wait_ge(c_psum, 1)
            for i in range(2):
                act.copy(Cc[:, i, :, :].rearrange("p r c -> p (r c)"), ps[:, 4 + i, :]).then_inc(c_ready, 1)

            act.wait_ge(lam_psum, 8)
            for o in range(PAIRS // OCT):
                act.copy(decay[o].rearrange("p (r m) -> p r m", r=OCT)[:, :, 1:M],
                         spread(ps[:, 7, OCT * o:OCT * o + OCT], 2, M - 1)).then_inc(decay_ready, 1)

            def first(o):
                for i in range(2):
                    for g in range(2):
                        h = slice(64 * g, 64 * g + 64)
                        act.copy(W1[h, i, :, 0, 16 * g:16 * g + 16], Bb[h, i, OCT * o:OCT * o + OCT, :]).then_inc(w1_first, 1)

            def own(half):
                act.wait_ge(k_ready, half + 1)
                for j in range(SB):
                    for r in range(4):
                        kps = ps[32 * r:32 * r + 32, 6 + half, :].rearrange("p (q n) -> p q n", q=KD // 2)
                        dst = Fw[32 * j:32 * j + 32, 16 * half:16 * half + 16, :].rearrange("p (q a) n -> p q a n", a=4)
                        act.copy(dst[:, :, r, 32 * (3 - j):P], kps[:, :, 0:32 * (j + 1)]).then_inc(f_ready, 1)

            act.wait_ge(u_done, 4)
            act.wait_ge(normed, 2)
            for n in range(16):
                stack(act.copy, 0, n).then_inc(u4_ready, 1)
            act.wait_ge(bbar_ready, 1)
            act.wait_ge(cleared, 3)
            first(0)
            act.wait_ge(u_done, 8)
            for n in range(16):
                stack(act.copy, 1, n).then_inc(u4_ready, 1)
            for o in range(PAIRS // OCT):
                act.wait_ge(w1_turned, o + 1)
                if o >= 1:
                    act.wait_ge(v_done, 2 * o)
                for b in (0, 2, 1, 3):
                    act.copy(W1T[:, b // 2, 4 * (b % 2):4 * (b % 2) + 4, :].rearrange("p r c -> p (r c)"),
                             ps[:, b, :]).then_inc(w1T_ready, 1)
                if o + 1 < PAIRS // OCT:
                    act.wait_ge(k_done, o + 1)
                    first(o + 1)
                if o >= 2:
                    own(o - 2)
            act.wait_ge(table_ready, 4)
            for b in range(4):
                act.wait_ge(y_done, 8 * b + 8)
                for n in range(16):
                    quad, s = n // 4, n % 4
                    src = ps[32 * s:32 * s + 32, b, :].rearrange("p (c a m) -> p c a m", c=2, a=4)[:, :, quad, :]
                    dst = gT[32 * quad:32 * quad + 32, 2 * b:2 * b + 2, :].rearrange("p c (m s) -> p c m s", s=SB)[:, :, :, s]
                    act.activation(dst, src, ACT.Gelu_apprx_tanh).then_inc(g_ready, 1)
            for n in range(4):
                act.wait_ge(glu_done, n + 1)
                if n >= 1:
                    act.wait_ge(mixed, n)
                act.activation(sig[:, 0, :], ps[:, 5 + 2 * (n % 2), :], ACT.Sigmoid).then_inc(sig_ready, 1)

            def moe(l):
                act.wait_ge(logits_turned, l + 1)
                act.copy(lgT[0:NG + E, :], ps[0:NG + E, 4, 0:T]).then_inc(logits_kept, 1)
                act.copy(parts[0], xr[:]).then_inc(part_ready, 1)
                act.wait_ge(gate_sub, 2 * l + 1)
                act.activation(rt[:, 8:16], rt[:, 8:16], ACT.Exp).then_inc(gate_exp, 1)
                act.wait_ge(gate_sub, 2 * l + 2)
                act.activation(rt[:, 128:144], rt[:, 128:144], ACT.Exp).then_inc(gate_exp, 1)
                for i in range(2):
                    act.wait_ge(rest_ready, 2 * l + i + 1)
                    act.copy(parts[i + 1], xr[:]).then_inc(part_ready, 1)
                act.wait_ge(cum_ready, l + 1)
                with act.Fori(0, NQ) as q:
                    n0, passes = passes_of(act, l, q)
                    with act.Fori(0, passes) as p:
                        n = n0 + p
                        act.wait_ge(sw_turned, n + 1)
                        act.copy(kept[:, bass.ds(p, 1), 256:512].rearrange("p n c -> p (n c)"), ps[:, 3, 0:256]).then_inc(sw_ready, 1)
                        act.wait_ge(gathered, 2 * n + 2)
                        act.copy(xg[:, 4:8, :].rearrange("p k s -> p (k s)"), ps[:, 1, :]).then_inc(xg_ready, 1)
                        act.wait_ge(gu_done, n + 1)
                        act.activation(sil, ps[:, 2, 0:256], ACT.Silu).then_inc(sil_ready, 1)
                    with act.Fori(0, passes) as p:
                        n = n0 + p
                        act.wait_ge(sw_ready, n + 1)
                        act.wait_ge(scattered, 2 * n + 1)
                        act.copy(swT, kept[:, bass.ds(p, 1), 256:512].rearrange("p n c -> p (n c)")).then_inc(back_ready, 1)
                        act.wait_ge(down_done, n + 2)
                        act.copy(yy[:, 0:512], ps[:, 4, :]).then_inc(y_ready, 1)
                total = passes_through(act, l)
                return total

            norm(1, mixed, 2, 4)
            total = moe(0)
            for n, name in enumerate(("q1", "k1", "q2", "k2")):
                dma(lam4[:, n, :], a["attn_lambda_" + name][0].partition_broadcast(P), s_att)
            dma(subg, a["attn_subln_g"][0].partition_broadcast(P), s_att)
            norm(2, x_added, 2 * total + 1, 2 * total + 2)
            act.wait_ge(lam_sum, 1)
            act.activation(asm[:, 2:4], asm[:, 0:2], ACT.Exp).then_inc(lam_exp, 1)
            def keep_v(tt):
                for c in range(4, 6):
                    act.wait_ge(qkv_done, 6 * tt + c + 1)
                    act.copy(vv[:, tt, 512 * c - 2048:512 * c - 1536], ps[:, c if tt == 0 else c % 2, :]).then_inc(v_kept, 1)

            def keep_qk(tt, c):
                act.wait_ge(qk_turned, 4 * tt + c + 1)
                act.copy(qk[:, 4 * c:4 * c + 4, tt * P:(tt + 1) * P],
                         ps[:, (6 if tt == 0 else 2) + c % 2, :].rearrange("p (h t) -> p h t", h=4)).then_inc(qkT_ready, 1)

            def soft(g):
                b, _, heads, sbank, _, _, _ = groups[g]
                keys = P * (b + 1)
                row = soft_row[:, g % 2, :]
                act.wait_ge(peak_ready, g + 1)
                if g >= 2:
                    act.wait_ge(att_ready, g - 1)
                for j in range(2):
                    for h in range(heads):
                        n = heads * j + h
                        act.activation(Pb[:, g % 2, j, keys * h:keys * h + keys], ps[:, sbank + j, keys * h:keys * h + keys],
                                       ACT.Exp, bias=row[:, 8 + n:9 + n], scale=DH ** -0.5,
                                       accum_out=row[:, 16 + n:17 + n]).then_inc(exp_ready, 1)

            def keep_att(g):
                act.wait_ge(att_turned, g + 1)
                if g >= 2:
                    act.wait_ge(av_done, g - 1)
                act.copy(atT[:, g % 2, :], ps[:, groups[g][4], :]).then_inc(attT_ready, 1)

            def keep_o(n):
                act.wait_ge(av_done, (1, 2, 4, 6)[n])
                act.copy(osb[n // 2][:, 512 * (n % 2):512 * (n % 2) + 512], ps[:, (7, 7, 6, 7)[n], :]).then_inc(osq, 1)

            def root_o(b):
                act.wait_ge(ovar, b + 1)
                act.activation(asm[:, 32 + 8 * b:40 + 8 * b], asm[:, 16 + 8 * b:24 + 8 * b], ACT.Sqrt).then_inc(oroot, 1)

            def keep_oT(b, c, bank):
                act.wait_ge(o_turned, 2 * b + c + 1)
                act.copy(oT[:, 4 * c:4 * c + 4, b * P:(b + 1) * P],
                         ps[:, bank, :].rearrange("p (h t) -> p h t", h=4)).then_inc(oT_ready, 1)

            for c in range(4):
                keep_qk(0, c)
            keep_v(0)
            soft(0)
            soft(1)
            keep_att(0)
            keep_o(0)
            keep_qk(1, 0)
            keep_att(1)
            keep_o(1)
            for c in range(1, 4):
                keep_qk(1, c)
            root_o(0)
            keep_v(1)
            soft(2)
            soft(3)
            keep_att(2)
            keep_oT(0, 0, 5)
            soft(4)
            keep_att(3)
            keep_oT(0, 1, 5)
            keep_o(2)
            soft(5)
            keep_att(4)
            keep_att(5)
            keep_o(3)
            root_o(1)
            keep_oT(1, 0, 4)
            keep_oT(1, 1, 5)
            norm(3, mixed, 8, 8)
            total = moe(1)
            norm(4, x_added, 2 * total + 1, 2 * total + 2)

        @block.vector
        def _(dve):
            count = [0]

            def link(ins):
                count[0] += 1
                ins.then_inc(dstep, 1)
                dve.wait_ge(dstep, count[0])

            TTo, TS, STT, RED = dve.tensor_tensor, dve.tensor_scalar, dve.scalar_tensor_tensor, dve.tensor_reduce

            def norm(i):
                dve.wait_ge(squares, 2 * i + 2)
                TS(small[:, 10:12], small[:, 8:10], 1.0 / D, EPS, ALU.mult, ALU.add).then_inc(var_ready, 1)
                dve.wait_ge(root_ready, i + 1)
                link(dve.reciprocal(small[:, 14:16], small[:, 12:14]))
                if i == 0:
                    dve.wait_ge(s_gain0, 16)
                else:
                    dve.wait_ge(s_gain, 16 * i)
                for tt in range(TT):
                    if i < 4:
                        STT(xr[:, tt, :, :], x[:, tt, :].rearrange("p (q k) -> p k q", k=KD), small[:, 14 + tt:15 + tt],
                            gains[:, i % 2, :].rearrange("p (q k) -> p k q", k=KD), ALU.mult, ALU.mult).then_inc(normed, 1)
                    else:
                        STT(xr[:, tt, :, :].rearrange("p k q -> p (k q)"), x[:, tt, :], small[:, 14 + tt:15 + tt],
                            gains[:, i % 2, :], ALU.mult, ALU.mult).then_inc(final_ready, 1)

            for first in (x_added, x_added, y_ready, sel_ready, hidT_kept):
                dve.sem_inc(first, 1)
            norm(0)
            L = lambda n: lam[:, n, :]
            V = lambda n: lam2[:, n, :]
            dve.wait_ge(dt_ready, 1)
            dtb = spread(small[0:32, 2:4], 2, 64)
            two = lambda v: v.rearrange("p (g c) -> p g c", g=2)
            TTo(two(L(2)), two(L(0)), dtb, ALU.mult).then_inc(er_ready, 1)
            link(TTo(two(L(3)), two(L(1)), dtb, ALU.mult))
            MAGIC = 1.5 * 2.0 ** 23
            link(TS(V(0), L(3), 1.0 / (2 * math.pi), MAGIC, ALU.mult, ALU.add))
            link(TS(V(0), V(0), -MAGIC, None, ALU.add))
            C1 = 6.28125
            C2 = float(np.float32(np.round((2 * math.pi - C1) * 2.0 ** 22) / 2.0 ** 22))
            C3 = 2 * math.pi - C1 - C2
            link(STT(V(1), V(0), -C1, L(3), ALU.mult, ALU.add))
            link(STT(V(1), V(0), -C2, V(1), ALU.mult, ALU.add))
            link(STT(V(1), V(0), -C3, V(1), ALU.mult, ALU.add))
            PI_IN = 3.1415925
            link(TS(L(6), V(1), PI_IN, -PI_IN, ALU.min, ALU.max))
            link(STT(V(2), L(6), -1.0, L(6), ALU.mult, ALU.max))
            link(TS(L(5), V(2), -1.0, math.pi / 2, ALU.mult, ALU.add))
            dve.sem_inc(arg_ready, 1)
            link(TTo(V(0), L(0), L(0), ALU.mult))
            link(TTo(V(1), L(1), L(1), ALU.mult))
            link(TTo(V(0), V(0), V(1), ALU.add))
            link(dve.reciprocal(V(0), V(0)))
            dve.wait_ge(sin_ready, 3)
            link(TTo(V(1), L(4), L(5), ALU.mult))
            link(TTo(V(2), L(4), L(6), ALU.mult))
            link(TS(V(3), V(1), -1.0, None, ALU.add))
            link(TTo(V(4), V(3), L(0), ALU.mult))
            link(TTo(V(5), V(2), L(1), ALU.mult))
            link(TTo(V(4), V(4), V(5), ALU.add))
            link(TTo(V(5), V(2), L(0), ALU.mult))
            link(TTo(V(6), V(3), L(1), ALU.mult))
            link(TTo(V(5), V(5), V(6), ALU.subtract))
            link(TTo(V(3), V(4), V(0), ALU.mult))
            link(TTo(V(4), V(5), V(0), ALU.mult))
            link(TTo(V(7), L(4), L(4), ALU.mult))
            link(TTo(V(7), V(7), V(7), ALU.mult))
            dve.sem_inc(lam_ready, 1)
            dve.wait_ge(lam_psum, 8)
            TP = ps[:, 6, 0:192].rearrange("p (n r) -> p n r", n=6)
            dve.memset(Pw[:, 0, 0, :], 1.0)
            dve.memset(Pw[:, 1:3, 0, :], 0.0)
            dve.memset(turns[:, 0, 0, :], 1.0)
            dve.memset(turns[:, 1, 0, :], 0.0)
            dve.memset(turns8[:, 0, 0, :], 1.0)
            dve.memset(turns8[:, 1, 0, :], 0.0)
            dve.memset(X[:].rearrange("p o i r m -> p (o i r) m")[:, :, 0:1], 0.0)
            dve.tensor_copy(Pw[:, 0, 1, :], TP[:, 0, :])
            dve.tensor_copy(Pw[:, 1, 1, :], TP[:, 1, :])
            dve.tensor_copy(turns2[:, :, 0, :], TP[:, 4:6, :])
            dve.tensor_copy(sc2[:], TP[:, 2:4, :])
            link(dve.tensor_copy(dcol, ps[:, 6, 192:200]))
            TTo(skip, spread(con[:, C_SKIP:C_SKIP + PC], 1, KD), spread(dcol, 2, PC), ALU.mult)

            def cmul(dst, n, v, w):
                s = [t1[:, 128 * k:128 * k + 32 * n].rearrange("p (n r) -> p n r", n=n) for k in range(4)]
                TTo(s[0], v(0), w(0), ALU.mult)
                TTo(s[1], v(1), w(1), ALU.mult)
                TTo(s[2], v(0), w(1), ALU.mult)
                link(TTo(s[3], v(1), w(0), ALU.mult))
                TTo(dst(0), s[0], s[1], ALU.subtract)
                link(TTo(dst(1), s[2], s[3], ALU.add))

            def powers(table, lo, n, by, base):
                cmul(lambda i: table[:, i, lo:lo + n, :], n,
                     lambda i: table[:, i, base:base + n, :], lambda i: spread(table[:, i, by, :], 1, n))

            def to_one(table, n):
                s = [t[:, 0:32 * n].rearrange("p (n r) -> p n r", n=n) for t in (t1, t2)]
                v = [table[:, i, 1:n + 1, :] for i in range(2)]
                TTo(s[0], v[0], v[0], ALU.mult)
                link(TTo(s[1], v[1], v[1], ALU.mult))
                link(TTo(s[0], s[0], s[1], ALU.add))
                link(TS(s[0], s[0], -0.5, 1.5, ALU.mult, ALU.add))
                TTo(v[0], v[0], s[0], ALU.mult)
                link(TTo(v[1], v[1], s[0], ALU.mult))

            powers(Pw, 2, 1, 1, 1)
            powers(Pw, 3, 2, 2, 1)
            link(TS(Pw[:, 2, 1:5, :], Pw[:, 1, 1:5, :], -1.0, None, ALU.mult))
            dve.sem_inc(pow_ready, 1)
            dve.wait_ge(s_bc, 64)
            r16 = lambda v: v.rearrange("p (r c) -> p r c", r=PAIRS)
            for i in range(2):
                TTo(r16(t1), Bn[:, i, :, :], spread(sc2[:, 0, :], 2, 16), ALU.mult)
                link(TTo(r16(t2), Bn[:, 1 - i, :, :], spread(sc2[:, 1, :], 2, 16), ALU.mult))
                link(TTo(Bb[:, i, :, :], r16(t1), r16(t2), ALU.add if i else ALU.subtract))
            dve.sem_inc(bbar_ready, 1)
            dve.wait_ge(c_ready, 2)
            dve.wait_ge(cleared, 3)
            for g in range(2):
                h = slice(64 * g, 64 * g + 64)
                dve.tensor_copy(Cb[h, 0, :, 16 * g:16 * g + 16], Cc[h, 0, :, :])
                link(TS(Cb[h, 1, :, 16 * g:16 * g + 16], Cc[h, 1, :, :], -1.0, None, ALU.mult))
            v3 = lambda v: v[:, 0:OCT * 48].rearrange("p (r j c) -> p r j c", r=OCT, j=3)

            def weights(o):
                pr = slice(OCT * o, OCT * o + OCT)
                pw = lambda i: spread(Pw[:, i, 1:4, pr].rearrange("p j r -> p r j"), 3, 16)
                bb = lambda i: spread(Bb[:, i, pr, :], 2, 3)
                if o >= 1:
                    dve.wait_ge(w1_turned, o)
                for i in range(2):
                    TTo(v3(t1), pw(0), bb(i), ALU.mult)
                    link(TTo(v3(t2), pw(1), bb(1 - i), ALU.mult))
                    for g in range(2):
                        h = slice(64 * g, 64 * g + 64)
                        ins = TTo(W1[h, i, :, 1:4, 16 * g:16 * g + 16], v3(t1)[h], v3(t2)[h], ALU.add if i else ALU.subtract)
                        if g == 0:
                            ins.then_inc(dstep, 1)
                            count[0] += 1
                    link(ins)
                dve.sem_inc(w1_ready, 1)

            weights(0)
            cmul(lambda i: turns2[:, i, 1:2, :], 1, lambda i: turns2[:, i, 0:1, :], lambda i: turns2[:, i, 0:1, :])
            cmul(lambda i: turns[:, i, 1:2, :], 1, lambda i: turns2[:, i, 1:2, :], lambda i: turns2[:, i, 1:2, :])
            to_one(turns, 1)
            powers(turns, 2, 1, 1, 1)
            powers(turns, 3, 2, 2, 1)
            powers(turns, 5, 4, 4, 1)
            to_one(turns, 8)
            dve.tensor_copy(turns8[:, 0, 1, :], turns[:, 0, 8, :])
            link(dve.tensor_copy(turns8[:, 1, 1, :], turns[:, 1, 8, :]))
            powers(turns8, 2, 1, 1, 1)
            powers(turns8, 3, 2, 2, 1)
            powers(turns8, 5, 3, 4, 1)
            to_one(turns8, 7)
            dve.sem_inc(turns_ready, 1)
            v8 = lambda v: v.rearrange("p (r h l) -> p r h l", r=OCT, h=8)
            def tabulate(o):
                high, low, place = table_of(o)
                for i, op in enumerate((ALU.subtract, ALU.add)):
                    TTo(v8(t1), high(0), low(i), ALU.mult)
                    link(TTo(v8(t2), high(1), low(1 - i), ALU.mult))
                    link(TTo(place(i), v8(t1), v8(t2), op))
                dve.sem_inc(table_ready, 1)

            def states(o):
                pr = slice(OCT * o, OCT * o + OCT)
                dve.wait_ge(v_done, 2 * o + 2)
                dve.wait_ge(table_ready, 4 if o >= 2 else 2)
                v = ps[:, 4:6, :].rearrange("p b n -> p (b n)").rearrange("p (r i m) -> p i r m", r=OCT, i=2)[:, :, :, 0:M - 1]
                z = X[:, o, :, :, 1:M]
                cos = spread(table[:, 0, pr, 1:M], 1, 2)
                sin = table[:, 1, pr, 1:M]
                r1, r2 = (b.rearrange("p (i r m) -> p i r m", i=2, r=OCT)[:, :, :, 1:M] for b in (rot1, rot2))
                TTo(z, v, cos, ALU.mult)
                TTo(r1[:, 0], v[:, 1], sin, ALU.mult)
                link(TTo(r1[:, 1], v[:, 0], sin, ALU.mult))
                dve.sem_inc(v_ready, 1)
                TTo(z[:, 0], z[:, 0], r1[:, 0], ALU.add)
                link(TTo(z[:, 1], z[:, 1], r1[:, 1], ALU.subtract))
                if o == 0:
                    dve.wait_ge(decay_ready, 4)
                    dve.wait_ge(cleared, 7)
                for i in range(2):
                    lane = X[:, o, i, :, :].rearrange("p r m -> p (r m)")
                    ins = dve.tensor_tensor_scan(lane, decay[o], lane, 0.0, ALU.mult, ALU.add)
                    if i == 0:
                        ins.then_inc(dstep, 1)
                        count[0] += 1
                link(ins)
                if o < 3:
                    dve.sem_inc(scanned, 1)
                    return
                TTo(r2, z, cos, ALU.mult)
                TTo(r1[:, 0], z[:, 1], sin, ALU.mult)
                link(TTo(r1[:, 1], z[:, 0], sin, ALU.mult))
                TTo(z[:, 0], r2[:, 0], r1[:, 0], ALU.subtract)
                link(TTo(z[:, 1], r2[:, 1], r1[:, 1], ALU.add))
                dve.sem_inc(last_state, 1)

            def skips(half):
                dve.wait_ge(k_done, 2 * half + 2)
                taps = ps[:, 6 + half, :].rearrange("p (q n) -> p q n", q=KD // 2)[:, :, 0:PC]
                TTo(taps, taps, skip[:, 4 * half:4 * half + 4, :], ALU.add).then_inc(k_ready, 1)

            tabulate(0)
            for o in range(3):
                weights(o + 1)
                if o == 0:
                    tabulate(1)
                states(o)
                if o >= 1:
                    skips(o - 1)
            states(3)
            for n in range(4):
                tt, c = n // 2, n % 2
                dve.wait_ge(sig_ready, n + 1)
                link(TTo(sig[:, 1, :], ps[:, 4 + 2 * (n % 2), :], sig[:, 0, :], ALU.mult))
                TTo(x[:, tt, 512 * c:512 * c + 512], x[:, tt, 512 * c:512 * c + 512], sig[:, 1, :], ALU.add).then_inc(mixed, 1)

            def first_best(dst, v, n, best, tmp, least):
                link(RED(best, v, AX.X, ALU.max))
                link(TTo(tmp, v, spread(best, 2, n), ALU.is_equal))
                link(STT(tmp, tmp, -16.0, spread(con[:, C_SLOT:C_SLOT + n], 1, TT), ALU.mult, ALU.add))
                link(RED(least, tmp, AX.X, ALU.min))
                link(TTo(dst, tmp, spread(least, 2, n), ALU.is_equal))

            def moe(l):
                r = lambda off, n: rt[:, off:off + TT * n].rearrange("p (a n) -> p a n", a=TT)
                c2 = lambda off: rt[:, off:off + TT]
                r48 = lambda off: rt[:, off:off + 64].rearrange("p (a g e) -> p a g e", a=TT, g=NG)
                dve.wait_ge(s_router, 128)
                dve.wait_ge(logits_done, l + 1)
                link(dve.tensor_copy(lg, ps[:, 5, 0:72].rearrange("p (a n) -> p a n", a=TT)))
                gl, el = lg[:, :, 0:NG], lg[:, :, NG:].rearrange("p a (g e) -> p a g e", g=NG)
                link(RED(c2(0), gl, AX.X, ALU.max))
                TTo(r(8, 4), gl, spread(c2(0), 2, NG), ALU.subtract).then_inc(gate_sub, 1)
                link(TTo(r(16, 4), gl, spread(rb[:, l, 0:NG], 1, TT), ALU.add))
                first_best(r(24, 4), r(16, 4), NG, c2(2), r(32, 4), c2(4))
                goh = r(24, 4)
                gb = spread(goh, 3, NE)
                link(TTo(r48(192), el, gb, ALU.mult))
                link(RED(r(64, 8), r48(192).rearrange("p a g e -> p a e g"), AX.X, ALU.add))
                link(RED(c2(0), r(64, 8), AX.X, ALU.max))
                TTo(r(128, 8), r(64, 8), spread(c2(0), 2, NE), ALU.subtract).then_inc(gate_sub, 1)
                b48 = rb[:, l, NG:].rearrange("p (g e) -> p g e", g=NG)
                link(TTo(r48(192), spread(b48, 1, TT), gb, ALU.mult))
                link(RED(r(80, 8), r48(192).rearrange("p a g e -> p a e g"), AX.X, ALU.add))
                dve.wait_ge(gate_exp, 2 * l + 2)
                link(RED(c2(2), r(128, 8), AX.X, ALU.add))
                link(dve.reciprocal(c2(4), c2(2)))
                link(TTo(r(64, 8), r(128, 8), spread(c2(4), 2, NE), ALU.mult))
                link(TTo(r(96, 8), r(64, 8), r(80, 8), ALU.add))
                first_best(r(112, 8), r(96, 8), NE, c2(2), r(144, 8), c2(4))
                link(STT(r(96, 8), r(112, 8), NO, r(96, 8), ALU.mult, ALU.add))
                first_best(r(160, 8), r(96, 8), NE, c2(2), r(144, 8), c2(4))
                link(TTo(r(112, 8), r(112, 8), r(160, 8), ALU.add))
                gs = spread(goh, 3, NE)
                ge = lambda v: v.rearrange("p a (g e) -> p a g e", g=NG)
                link(TTo(ge(msk), gs, spread(r(112, 8), 2, NG), ALU.mult))
                dve.sem_inc(mask_ready, 1)
                dve.wait_ge(gate_exp, 2 * l + 1)
                RED(c2(40), r(8, 4), AX.X, ALU.add)
                TTo(r(64, 8), r(64, 8), r(112, 8), ALU.mult)
                link(TTo(r(32, 4), r(8, 4), goh, ALU.mult))
                dve.reciprocal(c2(42), c2(40))
                RED(c2(2), r(64, 8), AX.X, ALU.add)
                link(RED(c2(44), r(32, 4), AX.X, ALU.add))
                TTo(c2(46), c2(44), c2(42), ALU.mult)
                link(dve.reciprocal(c2(4), c2(2)))
                link(TTo(c2(4), c2(4), c2(46), ALU.mult))
                link(TTo(r(64, 8), r(64, 8), spread(c2(4), 2, NE), ALU.mult))
                link(TTo(ge(comb[:, :, 0:E]), gs, spread(r(64, 8), 2, NG), ALU.mult))
                dve.wait_ge(pos_done, l + 1)
                link(STT(slot1[:, :, 0:E], ps[:, 5, 128:192].rearrange("p (a e) -> p a e", a=TT), 1.0, msk, ALU.add, ALU.mult))
                link(RED(rt[:, 0:8], ps[:, 5, 192:224].rearrange("p (q e) -> p q e", q=NQ), AX.X, ALU.max))
                link(TTo(rt[:, 64:120].rearrange("p (q s) -> p q s", q=NQ), spread(rt[:, 0:8], 2, 7),
                         con[:, C_STEP:C_STEP + 56].rearrange("p (q s) -> p q s", q=NQ), ALU.is_gt))
                link(RED(rt[:, 8:16], rt[:, 64:120].rearrange("p (q s) -> p q s", q=NQ), AX.X, ALU.add))
                link(TS(rt[:, 8:16], rt[:, 8:16], 1.0, None, ALU.add))
                link(TTo(rt[:, 128:200].rearrange("p (q s) -> p q s", q=9), spread(rt[:, 8:16], 1, 9),
                         con[:, C_UPTO:C_UPTO + 72].rearrange("p (q s) -> p q s", q=9), ALU.mult))
                link(RED(rt[:, 16:25], rt[:, 128:200].rearrange("p (q s) -> p q s", q=9), AX.X, ALU.add))
                if l == 1:
                    link(TS(rt[:, 16:25], rt[:, 16:25], small[:, 20:21], None, ALU.add))
                link(dve.tensor_copy(cum[l][:, 0:17], rt[:, 8:25]))
                if l == 0:
                    link(dve.tensor_copy(small[:, 20:21], rt[:, 24:25]))
                dve.sem_inc(cum_ready, 1)
                sel4 = lambda v: v.rearrange("p a (e s) -> p a e s", e=QE)


                strip = lambda q: bass.ds(q * QE, QE)
                slots = lambda p: bass.ds(p * SLOTS + C_SLOT, SLOTS)

                def choose(q, p, builds):
                    for tt in range(TT):
                        TTo(sel4(sel)[:, tt], spread(slot1[:, tt, strip(q)], 2, SLOTS),
                            spread(con[:, slots(p)], 1, QE), ALU.is_equal).then_inc(sel_built, 1)
                    dve.wait_ge(sel_built, 2 * builds)
                    for tt in range(TT):
                        TTo(sel4(scw)[:, tt], sel4(sel)[:, tt],
                            spread(comb[:, tt, strip(q)], 2, SLOTS), ALU.mult).then_inc(sel_ready, 1)

                start = 0 if l == 0 else passes_through(dve, 0) + (NQ + 1) * l
                dve.wait_ge(sel_ready, 2 * start + 1)
                choose(0, 0, start + 1)
                with dve.Fori(0, NQ) as q:
                    n0, passes = passes_of(dve, l, q)
                    built = n0 + q + (NQ + 1) * l
                    with dve.Fori(0, passes) as p:
                        n = n0 + p
                        dve.wait_ge(gathered, 2 * n + 1)
                        dve.tensor_copy(xg[:, 0:4, :].rearrange("p k s -> p (k s)"), ps[:, 0, :]).then_inc(xg_ready, 1)
                        dve.wait_ge(gathered, 2 * n + 2)
                        choose(q, p + 1, built + p + 2)
                        dve.wait_ge(sil_ready, n + 1)
                        TTo(hid, ps[:, 2, 256:512], sil, ALU.mult).then_inc(hid_ready, 1)
                        dve.wait_ge(hid_turned, n + 1)
                        dve.tensor_copy(kept[:, bass.ds(p, 1), 0:256].rearrange("p n c -> p (n c)"), ps[:, 3, 256:512]).then_inc(hidT_kept, 1)
                    dve.wait_ge(hidT_kept, n0 + 2)
                    dve.wait_ge(down_done, n0 + 1)
                    dve.tensor_copy(hidT, kept[:, 0, 0:256]).then_inc(down_ready, 1)
                    dve.wait_ge(sel_ready, 2 * (built + passes) + 3)
                    choose(q + 1, 0, built + passes + 2)
                    with dve.Fori(0, passes) as p:
                        n = n0 + p
                        dve.wait_ge(down_done, n + 2)
                        dve.tensor_copy(yy[:, 512:1024], ps[:, 5, :]).then_inc(y_ready, 1)
                        dve.tensor_copy(hidT, kept[:, bass.ds(p + 1, 1), 0:256].rearrange("p n c -> p (n c)")).then_inc(down_ready, 1)
                        for tt in range(TT):
                            dve.wait_ge(scattered, 2 * n + 2 + tt)
                            b = 6 if tt else 0
                            TTo(x[:, tt, :], x[:, tt, :], ps[:, b:b + 2, :].rearrange("p b n -> p (b n)"), ALU.add).then_inc(x_added, 1)

            norm(1)
            moe(0)
            norm(2)
            lambda_init = 0.8 - 0.6 * math.exp(-0.3)
            dve.wait_ge(s_att, 80)
            l4 = lam4.rearrange("p (n i) c -> p n i c", i=2)
            link(TTo(rope1[:, 0:128].rearrange("p (n c) -> p n c", n=2), l4[:, :, 0, :], l4[:, :, 1, :], ALU.mult))
            RED(asm[:, 0:2], rope1[:, 0:128].rearrange("p (n c) -> p n c", n=2), AX.X, ALU.add).then_inc(lam_sum, 1)
            dve.wait_ge(lam_exp, 1)
            link(TTo(asm[:, 4:5], asm[:, 3:4], asm[:, 2:3], ALU.subtract))
            link(TS(asm[:, 4:5], asm[:, 4:5], -lambda_init, None, ALU.add))
            link(TS(subg, subg, 1.0 - lambda_init, None, ALU.mult))
            def rotate(tt, c):
                cs = con[:, C_ROPE + 128 * tt:C_ROPE + 128 * tt + 64]
                sn = con[:, C_ROPE + 128 * tt + 64:C_ROPE + 128 * tt + 128]
                i = 4 * tt + c
                dve.wait_ge(qkv_done, 6 * tt + c + 1)
                if i:
                    dve.wait_ge(qkv_kept, i)
                if i >= 2:
                    dve.wait_ge(qk_turned, i - 1)
                src = ps[:, c if tt == 0 else c % 2, :].rearrange("p (h n) -> p h n", h=8)
                ra, rc = (v.rearrange("p (h n) -> p h n", h=8) for v in (rope1, rope2))
                TTo(ra, src, spread(cs, 1, 8), ALU.mult).then_inc(dstep, 1)
                TTo(rc[:, :, 0:32], src[:, :, 32:64], spread(sn[:, 0:32], 1, 8), ALU.mult).then_inc(dstep, 1)
                count[0] += 2
                link(TTo(rc[:, :, 32:64], src[:, :, 0:32], spread(sn[:, 32:64], 1, 8), ALU.mult))
                TTo(nat[:, c % 2, :], rope1, rope2, ALU.add).then_inc(qkv_kept, 1)

            def peak(g):
                b, _, heads, sbank, _, _, _ = groups[g]
                keys = P * (b + 1)
                row = soft_row[:, g % 2, :]
                dve.wait_ge(scores_done, g + 1)
                sv = ps[:, sbank:sbank + 2, :].rearrange("p j (h n) -> p j h n", h=heads)
                for j in range(2):
                    ins = dve.memset(sv[0:CHUNK, j, :, keys - CHUNK:keys], NO)
                link(ins)
                link(RED(row[:, 0:2 * heads].rearrange("p (j h) -> p j h", j=2), sv, AX.X, ALU.max))
                TS(row[:, 8:8 + 2 * heads], row[:, 0:2 * heads], -(DH ** -0.5), None, ALU.mult).then_inc(peak_ready, 1)

            def combine(g):
                b, _, heads, _, _, _, _ = groups[g]
                keys = P * (b + 1)
                row = soft_row[:, g % 2, :]
                dve.wait_ge(exp_ready, exps[g])
                link(dve.reciprocal(row[:, 24:24 + 2 * heads], row[:, 16:16 + 2 * heads]))
                link(TS(row[:, 32:32 + heads], row[:, 24 + heads:24 + 2 * heads], asm[:, 4:5], None, ALU.mult))
                if g >= 1:
                    dve.wait_ge(att_turned, g)
                for h in range(heads):
                    k = slice(keys * h, keys * h + keys)
                    ins = TS(at[:, k], Pb[:, g % 2, 1, k], row[:, 32 + h:33 + h], None, ALU.mult)
                link(ins)
                for h in range(heads):
                    k = slice(keys * h, keys * h + keys)
                    ins = STT(at[:, k], Pb[:, g % 2, 0, k], row[:, 24 + h:25 + h], at[:, k], ALU.mult, ALU.add)
                ins.then_inc(att_ready, 1)

            def norm_o(b):
                hv = osb[b].rearrange("p (h e) -> p h e", h=H)
                sqv = osq2.rearrange("p (h e) -> p h e", h=H)
                dve.wait_ge(osq, 2 * b + 2)
                dve.wait_ge(qkv_kept, 8)
                link(TTo(sqv, hv, hv, ALU.mult))
                link(RED(asm[:, 16 + 8 * b:24 + 8 * b], sqv, AX.X, ALU.add))
                TS(asm[:, 16 + 8 * b:24 + 8 * b], asm[:, 16 + 8 * b:24 + 8 * b], 1.0 / P, EPS, ALU.mult, ALU.add).then_inc(ovar, 1)
                dve.wait_ge(oroot, b + 1)
                link(dve.reciprocal(asm[:, 32 + 8 * b:40 + 8 * b], asm[:, 32 + 8 * b:40 + 8 * b]))
                link(TTo(hv, hv, spread(asm[:, 32 + 8 * b:40 + 8 * b], 2, P), ALU.mult))
                TTo(hv, hv, spread(subg, 1, H), ALU.mult).then_inc(o_ready, 1)

            def add_mix(n, bank):
                b, c = n // 2, n % 2
                dve.wait_ge(wo_done, n + 1)
                TTo(x[:, b, 512 * c:512 * c + 512], x[:, b, 512 * c:512 * c + 512], ps[:, bank, :], ALU.add).then_inc(mixed, 1)

            for c in range(4):
                rotate(0, c)
            peak(0)
            rotate(1, 0)
            peak(1)
            combine(0)
            rotate(1, 1)
            combine(1)
            rotate(1, 2)
            rotate(1, 3)
            norm_o(0)
            peak(2)
            peak(3)
            combine(2)
            peak(4)
            combine(3)
            add_mix(0, 5)
            peak(5)
            combine(4)
            add_mix(1, 5)
            combine(5)
            norm_o(1)
            add_mix(2, 0)
            add_mix(3, 1)
            norm(3)
            moe(1)
            norm(4)

        @block.tensor
        def _(pe):
            mm = pe.matmul

            def turn(i):
                for tt in range(TT):
                    pe.wait_ge(normed, 2 * i + 1 + tt)
                    for k in range(KD):
                        ins = pe.transpose(ps[:, k // 2, 256 * (k % 2) + P * tt:256 * (k % 2) + P * tt + P], xr[:, tt, k, :], ident)
                ins.then_inc(hT_psum, 1)

            for first in (down_done, scattered):
                pe.sem_inc(first, 1)
            pe.wait_ge(s_con, 16)
            turn(0)
            for c in range(KD):
                if c % 4 == 0:
                    pe.wait_ge(landed[c // 4], 32)
                if c == 3:
                    pe.wait_ge(lam_ready, 1)
                    for n, row in enumerate([lam2[:, v, :] for v in (1, 2, 3, 4)] + [lam[:, v, :] for v in (5, 6)]):
                        pe.transpose(ps[:, 6, 32 * n:32 * n + 32], row, ident[0:32, 0:32]).then_inc(lam_psum, 1)
                    pe.transpose(ps[:, 7, 0:32], lam2[:, 7, :], ident[0:32, 0:32]).then_inc(lam_psum, 1)
                    pe.transpose(ps[:, 6, 192:200], drep[0:8, :], ident[0:8, 0:8]).then_inc(lam_psum, 1)
                    pe.wait_ge(s_bc, 64)
                    idg = ident.rearrange("p (r g h) -> p r g h", g=2, h=16)
                    for i in range(2):
                        for q in range(KD):
                            for g in range(2):
                                ins = mm(ps[64 * g:64 * g + 64, 4 + i, 64 * q:64 * q + 64], Cn[:, i, q, :], idg[:, :, g, :],
                                         start=True, stop=True)
                    ins.then_inc(c_psum, 1)
                for k in range(KD):
                    if c == 0 and k == 4:
                        pe.wait_ge(hT_ready, 4)
                    if c == 0 and k == 0:
                        pe.wait_ge(hT_ready, 2)
                    ins = mm(ps[:, c // 2, 256 * (c % 2):256 * (c % 2) + 256], win[c // 4][:, k, P * (c % 4):P * (c % 4) + P],
                             hT[:, k, :], start=(k == 0), stop=(k == KD - 1))
                ins.then_inc(u_done, 1)
            pe.wait_ge(u_done, 8)
            for u in range(2):
                pe.sem_inc(used[u], 1)

            def taps(o):
                pe.wait_ge(w2_ready, o + 1)
                for r in range(OCT):
                    pair = OCT * o + r
                    q = slice(32 * (pair % 4), 32 * (pair % 4) + 32)
                    at0 = P * (pair // 4 % 4)
                    for lo, hi, tap in ((0, PC, Cb), (PC, P, W2)):
                        for i in range(2):
                            ins = mm(ps[q, 6 + pair // 16, at0 + lo:at0 + hi], W1[:, i, r, 0, :], tap[:, i, pair, 0:hi - lo],
                                     start=(i == 0), stop=(i == 1))
                ins.then_inc(k_done, 1)

            for o in range(PAIRS // OCT):
                pe.wait_ge(w1_ready, o + 1)
                pe.wait_ge(w1_first, 4 * o + 4)
                taps(o)
                if o == 0:
                    pe.wait_ge(u4_ready, 32)
                else:
                    pe.wait_ge(w1T_ready, 4 * o)
                if o == PAIRS // OCT - 1:
                    for _ in range(2):
                        mm(ps[:, 0, :], ident, con[:, 0:512], start=True, stop=True)
                for i in range(2):
                    for r in range(OCT):
                        ins = pe.transpose(ps[:, 2 * i + r // 4, P * (r % 4):P * (r % 4) + P],
                                           W1[:, i, r, :, :].rearrange("p j c -> p (j c)"), ident)
                ins.then_inc(w1_turned, 1)
                if o >= 1:
                    pe.wait_ge(v_ready, o)
                for r in range(OCT):
                    if r % 4 == 0:
                        pe.wait_ge(w1T_ready, 4 * o + 2 + r // 2)
                    for i in range(2):
                        ins = mm(ps[:, 4 + r // 4, P * (r % 4) + 64 * i:P * (r % 4) + 64 * i + 64], W1T[:, i, r, :],
                                 U4[:, OCT * o + r, :], start=True, stop=True)
                    if r % 4 == 3:
                        ins.then_inc(v_done, 1)
            def y(pair):
                return ps[:, pair // 8, 64 * (pair % 8):64 * (pair % 8) + 64]

            for o in range(4):
                pe.wait_ge(f_ready, 16 if o < 2 else 32)
                for r in range(OCT * o, OCT * o + OCT):
                    mm(y(r), Fw[:, r, :], U4[:, r, :], start=(r % 8 == 0), stop=False, skip_group_check=True)
                if o < 3:
                    pe.wait_ge(state, o + 1)
                else:
                    pe.wait_ge(last_state, 1)
                for r in range(OCT):
                    for i in range(2):
                        ins = mm(y(OCT * o + r), W2[:, i, OCT * o + r, :], X[:, o, i, r, :], start=False, stop=(i == 1),
                                 skip_group_check=True)
                    ins.then_inc(y_done, 1)
            for n in range(4):
                tt, c = n // 2, n % 2
                if n >= 2:
                    pe.wait_ge(mixed, n - 1)
                for half in range(2):
                    u = 2 + 2 * half + c
                    pe.wait_ge(landed[u], 32)
                    for k in range(KD):
                        if n == 0 and half == 0 and k % 2 == 0:
                            pe.wait_ge(g_ready, 8 * k + 16)
                        ins = mm(ps[:, 4 + 2 * (n % 2) + half, :], gT[:, k, tt * P:(tt + 1) * P], win[u][:, k, :],
                                 start=(k == 0), stop=(k == KD - 1))
                    if n >= 2:
                        if half == 0:
                            ins.then_inc(used[u], 1)
                ins.then_inc(glu_done, 1)
                if n == 3:
                    pe.wait_ge(glu_done, 4)
                    for u in (4, 5):
                        pe.sem_inc(used[u], 1)

            def moe(l):
                pe.wait_ge(s_router, 128)
                for k in range(KD):
                    if k % 2 == 0:
                        pe.wait_ge(hT_ready, 8 * l + 5 + k // 2)
                    ins = mm(ps[0:NG + E, 4, 0:T], wr[:, l, k, :], hT[:, k, :], start=(k == 0), stop=(k == KD - 1))
                ins.then_inc(logits_turned, 1)
                pe.wait_ge(logits_kept, l + 1)
                for tt in range(TT):
                    ins = pe.transpose(ps[:, 5, 36 * tt:36 * tt + 36], lgT[0:NG + E, tt * P:(tt + 1) * P], ident[0:NG + E, 0:NG + E])
                ins.then_inc(logits_done, 1)
                pe.wait_ge(mask_ready, l + 1)
                mm(ps[:, 5, 128:160], before, msk[:, 0, :], start=True, stop=True)
                mm(ps[:, 5, 160:192], before, msk[:, 1, :], start=True, stop=False)
                mm(ps[:, 5, 160:192], ones, msk[:, 0, :], start=False, stop=True)
                mm(ps[:, 5, 192:224], ones, msk[:, 0, :], start=True, stop=False)
                mm(ps[:, 5, 192:224], ones, msk[:, 1, :], start=False, stop=True).then_inc(pos_done, 1)
                pe.wait_ge(cum_ready, l + 1)
                pe.wait_ge(part_ready, 3 * l + 3)
                with pe.Fori(0, NQ // 2) as h:
                    for odd in range(2):
                        q = 2 * h + odd
                        n0, passes = passes_of(pe, l, q)
                        rounds = (q + (qround(l, 0) + 1)) * 32
                        dn_here, dn_landed, place = down_at(l, odd)
                        dn_rounds = (h + (4 * l + 1 if place else 5 * l + 2)) * 32
                        with pe.Fori(0, passes) as p:
                            n = n0 + p
                            pe.wait_ge(sel_ready, 2 * (n + q) + (2 * (NQ + 1) * l + 3))
                            pe.wait_ge(hidT_kept, n + 1)
                            for tt in range(TT):
                                ins = pe.transpose(ps[:, 3, P * tt:P * tt + P], scw[:, tt, :], ident)
                            ins.then_inc(sw_turned, 1)
                            pe.wait_ge(x_added, 2 * n0 + 1)
                            for k in range(KD):
                                for tt in range(TT):
                                    for i in range(3):
                                        ins = mm(ps[:, k // 4, P * (k % 4):P * (k % 4) + P], parts[i][:, tt, k, :], sel[:, tt, :],
                                                 start=(tt == 0 and i == 0), stop=(tt == TT - 1 and i == 2))
                                if k % 4 == 3:
                                    ins.then_inc(gathered, 1)
                            pe.wait_ge(xg_ready, 2 * n + 2)
                            for k in range(KD):
                                if k % 2 == 0:
                                    pe.wait_ge(landed[k // 2], rounds)
                                for e in range(QE):
                                    s = slice(32 * e, 32 * e + 32)
                                    ins = mm(ps[s, 2, :], xg[:, k, s], gu[k // 2][:, e, :, k % 2, :],
                                             start=(k == 0), stop=(k == KD - 1))
                                if k % 2 == 1 and k < KD - 1:
                                    ins.then_inc(used[k // 2], 1)
                            ins.then_inc(gu_done, 1)
                            pe.wait_ge(gu_done, n + 1)
                            pe.wait_ge(hid_ready, n + 1)
                            pe.wait_ge(sw_ready, n + 1)
                            pe.transpose(ps[:, 3, 256:384], hid[:, 0:P], ident).then_inc(used[3], 1)
                            pe.transpose(ps[:, 3, 384:512], hid[:, P:2 * P], ident).then_inc(hid_turned, 1)
                        with pe.Fori(0, passes) as p:
                            n = n0 + p
                            pe.wait_ge(down_ready, n + 1 + (q + NQ * l))
                            pe.wait_ge(y_ready, 2 * n + 1)
                            for k in range(2):
                                pe.wait_ge(dn_landed[k], dn_rounds)
                                for half in range(2):
                                    for e in range(QE):
                                        s = slice(32 * e, 32 * e + 32)
                                        ins = mm(ps[s, 4 + half, :], hidT[:, P * k + 32 * e:P * k + 32 * e + 32],
                                                 dn_here[k][:, e, 512 * half:512 * half + 512], start=(k == 0), stop=(k == 1))
                            ins.then_inc(down_done, 1)
                            pe.wait_ge(back_ready, n + 1)
                            pe.wait_ge(y_ready, 2 * n + 3)
                            pe.wait_ge(x_added, 2 * n + 2)
                            for tt in range(TT):
                                for half in range(2):
                                    ins = mm(ps[:, (6 if tt else 0) + half, :], swT[:, P * tt:P * tt + P],
                                             yy[:, 512 * half:512 * half + 512], start=True, stop=True)
                                ins.then_inc(scattered, 1)

            turn(1)
            moe(0)
            turn(2)
            def project(tt, c):
                pe.wait_ge(landed[c], 32 * (NQ + 2 if c < 4 else NQ // 2 + 2))
                if tt:
                    if c in (0, 1):
                        pe.wait_ge(qkv_kept, 2)
                    elif c in (2, 3):
                        pe.wait_ge(qkv_kept, 3 + c)
                    else:
                        pe.wait_ge(qkv_kept, 3 + c)
                for k in range(KD):
                    ins = mm(ps[:, c if tt == 0 else c % 2, :], hT[:, k, tt * P:(tt + 1) * P], win[c][:, k, :],
                             start=(k == 0), stop=(k == KD - 1))
                ins.then_inc(qkv_done, 1)

            def turn_qk(tt, c):
                i = 4 * tt + c
                pe.wait_ge(qkv_kept, i + 1)
                if i in (2, 3, 6, 7):
                    pe.wait_ge(qkT_ready, i - 1)
                for h in range(4):
                    ins = pe.transpose(ps[:, (6 if tt == 0 else 2) + c % 2, P * h:P * h + P], nat[:, c % 2, P * h:P * h + P], ident)
                ins.then_inc(qk_turned, 1)

            def scores(g):
                b, h0, heads, sbank, _, _, _ = groups[g]
                keys = P * (b + 1)
                pe.wait_ge(qkT_ready, 4 * (b + 1))
                if g in (1, 4, 5):
                    pe.wait_ge(exp_ready, exps[0 if g == 1 else g - 2])
                for h in range(heads):
                    for j in range(2):
                        s = slice(64 * j, 64 * j + 64)
                        ins = mm(ps[:, sbank + j, keys * h:keys * h + keys], qk[s, h0 + h, b * P:(b + 1) * P],
                                 qk[s, 8 + h0 + h, 0:keys], start=True, stop=True)
                ins.then_inc(scores_done, 1)

            def turn_att(g):
                pe.wait_ge(att_ready, g + 1)
                if g:
                    pe.wait_ge(attT_ready, g)
                for n in range(4):
                    ins = pe.transpose(ps[:, groups[g][4], P * n:P * n + P], at[:, P * n:P * n + P], ident)
                ins.then_inc(att_turned, 1)

            def values(g):
                b, h0, heads, _, _, obank, col = groups[g]
                pe.wait_ge(attT_ready, g + 1)
                pe.wait_ge(v_kept, 2 * b + 2)
                if g == 1:
                    pe.wait_ge(osq, 1)
                if g >= 2:
                    pe.wait_ge(osq, 2)
                for h in range(heads):
                    for k in range(b + 1):
                        n = (b + 1) * h + k
                        ins = mm(ps[:, obank, col + P * h:col + P * h + P], atT[:, g % 2, P * n:P * n + P],
                                 vv[:, k, P * (h0 + h):P * (h0 + h) + P], start=(k == 0), stop=(k == b))
                ins.then_inc(av_done, 1)

            def turn_o(b, c, bank):
                pe.wait_ge(o_ready, b + 1)
                if b == 0 and c == 1:
                    pe.wait_ge(oT_ready, 1)
                for h in range(4):
                    ins = pe.transpose(ps[:, bank, P * h:P * h + P], osb[b][:, 512 * c + P * h:512 * c + P * h + P], ident)
                ins.then_inc(o_turned, 1)

            def out_proj(n, bank):
                b, c = n // 2, n % 2
                pe.wait_ge(s_wo, 16)
                pe.wait_ge(oT_ready, 2 * b + 2)
                if n:
                    pe.wait_ge(mixed, 4 + min(n, 2))
                for k in range(KD):
                    ins = mm(ps[:, bank, :], oT[:, k, b * P:(b + 1) * P], wo[:, k, 512 * c:512 * c + 512],
                             start=(k == 0), stop=(k == KD - 1))
                ins.then_inc(wo_done, 1)

            pe.wait_ge(hT_ready, 12)
            project(0, 0)
            project(0, 1)
            turn_qk(0, 0)
            project(0, 2)
            turn_qk(0, 1)
            project(0, 3)
            turn_qk(0, 2)
            project(0, 4)
            turn_qk(0, 3)
            project(0, 5)
            pe.wait_ge(v_kept, 2)
            scores(0)
            project(1, 0)
            scores(1)
            project(1, 1)
            turn_att(0)
            turn_qk(1, 0)
            values(0)
            project(1, 2)
            turn_att(1)
            turn_qk(1, 1)
            values(1)
            project(1, 3)
            turn_qk(1, 2)
            project(1, 4)
            turn_qk(1, 3)
            project(1, 5)
            pe.wait_ge(v_kept, 4)
            scores(2)
            scores(3)
            turn_att(2)
            turn_o(0, 0, 5)
            values(2)
            scores(4)
            turn_att(3)
            turn_o(0, 1, 5)
            values(3)
            out_proj(0, 5)
            scores(5)
            turn_att(4)
            values(4)
            out_proj(1, 5)
            turn_att(5)
            values(5)
            turn_o(1, 0, 4)
            turn_o(1, 1, 5)
            out_proj(2, 0)
            out_proj(3, 1)
            turn(3)
            moe(1)


_INS = ['x', 'norm_mix_g', 'norm_ffn_g', 'final_norm_g', 'ssm_w_in', 'ssm_lam_re', 'ssm_lam_im', 'ssm_log_dt',
        'ssm_b_re', 'ssm_b_im', 'ssm_c_re', 'ssm_c_im', 'ssm_d', 'ssm_w_glu', 'attn_w_qkv', 'attn_lambda_q1',
        'attn_lambda_k1', 'attn_lambda_q2', 'attn_lambda_k2', 'attn_subln_g', 'attn_w_o', 'moe_w_router_group',
        'moe_b_router_group', 'moe_w_router_expert', 'moe_b_router_expert', 'moe_w_gate', 'moe_w_up', 'moe_w_down']


def kernel(**inputs):
    import concourse.bacc as bacc
    from concourse.bass_utils import run_bass_kernel_spmd as run

    nc = bacc.Bacc("TRN2", target_bir_lowering=False, num_devices=1)
    arrays = {"in_con": constants()}
    for name in _INS:
        arrays["in_" + name] = np.ascontiguousarray(inputs[name])
    aps = {n[3:]: nc.dram_tensor(n, v.shape, mybir.dt.from_np(v.dtype), kind="ExternalInput").ap() for n, v in arrays.items()}
    out = nc.dram_tensor("out", (1, T, D), F32, kind="ExternalOutput").ap()
    build(nc, aps, out)
    return run(nc, [arrays], core_ids=[0]).results[0]["out"]
```
